# Optimizing a Trainium2 kernel written in Bass

```python
import math
import jax, jax.numpy as jnp
from jax import lax
import numpy as np

D_MODEL = 1024
BATCH = 1
SEQ = 256
DEPTH = 1

CHUNK = 64
CONV_A_GROUPS = 8
CONV_A_GROUP_DIM = D_MODEL // 16
CONV_A_DIM = CONV_A_GROUPS * CONV_A_GROUP_DIM
CONV_A_WIDTH = 3
DN_HEADS = 4
DN_HEAD_DIM = D_MODEL // 8
DN_DIM = DN_HEADS * DN_HEAD_DIM
DN_CONV_WIDTH = 4
MIX_DIM = CONV_A_DIM + DN_DIM
IN_PROJ_DIM = 3 * CONV_A_DIM + 4 * DN_DIM + 2 * DN_HEADS
N_GROUPS = 4
EXPERTS_PER_GROUP = 8
N_EXPERTS = N_GROUPS * EXPERTS_PER_GROUP
TOP_K = 2
EXPERT_FF = D_MODEL // 2
MOE_BLOCK = 128
EPS = 1e-6


def rms_norm(x, g):
    xf = x.astype(jnp.float32)
    y = xf * lax.rsqrt(jnp.mean(xf * xf, axis=-1, keepdims=True) + EPS)
    return (y * g.astype(jnp.float32)).astype(x.dtype)

def causal_dwconv(x, w):
    K = w.shape[0]
    S = x.shape[1]
    xp = jnp.pad(x, ((0, 0), (K - 1, 0), (0, 0)))
    y = xp[:, 0:S] * w[0]
    for j in range(1, K):
        y = y + xp[:, j:j + S] * w[j]
    return y

def short_conv_mixer(hx, b, c, conv_w, norm_g):
    Bsz, S, _ = hx.shape
    y = b * causal_dwconv(c * hx, conv_w)
    y = y.reshape(Bsz, S, CONV_A_GROUPS, CONV_A_GROUP_DIM)
    y = rms_norm(y, norm_g.reshape(CONV_A_GROUPS, CONV_A_GROUP_DIM))
    return y.reshape(Bsz, S, CONV_A_DIM)

def chunk_gated_delta(q, k, v, beta, g):
    Bsz, H, S, dk = q.shape
    dv = v.shape[-1]
    n = S // CHUNK

    def chunks(t):
        return t.reshape((Bsz, H, n, CHUNK) + t.shape[3:])

    q, k, v, beta, g = chunks(q), chunks(k), chunks(v), chunks(beta), chunks(g)
    g = jnp.cumsum(g, axis=-1)
    causal = jnp.tril(jnp.ones((CHUNK, CHUNK), bool))
    strict = jnp.tril(jnp.ones((CHUNK, CHUNK), bool), -1)
    decay = jnp.exp(jnp.where(causal, g[..., :, None] - g[..., None, :], -jnp.inf))
    k_beta = k * beta[..., None]
    L = jnp.where(strict, jnp.einsum('bhncd,bhnjd->bhncj', k_beta, k) * decay, 0.0)
    eye = jnp.eye(CHUNK, dtype=jnp.float32)
    rhs = jnp.concatenate([v * beta[..., None], k_beta * jnp.exp(g)[..., None]], axis=-1)
    uw = lax.linalg.triangular_solve(eye + L, rhs, left_side=True, lower=True, unit_diagonal=True)
    u, w = uw[..., :dv], uw[..., dv:]
    intra = jnp.einsum('bhncd,bhnjd->bhncj', q, k) * decay
    q_dec = q * jnp.exp(g)[..., None]
    g_last = g[..., -1]
    k_dec = k * jnp.exp(g_last[..., None] - g)[..., None]

    def to_scan(t):
        return jnp.moveaxis(t, 2, 0)

    xs = (to_scan(u), to_scan(w), to_scan(q_dec), to_scan(intra), to_scan(k_dec), to_scan(g_last))

    def step(state, inp):
        u_i, w_i, qd_i, a_i, kd_i, gl_i = inp
        v_new = u_i - jnp.einsum('bhck,bhkv->bhcv', w_i, state)
        o_i = jnp.einsum('bhck,bhkv->bhcv', qd_i, state) + jnp.einsum('bhcj,bhjv->bhcv', a_i, v_new)
        state = state * jnp.exp(gl_i)[..., None, None] + jnp.einsum('bhck,bhcv->bhkv', kd_i, v_new)
        return state, o_i

    s0 = jnp.zeros((Bsz, H, dk, dv), jnp.float32)
    _, o = lax.scan(step, s0, xs)
    return jnp.moveaxis(o, 0, 2).reshape(Bsz, H, S, dv)

def gated_deltanet(q, k, v, z, beta_logit, a_logit, conv_w, a_log, dt_bias, norm_g):
    Bsz, S, _ = q.shape
    dtype = q.dtype
    qkv = jax.nn.silu(causal_dwconv(jnp.concatenate([q, k, v], axis=-1), conv_w)).astype(jnp.float32)
    q, k, v = jnp.split(qkv, 3, axis=-1)

    def heads(t):
        return t.reshape(Bsz, S, DN_HEADS, DN_HEAD_DIM).transpose(0, 2, 1, 3)

    q, k, v = heads(q), heads(k), heads(v)
    q = q * lax.rsqrt(jnp.sum(q * q, axis=-1, keepdims=True) + EPS) * (DN_HEAD_DIM ** -0.5)
    k = k * lax.rsqrt(jnp.sum(k * k, axis=-1, keepdims=True) + EPS)
    beta = jax.nn.sigmoid(beta_logit.astype(jnp.float32)).transpose(0, 2, 1)
    g = (-jnp.exp(a_log.astype(jnp.float32))
         * jax.nn.softplus(a_logit.astype(jnp.float32) + dt_bias.astype(jnp.float32))).transpose(0, 2, 1)
    o = chunk_gated_delta(q, k, v, beta, g).transpose(0, 2, 1, 3)
    zf = z.astype(jnp.float32).reshape(Bsz, S, DN_HEADS, DN_HEAD_DIM)
    o = rms_norm(o, norm_g) * jax.nn.silu(zf)
    return o.reshape(Bsz, S, DN_DIM).astype(dtype)

def hier_moe(h, router_group_w, router_expert_w, w_gate, w_up, w_down):
    N, D = h.shape
    group_logits = (h @ router_group_w).astype(jnp.float32)
    group_idx = jnp.argmax(group_logits, axis=-1)
    group_prob = jnp.take_along_axis(jax.nn.softmax(group_logits, axis=-1), group_idx[:, None], axis=1)
    exp_logits = (h @ router_expert_w).astype(jnp.float32).reshape(N, N_GROUPS, EXPERTS_PER_GROUP)
    exp_logits = jnp.take_along_axis(exp_logits, group_idx[:, None, None], axis=1)[:, 0]
    top_p, top_local = lax.top_k(jax.nn.softmax(exp_logits, axis=-1), TOP_K)
    gate = group_prob * top_p / jnp.sum(top_p, axis=-1, keepdims=True)
    expert_id = (group_idx[:, None] * EXPERTS_PER_GROUP + top_local).astype(jnp.int32)

    flat_e = expert_id.reshape(-1)
    flat_tok = jnp.repeat(jnp.arange(N, dtype=jnp.int32), TOP_K)
    flat_gate = gate.reshape(-1)
    order = jnp.argsort(flat_e)
    sorted_e = flat_e[order]
    counts = jnp.bincount(flat_e, length=N_EXPERTS)
    padded = (counts + MOE_BLOCK - 1) // MOE_BLOCK * MOE_BLOCK
    pad_end = jnp.cumsum(padded)
    pad_start = pad_end - padded
    start = jnp.cumsum(counts) - counts
    dest = pad_start[sorted_e] + jnp.arange(N * TOP_K, dtype=jnp.int32) - start[sorted_e]
    P = N * TOP_K + N_EXPERTS * MOE_BLOCK
    slot_tok = jnp.full((P,), N, jnp.int32).at[dest].set(flat_tok[order])
    slot_gate = jnp.zeros((P,), jnp.float32).at[dest].set(flat_gate[order])
    n_blocks = P // MOE_BLOCK
    block_expert = jnp.minimum(
        jnp.searchsorted(pad_end, jnp.arange(n_blocks, dtype=jnp.int32) * MOE_BLOCK, side='right'),
        N_EXPERTS - 1)
    h_pad = jnp.concatenate([h, jnp.zeros((1, D), h.dtype)], axis=0)
    xb = h_pad[slot_tok].reshape(n_blocks, MOE_BLOCK, D)

    def expert_block(args):
        xblk, e = args
        a = xblk @ w_gate[e]
        b = xblk @ w_up[e]
        return (jax.nn.silu(a) * b) @ w_down[e]

    yb = lax.map(expert_block, (xb, block_expert)).reshape(P, D)
    out = jnp.zeros((N + 1, D), jnp.float32).at[slot_tok].add(yb.astype(jnp.float32) * slot_gate[:, None])
    return out[:N].astype(h.dtype)

def first_inputs(seed: int = 0) -> dict:
    key = jax.random.key(seed)
    ks = jax.random.split(key, 18)
    f32 = jnp.float32

    def normal(k, shape, scale):
        return jax.random.normal(k, shape, f32) * scale

    def gain(k, shape):
        return 1.0 + 0.05 * jax.random.normal(k, shape, f32)

    dt = jnp.exp(jax.random.uniform(ks[7], (DEPTH, DN_HEADS), f32, math.log(1e-3), math.log(1e-1)))
    return {
        "x": normal(ks[0], (BATCH, SEQ, D_MODEL), 1.0),
        "mix_norm_g": gain(ks[1], (DEPTH, D_MODEL)),
        "w_in": normal(ks[2], (DEPTH, D_MODEL, IN_PROJ_DIM), D_MODEL ** -0.5),
        "conv_a_w": normal(ks[3], (DEPTH, CONV_A_WIDTH, CONV_A_DIM), CONV_A_WIDTH ** -0.5),
        "conv_a_norm_g": gain(ks[4], (DEPTH, CONV_A_DIM)),
        "dn_conv_w": normal(ks[5], (DEPTH, DN_CONV_WIDTH, 3 * DN_DIM), DN_CONV_WIDTH ** -0.5),
        "dn_a_log": jnp.log(jax.random.uniform(ks[6], (DEPTH, DN_HEADS), f32, 1.0, 16.0)),
        "dn_dt_bias": dt + jnp.log(-jnp.expm1(-dt)),
        "dn_norm_g": gain(ks[8], (DEPTH, DN_HEAD_DIM)),
        "w_out": normal(ks[9], (DEPTH, MIX_DIM, D_MODEL), MIX_DIM ** -0.5),
        "ffn_norm_g": gain(ks[10], (DEPTH, D_MODEL)),
        "router_group_w": normal(ks[11], (DEPTH, D_MODEL, N_GROUPS), D_MODEL ** -0.5),
        "router_expert_w": normal(ks[12], (DEPTH, D_MODEL, N_EXPERTS), D_MODEL ** -0.5),
        "w_gate": normal(ks[13], (DEPTH, N_EXPERTS, D_MODEL, EXPERT_FF), D_MODEL ** -0.5),
        "w_up": normal(ks[14], (DEPTH, N_EXPERTS, D_MODEL, EXPERT_FF), D_MODEL ** -0.5),
        "w_down": normal(ks[15], (DEPTH, N_EXPERTS, EXPERT_FF, D_MODEL), EXPERT_FF ** -0.5),
        "final_norm_g": gain(ks[16], (D_MODEL,)),
    }

def first_block(x, mix_norm_g, w_in, conv_a_w, conv_a_norm_g, dn_conv_w, dn_a_log, dn_dt_bias,
              dn_norm_g, w_out, ffn_norm_g, router_group_w, router_expert_w, w_gate, w_up, w_down,
              final_norm_g):
    Bsz, S, D = x.shape
    sizes = (CONV_A_DIM,) * 3 + (DN_DIM,) * 4 + (DN_HEADS,) * 2
    split_idx = []
    acc = 0
    for s in sizes[:-1]:
        acc += s
        split_idx.append(acc)
    for l in range(DEPTH):
        h = rms_norm(x, mix_norm_g[l])
        proj = h @ w_in[l]
        a_h, a_b, a_c, d_q, d_k, d_v, d_z, d_beta, d_alpha = jnp.split(proj, split_idx, axis=-1)
        y_a = short_conv_mixer(a_h, a_b, a_c, conv_a_w[l], conv_a_norm_g[l])
        y_b = gated_deltanet(d_q, d_k, d_v, d_z, d_beta, d_alpha, dn_conv_w[l], dn_a_log[l],
                             dn_dt_bias[l], dn_norm_g[l])
        x = x + jnp.concatenate([y_a, y_b], axis=-1) @ w_out[l]
        h = rms_norm(x, ffn_norm_g[l]).reshape(Bsz * S, D)
        x = x + hier_moe(h, router_group_w[l], router_expert_w[l], w_gate[l], w_up[l], w_down[l]).reshape(Bsz, S, D)
    return rms_norm(x, final_norm_g)


DEPTH_2 = 2

N_EVEN = (DEPTH_2 + 1) // 2
N_ODD = DEPTH_2 // 2
RET_HEADS = 4
RET_DV = D_MODEL // 2 // RET_HEADS
RET_DK = RET_DV
ROPE_BASE = 10000.0
GLA_HEADS = 4
GLA_DV = D_MODEL // 2 // GLA_HEADS
GLA_DK = GLA_DV // 2
GLA_RANK = 16
GLA_TAU = 16.0
AB_SIZES = (RET_HEADS * RET_DK, RET_HEADS * RET_DK, RET_HEADS * RET_DV, RET_HEADS * RET_DV,
            GLA_HEADS * GLA_DK, GLA_HEADS * GLA_DK, GLA_HEADS * GLA_DV, GLA_HEADS * GLA_DV,
            GLA_RANK)
AB_IN = sum(AB_SIZES)
HGRN_DK = 128
HGRN_HEADS = D_MODEL // HGRN_DK
HGRN_DV = D_MODEL // HGRN_HEADS
C_IN = 4 * D_MODEL
D_FF = ((8 * D_MODEL // 3 + 255) // 256) * 256
N_EXPERTS_2 = 8
EXPERT_FF_2 = 7 * D_MODEL // 2
OUT_SCALE = (2 * DEPTH_2) ** -0.5


def rms_norm_2(x, g):
    xf = x.astype(jnp.float32)
    y = xf * lax.rsqrt(jnp.mean(xf * xf, axis=-1, keepdims=True) + EPS)
    return (y * g.astype(jnp.float32)).astype(x.dtype)

def rotary(x, positions):
    d = x.shape[-1]
    inv_freq = ROPE_BASE ** (-jnp.arange(0, d, 2, dtype=jnp.float32) / d)
    ang = positions.astype(jnp.float32)[..., None, None] * inv_freq
    cos, sin = jnp.cos(ang), jnp.sin(ang)
    xf = x.astype(jnp.float32)
    x1, x2 = xf[..., : d // 2], xf[..., d // 2:]
    return jnp.concatenate([x1 * cos - x2 * sin, x2 * cos + x1 * sin], axis=-1)

def _to_chunks(a):
    b, t, h, d = a.shape
    return a.reshape(b, t // CHUNK, CHUNK, h, d).transpose(1, 0, 3, 2, 4)

def _from_chunks(a):
    nc, b, h, c, d = a.shape
    return a.transpose(1, 0, 3, 2, 4).reshape(b, nc * c, h, d)

def _causal_mask():
    t = jnp.arange(CHUNK)
    return t[:, None] >= t[None, :]

def retention_chunkwise(q, k, v, log_gamma):
    b, _, h, dk = q.shape
    dv = v.shape[-1]
    t = jnp.arange(CHUNK, dtype=jnp.float32)
    lg = log_gamma.astype(jnp.float32)
    rel = t[:, None] - t[None, :]
    intra_decay = jnp.exp(jnp.where(_causal_mask()[None], rel[None] * lg[:, None, None], -jnp.inf))
    q_decay = jnp.exp((t[None, :] + 1.0) * lg[:, None])[..., None]
    k_decay = jnp.exp((CHUNK - 1.0 - t[None, :]) * lg[:, None])[..., None]
    chunk_decay = jnp.exp(CHUNK * lg)[:, None, None]

    def step(state, inp):
        qc, kc, vc = inp
        scores = jnp.einsum('bhid,bhjd->bhij', qc, kc) * intra_decay
        o = (jnp.einsum('bhij,bhjv->bhiv', scores, vc)
             + jnp.einsum('bhid,bhdv->bhiv', qc * q_decay, state))
        state = chunk_decay * state + jnp.einsum('bhjd,bhjv->bhdv', kc * k_decay, vc)
        return state, o

    s0 = jnp.zeros((b, h, dk, dv), jnp.float32)
    _, o = lax.scan(step, s0, (_to_chunks(q), _to_chunks(k), _to_chunks(v)))
    return _from_chunks(o)

def gated_chunkwise(q, k, v, log_f):
    b, _, h, dk = q.shape
    dv = v.shape[-1]
    mask = _causal_mask()[:, :, None]
    g_cum = jnp.cumsum(_to_chunks(log_f), axis=-2)

    def step(state, inp):
        qc, kc, vc, gc = inp
        diff = gc[:, :, :, None, :] - gc[:, :, None, :, :]
        decay = jnp.exp(jnp.where(mask, diff, -jnp.inf))
        scores = jnp.einsum('bhid,bhjd,bhijd->bhij', qc, kc, decay)
        g_last = gc[:, :, -1:, :]
        o = (jnp.einsum('bhij,bhjv->bhiv', scores, vc)
             + jnp.einsum('bhid,bhdv->bhiv', qc * jnp.exp(gc), state))
        state = (jnp.exp(g_last[:, :, 0, :])[..., None] * state
                 + jnp.einsum('bhjd,bhjv->bhdv', kc * jnp.exp(g_last - gc), vc))
        return state, o

    s0 = jnp.zeros((b, h, dk, dv), jnp.float32)
    _, o = lax.scan(step, s0, (_to_chunks(q), _to_chunks(k), _to_chunks(v), g_cum))
    return _from_chunks(o)

def retnet_gla_mixer(h, positions, w_in, w_a2, b_a2, ret_g, gla_g, w_out):
    b, t, _ = h.shape
    z = h @ w_in
    aq, ak, av, ag, bq, bk, bv, bg, ba = jnp.split(z, np.cumsum(AB_SIZES)[:-1], axis=-1)
    f32 = jnp.float32

    def heads(a, n):
        return a.reshape(b, t, n, -1).astype(f32)

    qa = rotary(heads(aq, RET_HEADS), positions)
    ka = rotary(heads(ak, RET_HEADS), positions) * (RET_DK ** -0.5)
    log_gamma = jnp.log1p(-jnp.exp2(-5.0 - jnp.arange(RET_HEADS, dtype=f32)))
    oa = retention_chunkwise(qa, ka, heads(av, RET_HEADS), log_gamma)
    oa = rms_norm_2(oa, ret_g) * jax.nn.silu(heads(ag, RET_HEADS))
    log_alpha = jax.nn.log_sigmoid((ba @ w_a2 + b_a2).astype(f32)) / GLA_TAU
    ob = gated_chunkwise(heads(bq, GLA_HEADS) * (GLA_DK ** -0.5), heads(bk, GLA_HEADS),
                         heads(bv, GLA_HEADS), heads(log_alpha, GLA_HEADS))
    ob = rms_norm_2(ob, gla_g) * jax.nn.silu(heads(bg, GLA_HEADS))
    o = jnp.concatenate([oa.reshape(b, t, -1), ob.reshape(b, t, -1)], axis=-1)
    return o.astype(h.dtype) @ w_out

def hgrn2_mixer(h, lb, w_in, norm_g, w_out):
    b, t, d = h.shape
    f32 = jnp.float32
    q, f, i, g = jnp.split(h @ w_in, 4, axis=-1)

    def heads(a):
        return a.reshape(b, t, HGRN_HEADS, -1).astype(f32)

    f = heads(f)
    lb = lb.astype(f32)
    log_f = jnp.logaddexp(jnp.log(lb), jnp.log1p(-lb) + jax.nn.log_sigmoid(f))
    k = (1.0 - lb) * jax.nn.sigmoid(-f)
    qh = jax.nn.silu(heads(q)) * (HGRN_DK ** -0.5)
    o = gated_chunkwise(qh, k, heads(i), log_f)
    o = rms_norm_2(o, norm_g) * jax.nn.silu(heads(g))
    return o.reshape(b, t, d).astype(h.dtype) @ w_out

def swiglu(h, w_gate, w_up, w_down):
    return (jax.nn.silu(h @ w_gate) * (h @ w_up)) @ w_down

def moe_swiglu(h, w_router, w_gate, w_up, w_down):
    b, t, d = h.shape
    xt = h.reshape(b * t, d)
    logits = (xt @ w_router).astype(jnp.float32)
    top_logits, top_idx = lax.top_k(logits, TOP_K)
    gates = jax.nn.softmax(top_logits, axis=-1)
    flat_e = top_idx.reshape(-1)
    order = jnp.argsort(flat_e)
    group_sizes = jnp.bincount(flat_e, length=N_EXPERTS_2).astype(jnp.int32)
    xs = xt[order // TOP_K]
    hid = (jax.nn.silu(lax.ragged_dot(xs, w_gate, group_sizes))
           * lax.ragged_dot(xs, w_up, group_sizes))
    ys = lax.ragged_dot(hid, w_down, group_sizes)
    y = jnp.zeros_like(ys).at[order].set(ys).reshape(b * t, TOP_K, d)
    out = jnp.einsum('nk,nkd->nd', gates.astype(y.dtype), y)
    return out.reshape(b, t, d)

def second_inputs(seed: int = 0) -> dict:
    key = jax.random.key(seed)
    ks = jax.random.split(key, 24)
    f32 = jnp.float32

    def nrm(k, shape, scale):
        return jax.random.normal(k, shape, f32) * scale

    def gain(k, shape):
        return 1.0 + 0.02 * jax.random.normal(k, shape, f32)

    ds = D_MODEL ** -0.5
    return {
        "x": nrm(ks[0], (BATCH, SEQ, D_MODEL), 1.0),
        "positions": jnp.broadcast_to(jnp.arange(SEQ, dtype=jnp.int32), (BATCH, SEQ)),
        "norm_mix_g": gain(ks[1], (DEPTH_2, D_MODEL)),
        "norm_ffn_g": gain(ks[2], (DEPTH_2, D_MODEL)),
        "final_norm_g": gain(ks[3], (D_MODEL,)),
        "ab_w_in": nrm(ks[4], (N_EVEN, D_MODEL, AB_IN), ds),
        "gla_w_a2": nrm(ks[5], (N_EVEN, GLA_RANK, GLA_HEADS * GLA_DK), GLA_RANK ** -0.5),
        "gla_b_a2": nrm(ks[6], (N_EVEN, GLA_HEADS * GLA_DK), 0.1),
        "ret_norm_g": gain(ks[7], (N_EVEN, RET_DV)),
        "gla_norm_g": gain(ks[8], (N_EVEN, GLA_DV)),
        "ab_w_out": nrm(ks[9], (N_EVEN, D_MODEL, D_MODEL), ds * OUT_SCALE),
        "ffn_w_gate": nrm(ks[10], (N_EVEN, D_MODEL, D_FF), ds),
        "ffn_w_up": nrm(ks[11], (N_EVEN, D_MODEL, D_FF), ds),
        "ffn_w_down": nrm(ks[12], (N_EVEN, D_FF, D_MODEL), D_FF ** -0.5 * OUT_SCALE),
        "hgrn_lb_logits": nrm(ks[13], (DEPTH_2, HGRN_HEADS * HGRN_DK), 0.1),
        "c_w_in": nrm(ks[14], (N_ODD, D_MODEL, C_IN), ds),
        "hgrn_norm_g": gain(ks[15], (N_ODD, HGRN_DV)),
        "c_w_out": nrm(ks[16], (N_ODD, D_MODEL, D_MODEL), ds * OUT_SCALE),
        "moe_router": nrm(ks[17], (N_ODD, D_MODEL, N_EXPERTS_2), ds),
        "moe_w_gate": nrm(ks[18], (N_ODD, N_EXPERTS_2, D_MODEL, EXPERT_FF_2), ds),
        "moe_w_up": nrm(ks[19], (N_ODD, N_EXPERTS_2, D_MODEL, EXPERT_FF_2), ds),
        "moe_w_down": nrm(ks[20], (N_ODD, N_EXPERTS_2, EXPERT_FF_2, D_MODEL), EXPERT_FF_2 ** -0.5 * OUT_SCALE),
    }

def second_block(x, positions, norm_mix_g, norm_ffn_g, final_norm_g, ab_w_in, gla_w_a2, gla_b_a2,
              ret_norm_g, gla_norm_g, ab_w_out, ffn_w_gate, ffn_w_up, ffn_w_down,
              hgrn_lb_logits, c_w_in, hgrn_norm_g, c_w_out, moe_router, moe_w_gate,
              moe_w_up, moe_w_down):
    lb_cum = jnp.cumsum(jax.nn.softmax(hgrn_lb_logits.astype(jnp.float32), axis=0), axis=0)
    lower_bounds = lb_cum - lb_cum[0:1]
    h = x
    for l in range(DEPTH_2):
        e = l // 2
        hn = rms_norm_2(h, norm_mix_g[l])
        if l % 2 == 0:
            h = h + retnet_gla_mixer(hn, positions, ab_w_in[e], gla_w_a2[e], gla_b_a2[e],
                                     ret_norm_g[e], gla_norm_g[e], ab_w_out[e])
            h = h + swiglu(rms_norm_2(h, norm_ffn_g[l]), ffn_w_gate[e], ffn_w_up[e], ffn_w_down[e])
        else:
            lb = lower_bounds[l].reshape(HGRN_HEADS, HGRN_DK)
            h = h + hgrn2_mixer(hn, lb, c_w_in[e], hgrn_norm_g[e], c_w_out[e])
            h = h + moe_swiglu(rms_norm_2(h, norm_ffn_g[l]), moe_router[e], moe_w_gate[e],
                               moe_w_up[e], moe_w_down[e])
    return rms_norm_2(h, final_norm_g)


def setup_inputs(seed=0):
    out = dict(first_inputs(seed))
    for name, value in second_inputs(seed + 1).items():
        if name != "x":
            out[name + "_2"] = value
    return out


def reference(
    x, mix_norm_g, w_in, conv_a_w, conv_a_norm_g, dn_conv_w, dn_a_log, dn_dt_bias, dn_norm_g,
    w_out, ffn_norm_g, router_group_w, router_expert_w, w_gate, w_up, w_down, final_norm_g,
    positions_2, norm_mix_g_2, norm_ffn_g_2, final_norm_g_2, ab_w_in_2, gla_w_a2_2, gla_b_a2_2,
    ret_norm_g_2, gla_norm_g_2, ab_w_out_2, ffn_w_gate_2, ffn_w_up_2, ffn_w_down_2,
    hgrn_lb_logits_2, c_w_in_2, hgrn_norm_g_2, c_w_out_2, moe_router_2, moe_w_gate_2,
    moe_w_up_2, moe_w_down_2,
):
    x = first_block(
        x, mix_norm_g, w_in, conv_a_w, conv_a_norm_g, dn_conv_w, dn_a_log, dn_dt_bias,
        dn_norm_g, w_out, ffn_norm_g, router_group_w, router_expert_w, w_gate, w_up, w_down,
        final_norm_g,
    )
    return second_block(
        x, positions_2, norm_mix_g_2, norm_ffn_g_2, final_norm_g_2, ab_w_in_2, gla_w_a2_2,
        gla_b_a2_2, ret_norm_g_2, gla_norm_g_2, ab_w_out_2, ffn_w_gate_2, ffn_w_up_2,
        ffn_w_down_2, hgrn_lb_logits_2, c_w_in_2, hgrn_norm_g_2, c_w_out_2, moe_router_2,
        moe_w_gate_2, moe_w_up_2, moe_w_down_2,
    )


_drawn_inputs = setup_inputs


def setup_inputs(seed=0):
    import zlib

    import numpy as np

    out = dict(_drawn_inputs(seed))
    spreads = {}
    factors = {'norm_mix_g_2': 2.91,
     'norm_ffn_g_2': 9.13,
     'final_norm_g_2': 8.076,
     'gla_b_a2_2': 4.074,
     'ret_norm_g_2': 22.853,
     'gla_norm_g_2': 8.0,
     'hgrn_lb_logits_2': 8.0,
     'hgrn_norm_g_2': 30.417}
    for name, (base, spread) in spreads.items():
        noise = np.random.default_rng([zlib.crc32(name.encode()), seed]).standard_normal(out[name].shape)
        drawn = base * np.exp(spread * noise) if base else spread * noise
        out[name] = __import__('jax').numpy.asarray(drawn.astype(out[name].dtype))
    for name, factor in factors.items():
        out[name] = (out[name] * factor).astype(out[name].dtype)
    return out
```

```python
from contextlib import ExitStack

import concourse.bass as bass
from concourse import mybir
import numpy as np

F32 = mybir.dt.float32
F32R = mybir.dt.float32r
I32 = mybir.dt.int32
ALU = mybir.AluOpType
ACT = mybir.ActivationFunctionType
AX_X = mybir.AxisListType.X
EXP_LN = "natural_log_exp_and_others"

P = 128
T = 256
NT = T // P
D = 1024
KC = D // P
CH = 64
NCH = T // CH
H4 = 4
HC = H4 * T
PIECE = 4096
SLOTS = 7
DENSE_SLOTS = 5
TOKENS, HIS = 5, 6
LEVELS = (32, 16, 8, 4, 2, 1)
EPS = 1e-6
BIG = 1e30

C_EYE, C_GROUP, C_CAUSAL, C_BEFORE, C_IOTA, C_ROT = (n * P for n in range(6))
C_LEVEL = 6 * P
C_RET = C_LEVEL + len(LEVELS) * P
C_RETQ = C_RET + H4 * P
C_RETK = C_RETQ + H4 * CH
C_HALF = C_RETK + H4
C_FREQ = C_HALF + 2
C_DESC = C_FREQ + 1
C_SMALL_END = C_DESC + 32
CONSTS = C_SMALL_END

_SMALL = [("mix_g", 8), ("ffn_g", 8), ("final_g", 8), ("mix2_g", 16), ("ffn2_g", 16), ("final2_g", 8),
          ("conv_a", 12), ("conv_a_g", 4), ("dn_conv", 48), ("dn_g", 1), ("ret_g", 1), ("gla_g", 1),
          ("hgrn_g", 1), ("lb", 16), ("gla_b", 2), ("a_log", 4), ("dt_bias", 4), ("router1", 288),
          ("router2", 64), ("tail1", 64), ("tail2", 128), ("gla_w", 256)]
SMALL = {}
_at = 0
for _name, _n in _SMALL:
    SMALL[_name] = _at
    _at += _n
SMALLS = _at

LOG_GAMMA = np.log1p(-np.exp2(-5.0 - np.arange(4, dtype=np.float32))).astype(np.float32)
CHUNK_DECAY = [float(x) for x in np.exp(CH * LOG_GAMMA)]


def constants():
    p, f = np.arange(P)[:, None], np.arange(P)[None, :]
    same = p // CH == f // CH
    c = np.zeros((P, CONSTS), np.float32)
    c[:, C_EYE:C_EYE + P] = p == f
    c[:, C_GROUP:C_GROUP + P] = same
    c[:, C_CAUSAL:C_CAUSAL + P] = same & (p <= f)
    c[:, C_BEFORE:C_BEFORE + P] = p < f
    c[:, C_IOTA:C_IOTA + P] = f
    c[:, C_ROT:C_ROT + P] = np.where(p == f + 64, -1.0, 0.0) + np.where(p == f - 64, 1.0, 0.0)
    for n, s in enumerate(LEVELS):
        both = p // (2 * s) == f // (2 * s)
        c[:, C_LEVEL + n * P:C_LEVEL + (n + 1) * P] = both & (p % (2 * s) < s) & (f % (2 * s) >= s)
    for h in range(H4):
        rel = (f - p).astype(np.float32)
        c[:, C_RET + h * P:C_RET + (h + 1) * P] = np.where(same & (p <= f), np.exp(np.minimum(rel, P) * LOG_GAMMA[h]), 0)
        c[:, C_RETQ + h * CH:C_RETQ + (h + 1) * CH] = np.exp((np.arange(CH, dtype=np.float32) + 1) * LOG_GAMMA[h])
        c[:, C_RETK + h] = np.exp((CH - 1.0 - np.arange(P) % CH) * LOG_GAMMA[h])
    c[:, C_HALF] = np.arange(P) < CH
    c[:, C_HALF + 1] = np.arange(P) >= CH
    c[:, C_FREQ] = np.float32(10000.0) ** (-(np.arange(P) % 64 * 2).astype(np.float32) / 128)
    c[:, C_DESC:C_DESC + 32] = 32 - np.arange(32)
    return c


class Steps:

    def __init__(self, sem, label, known, found):
        self.sem, self.label, self.known, self.found, self.n = sem, label, known, found, 0

    def step(self):
        self.n += 1
        return self.sem, 1

    def name(self, what):
        assert (self.label, what) not in self.found, (self.label, what)
        self.found[self.label, what] = self.n

    def at(self, what):
        return self.sem, self.known[self.label, what] if self.known else 1

    def last(self, back=0):
        return self.sem, self.n - back


def program(nc, known, A, upto=99):
    found = {}
    ctx = ExitStack()
    with ctx:
        def sb(name, shape, dt=F32):
            return ctx.enter_context(nc.sbuf_tensor(name, shape, dt))

        def sem(name):
            return ctx.enter_context(nc.semaphore(name))

        def steps(label):
            return Steps(sem(label), label, known, found)

        def two_views(name, shape, cuts):
            with ExitStack() as parts:
                rounded = [parts.enter_context(nc.sbuf_tensor(f"{name}_r{n}", [P, size], F32R))
                           for n, size in enumerate(cuts)]
            return sb(name, shape), rounded

        ring, ring_r = two_views("ring", [P, SLOTS, PIECE], [PIECE] * SLOTS)
        xT = sb("xT", [P, KC, T])
        hT = sb("hT", [P, KC, T])
        consts = sb("consts", [P, CONSTS])
        small = sb("small", [P, SMALLS])
        ones = sb("ones", [P, P])
        zero1 = sb("zero1", [P, 4])
        ARENA = 20700
        ARENA_CUTS = [2400, 7984, 10240]
        arena, arena_r = two_views("arena", [P, ARENA], ARENA_CUTS)
        trips = sb("trips", [P, 2], I32)
        psum = ctx.enter_context(nc.psum_tensor("psum", [P, 8, 512], F32))

        eye = consts[:, C_EYE:C_EYE + P]
        group_ones = consts[:, C_GROUP:C_GROUP + P]
        causal = consts[:, C_CAUSAL:C_CAUSAL + P]
        before = consts[:, C_BEFORE:C_BEFORE + P]

        def level_mask(n):
            return consts[:, C_LEVEL + n * P:C_LEVEL + (n + 1) * P]

        def param(name, n=1, at=0):
            return small[:, SMALL[name] + at:SMALL[name] + at + n]

        def carve(at, n):
            assert at + n <= ARENA
            return arena[:, at:at + n]

        def carve_r(at, n):
            part = 0
            while at >= ARENA_CUTS[part]:
                at -= ARENA_CUTS[part]
                part += 1
            assert at + n <= ARENA_CUTS[part]
            return arena_r[part][:, at:at + n]

        def bank(b, n=1):
            return psum[:, b:b + n, :].rearrange("p b c -> p (b c)")

        def per_head(ap):
            return ap.rearrange("p (h t) -> p h t", h=H4)

        def inst(ap, h, t):
            return ap[:, h * T + t * P:h * T + t * P + P]

        def spread(mask, n=8):
            return mask.unsqueeze(1).to_broadcast([P, n, P])

        def blocks(ap):
            return ap.rearrange("p (n i) -> p n i", i=P)

        loaded_small = sem("loaded_small")
        loaded_x = sem("loaded_x")
        landed = {part: [sem(f"{part}_landed_{s}") for s in range(SLOTS)]
                  for part in ("one", "moe1", "two", "moe2")}
        loaded_positions = sem("loaded_positions")
        out_written = sem("out_written")
        stages = ("mix1", "route1", "mix2", "ffn", "hgrn", "route2", "final")
        V = {s: steps(f"{s}_vector") for s in stages}
        S = {s: steps(f"{s}_scalar") for s in stages}
        E = {s: steps(f"{s}_tensor") for s in stages}
        G = {s: steps(f"{s}_pool") for s in stages}
        moe_sems = {}
        for m in ("moe1", "moe2"):
            moe_sems[m] = {w: sem(f"{m}_{w}") for w in (
                "gate_done", "up_done", "silu_done", "hidden_done", "hiddenT_done", "hiddenT_kept",
                "down_done", "y_kept", "shareT_done", "shareT_kept", "spread_done", "spread_added",
                "gathered", "gathered_kept", "pick_ready", "share_ready", "start")}
        gathered_lo, hiddenT_lo = sem("moe2_gathered_lo"), sem("moe2_hiddenT_lo")
        weights_hi, weights_lo = sem("moe2_weights_hi"), sem("moe2_weights_lo")

        def cols(w, c0, n=512):
            return w[:, c0:c0 + n].rearrange("(k p) n -> p k n", p=P), KC, n

        def rows(w, r0, k):
            return w[r0:r0 + k * P, :].rearrange("(k p) n -> p k n", p=P), k, D

        w_in, w_out = A["w_in"][0], A["w_out"][0]
        ab_in, ab_out = A["ab_w_in_2"][0], A["ab_w_out_2"][0]
        c_in, c_out = A["c_w_in_2"][0], A["c_w_out_2"][0]
        ffn_g, ffn_u, ffn_d = A["ffn_w_gate_2"][0], A["ffn_w_up_2"][0], A["ffn_w_down_2"][0]
        FF = ffn_g.shape[1]
        FFC = FF // 256
        ONE = [("a_h", cols(w_in, 0)), ("a_c", cols(w_in, 1024)), ("a_b", cols(w_in, 512)),
               ("q", cols(w_in, 1536)), ("k", cols(w_in, 2048)), ("v", cols(w_in, 2560)),
               ("z", cols(w_in, 3072)), ("out1_0", cols(w_out, 0)), ("out1_1", cols(w_out, 512))]
        TWO = [("bqk", cols(ab_in, 2048)), ("aq", cols(ab_in, 0)), ("ak", cols(ab_in, 512)),
               ("bv", cols(ab_in, 2560)), ("av", cols(ab_in, 1024)), ("bg", cols(ab_in, 3072)),
               ("ag", cols(ab_in, 1536)), ("out2_0", cols(ab_out, 0)), ("out2_1", cols(ab_out, 512))]
        for c in range(FFC):
            TWO.append((f"ffn_gu{c}", (cols(ffn_g, c * 256, 256), cols(ffn_u, c * 256, 256))))
            if c:
                TWO.append((f"ffn_d{c - 1}", rows(ffn_d, (c - 1) * 256, 2)))
        TWO.append((f"ffn_d{FFC - 1}", rows(ffn_d, (FFC - 1) * 256, 2)))
        for half in range(2):
            for what, at in (("f", 1024), ("q", 0), ("i", 2048), ("g", 3072)):
                TWO.append((f"h{what}{half}", cols(c_in, at + half * 512)))
        TWO += [("out3_0", cols(c_out, 0)), ("out3_1", cols(c_out, 512))]
        order = {"one": [n for n, _ in ONE], "two": [n for n, _ in TWO]}

        def piece(part, name):
            n = order[part].index(name)
            before_ = [order[part][m] for m in range(n % DENSE_SLOTS, n + 1, DENSE_SLOTS)]
            return (ring[:, n % DENSE_SLOTS, :], landed[part][n % DENSE_SLOTS],
                    sum(32 if x.startswith("ffn_gu") else 16 for x in before_))

        def slot_of(part, name):
            return order[part].index(name) % DENSE_SLOTS

        def piece_used(name):
            stage = ("mix1" if name in order["one"] else "ffn" if name.startswith("ffn") else
                     "hgrn" if name[0] == "h" or name.startswith("out3") else "mix2")
            return E[stage].at(f"{name}_1")

        NE1, NE2, FF1, FF2 = 32, 8, 512, 3584
        PAIRS = NE1 // 2
        UNITS = FF2 // 512
        C1, C2 = 64, 128
        PASSES1, PASSES2 = T // C1, T // C2
        wg1, wu1, wd1 = A["w_gate"][0], A["w_up"][0], A["w_down"][0]
        wg2, wu2, wd2 = A["moe_w_gate_2"][0], A["moe_w_up_2"][0], A["moe_w_down_2"][0]
        MOE2_ORDER = [("g", 0), ("u", 0)]
        for u in range(1, UNITS):
            MOE2_ORDER += [("g", u), ("u", u), ("d", u - 1)]
        MOE2_ORDER += [("d", UNITS - 1)]
        NP2 = len(MOE2_ORDER)
        TURNS2 = NP2 // SLOTS
        assert NP2 % SLOTS == 0

        tail_at = HC * 10
        a_pos = carve(tail_at + HC * 8, T).bitcast(I32)
        block = ctx.enter_context(nc.Block())

        @block.sync
        def _(sp):
            sp.dma_start(xT[:, :, :], A["xT"]).then_inc(loaded_x, 16)

            def send(view, slot, landed_sem):
                src, k, n = view
                sp.dma_start(ring[:, slot, 0:k * n].rearrange("p (k n) -> p k n", n=n), src)\
                    .then_inc(landed_sem, 16)

            def send_part(part, pieces, wait_before=None):
                for n, (name, view) in enumerate(pieces):
                    slot = n % DENSE_SLOTS
                    if n >= DENSE_SLOTS:
                        sp.wait_ge(*piece_used(pieces[n - DENSE_SLOTS][0]))
                    elif wait_before is not None:
                        wait_before(slot)
                    if name.startswith("ffn_gu"):
                        for half, (src, k, w) in enumerate(view):
                            sp.dma_start(ring[:, slot, :].rearrange("p (k a n) -> p k a n", a=2, n=256)[:, :, half, :],
                                         src).then_inc(landed[part][slot], 16)
                    else:
                        send(view, slot, landed[part][slot])

            send_part("one", ONE)

            if upto == 1:
                sp.wait_ge(*V["mix1"].at("x_out1"))
                sp.dma_start(A["out"], xT[:, :, :]).then_inc(out_written, 16)
                sp.wait_ge(out_written, 16)
                return
            def moe1_piece(expert, s):
                w, k, n = ((wg1, KC, FF1), (wu1, KC, FF1), (wd1, 4, D))[s // 2]
                return w[bass.ds(expert, 1), :, :].rearrange("e (k p) n -> p (e k) n", p=P), k, n

            n_one = len(ONE)
            for s in range(6):
                if s < DENSE_SLOTS:
                    last = max(n for n in range(n_one) if n % DENSE_SLOTS == s)
                    sp.wait_ge(*piece_used(ONE[last][0]))
                else:
                    sp.wait_ge(*piece_used("z"))
                w, k, n = ((wg1, KC, FF1), (wu1, KC, FF1), (wd1, 4, D))[s // 2]
                send((w[s % 2].rearrange("(k p) n -> p k n", p=P), k, n), s, landed["moe1"][s])
            sp.wait_ge(*V["route1"].at("trips"))
            trips1 = sp.value_load(trips[0:1, 0:1], min_val=PAIRS, max_val=PAIRS * PASSES1)
            pair_reg = sp.alloc_register("pair")
            with sp.Fori(1, trips1) as i:
                sp.reg_alu(pair_reg, i, PAIRS - 1, op=ALU.bitwise_and)
                pair = sp.snap(pair_reg, min_val=0, max_val=PAIRS - 1)
                expert = [sp.snap(pair * 2 + x, min_val=x, max_val=NE1 - 2 + x) for x in range(2)]
                for s in range(6):
                    sp.wait_ge(moe_sems["moe1"][("gate_done", "up_done", "down_done")[s // 2]], i + 1)
                    send(moe1_piece(expert[s % 2], s), s, landed["moe1"][s])

            def after_moe1(slot):
                if slot < 6:
                    sp.wait_ge(moe_sems["moe1"][("gate_done", "up_done", "down_done")[slot // 2]], trips1 + 1)

            if upto == 2:
                sp.wait_ge(moe_sems["moe1"]["spread_added"], trips1 * 4 + 5)
                sp.dma_start(A["out"], xT[:, :, :]).then_inc(out_written, 16)
                sp.wait_ge(out_written, 16)
                return
            sp.wait_ge(moe_sems["moe1"]["spread_added"], trips1 * 4 + 5)
            sp.dma_start(a_pos, A["positions"]).then_inc(loaded_positions, 16)
            for up_, mark in ((3, ("mix2", "x_out2")), (4, ("ffn", "x")), (5, ("hgrn", "x_out3"))):
                if upto == up_:
                    stop_after = {3: "out2_1", 4: f"ffn_d{FFC - 1}", 5: "out3_1"}[up_]
                    k_ = [n for n, _ in TWO].index(stop_after) + 1
                    send_part("two", TWO[:k_], after_moe1)
                    sp.wait_ge(*V[mark[0]].at(mark[1]))
                    sp.dma_start(A["out"], xT[:, :, :]).then_inc(out_written, 16)
                    sp.wait_ge(out_written, 16)
                    return
            send_part("two", TWO, after_moe1)

            n_two = len(TWO)

            def moe2_piece(e, m):
                what, u = MOE2_ORDER[m]
                if what == "d":
                    return (wd2[bass.ds(e, 1), u * 512:(u + 1) * 512, :] if not isinstance(e, int)
                            else wd2[e:e + 1, u * 512:(u + 1) * 512, :]).rearrange("e (k p) n -> p (e k) n", p=P), 4, D
                w = wg2 if what == "g" else wu2
                return (w[bass.ds(e, 1), :, u * 512:(u + 1) * 512] if not isinstance(e, int)
                        else w[e:e + 1, :, u * 512:(u + 1) * 512]).rearrange("e (k p) n -> p (e k) n", p=P), KC, 512

            def moe2_used(i, m):
                what, u = MOE2_ORDER[m - SLOTS]
                sem_ = moe_sems["moe2"][{"g": "gate_done", "u": "up_done", "d": "down_done"}[what]]
                return sem_, i * UNITS + (u + 2 - (UNITS if m < SLOTS else 0))

            for m in range(NP2):
                slot = m % SLOTS
                if m < SLOTS:
                    last = max(n for n in range(n_two) if n % DENSE_SLOTS == slot) if slot < DENSE_SLOTS else None
                    sp.wait_ge(*piece_used("hg1" if last is None else TWO[last][0]))
                else:
                    sp.wait_ge(*moe2_used(0, m))
                send(moe2_piece(0, m), slot, landed["moe2"][slot])
            sp.wait_ge(*V["route2"].at("trips"))
            trips2 = sp.value_load(trips[0:1, 1:2], min_val=NE2, max_val=NE2 * PASSES2)
            expert_reg = sp.alloc_register("expert")
            with sp.Fori(1, trips2) as i:
                sp.reg_alu(expert_reg, i, NE2 - 1, op=ALU.bitwise_and)
                e = sp.snap(expert_reg, min_val=0, max_val=NE2 - 1)
                for m in range(NP2):
                    sp.wait_ge(*moe2_used(i, m))
                    send(moe2_piece(e, m), m % SLOTS, landed["moe2"][m % SLOTS])
            sp.wait_ge(*moe2_used(trips2, 0))
            send(moe2_piece(0, 0), 0, landed["moe2"][0])

            sp.wait_ge(*V["final"].at("h"))
            sp.dma_start(A["out"], hT[:, :, :]).then_inc(out_written, 16)
            sp.wait_ge(out_written, 16)

        SQ = carve(0, KC * T)
        RSTD = carve(KC * T, T)

        def norm_scalar(act, st, tag, waits):
            s = S[st]
            for w in waits:
                act.wait_ge(*w)
            for half in range(2):
                sq = SQ[:, half * 1024:(half + 1) * 1024]
                nc.scalar.activation(sq.rearrange("p (k t) -> p k t", t=T), xT[:, half * 4:half * 4 + 4, :],
                                     ACT.Square).then_inc(*s.step())
                s.name(f"{tag}_sq{half}")
            act.wait_ge(*E[st].at(f"{tag}_sum"))
            nc.scalar.activation(RSTD, bank(7)[:, 0:T], ACT.Ln, bias=eps_col, scale=1.0 / D).then_inc(*s.step())
            act.wait_ge(*s.last())
            nc.scalar.activation(RSTD, RSTD, ACT.Exp, scale=-0.5).then_inc(*s.step())
            s.name(f"{tag}_rstd")

        def norm_tensor(pe, st, tag, waits=()):
            for w in waits:
                pe.wait_ge(*w)
            for k in range(KC):
                if k % 4 == 0:
                    pe.wait_ge(*S[st].at(f"{tag}_sq{k // 4}"))
                mm = nc.tensor.matmul(bank(7)[:, 0:T], ones[:, :], SQ[:, k * T:(k + 1) * T],
                                      start=(k == 0), stop=(k == KC - 1))
            mm.then_inc(*E[st].step())
            E[st].name(f"{tag}_sum")

        def norm_vector(v, st, tag, gain, out, name, waits=()):
            v.wait_ge(*S[st].at(f"{tag}_rstd"))
            for w in waits:
                v.wait_ge(*w)
            for k in range(KC):
                nc.vector.scalar_tensor_tensor(out[:, k, :], xT[:, k, :], gain[:, k:k + 1], RSTD,
                                               ALU.mult, ALU.mult).then_inc(*V[st].step())
                if k == 3:
                    V[st].name(f"{name}_first")
            V[st].name(name)

        eps_col = zero1[:, 0:1]

        proj_count = [0]

        def three(out, a, b, start, stop, **kw):
            (ah, al), (bh, bl) = a, b
            nc.tensor.matmul(out, ah, bh, start=start, stop=False, **kw)
            nc.tensor.matmul(out, ah, bl, start=False, stop=False, **kw)
            return nc.tensor.matmul(out, al, bh, start=False, stop=stop, **kw)

        tok = [ring_r[TOKENS][:, n * KC * T:(n + 1) * KC * T].rearrange("p (k t) -> p k t", t=T) for n in range(2)]
        w_hi = ring_r[HIS][:, :].rearrange("p (k n) -> p k n", n=512)

        def tokens_hi(act, st, tag="h"):
            for half in range(2):
                act.wait_ge(*V[st].at(tag if half else f"{tag}_first"))
                ks = slice(4 * half, 4 * half + 4)
                nc.scalar.activation(tok[0][:, ks, :], hT[:, ks, :], ACT.Copy).then_inc(*S[st].step())
                S[st].name(f"tok_hi{half}")

        def round_next(act, st, part, names, name, half):
            after = names[names.index(name) + 1]
            if not after.startswith("out"):
                weights_hi_of(act, st, part, after, (2 * half, 2 * half + 1), before=name)

        def tokens_lo(dve, st):
            for half in range(2):
                dve.wait_ge(*S[st].at(f"tok_hi{half}"))
                ks = slice(4 * half, 4 * half + 4)
                nc.vector.tensor_tensor(tok[1][:, ks, :], hT[:, ks, :], tok[0][:, ks, :].bitcast(F32), ALU.subtract)\
                    .then_inc(*V[st].step())
            V[st].name("tok_lo")

        def weights_hi_of(act, st, part, name, quarters, before=None):
            n = order[part].index(name)
            _, landed_sem, value = piece(part, name)
            w = ring[:, n % DENSE_SLOTS, :].rearrange("p (k n) -> p k n", n=512)
            act.wait_ge(landed_sem, value)
            for q in quarters:
                if before is not None:
                    act.wait_ge(*E[st].at(f"{before}_q{q}"))
                c = slice(q * P, (q + 1) * P)
                nc.scalar.activation(w_hi[:, :, c], w[:, :, c], ACT.Copy).then_inc(*S[st].step())
                S[st].name(f"{name}_hi{q}")

        def weights_lo_of(pool, st, part, name):
            n = order[part].index(name)
            w = ring[:, n % DENSE_SLOTS, :].rearrange("p (k n) -> p k n", n=512)
            lo = ring_r[n % DENSE_SLOTS][:, :].rearrange("p (k n) -> p k n", n=512)
            for q in range(4):
                pool.wait_ge(*S[st].at(f"{name}_hi{q}"))
                c = slice(q * P, (q + 1) * P)
                nc.gpsimd.tensor_tensor(lo[:, :, c], w[:, :, c], w_hi[:, :, c].bitcast(F32), ALU.subtract)\
                    .then_inc(*G[st].step())
                G[st].name(f"{name}_lo{q}")

        def project(pe, st, part, name, free):
            lo = ring_r[slot_of(part, name)][:, :].rearrange("p (k n) -> p k n", n=512)
            b0 = 2 * (proj_count[0] % 2)
            proj_count[0] += 1
            pe.wait_ge(*V[st].at("tok_lo"))
            for q in range(4):
                half, j = q // 2, q % 2
                if j == 0:
                    for wait in free(half):
                        pe.wait_ge(*wait)
                pe.wait_ge(*G[st].at(f"{name}_lo{q}"))
                c = slice(q * P, (q + 1) * P)
                for k in range(KC):
                    mm = three(bank(b0 + half)[:, j * T:(j + 1) * T], (w_hi[:, k, c], lo[:, k, c]),
                               (tok[0][:, k, :], tok[1][:, k, :]), k == 0, k == KC - 1)
                mm.then_inc(*E[st].step())
                E[st].name(f"{name}_q{q}")
                if j == 1:
                    E[st].name(f"{name}_{half}")
            return b0

        def project_rows(pe, st, part, name, free):
            lo = ring_r[slot_of(part, name)][:, :].rearrange("p (k n) -> p k n", n=512)
            b0 = 2 * (proj_count[0] % 2)
            proj_count[0] += 1
            pe.wait_ge(*V[st].at("tok_lo"))
            for half in range(2):
                pe.wait_ge(*G[st].at(f"{name}_lo{2 * half + 1}"))
                c = slice(half * 256, (half + 1) * 256)
                for t in range(NT):
                    if half == 0:
                        for wait in free(t):
                            pe.wait_ge(*wait)
                    ts = slice(t * P, (t + 1) * P)
                    for k in range(KC):
                        mm = three(bank(b0 + t)[:, c], (tok[0][:, k, ts], tok[1][:, k, ts]),
                                   (w_hi[:, k, c], lo[:, k, c]), k == 0, k == KC - 1)
                    mm.then_inc(*E[st].step())
                    if half == 1:
                        E[st].name(f"{name}_{t}")
                for q in (2 * half, 2 * half + 1):
                    E[st].name(f"{name}_q{q}")
            return b0

        class OutProjection:

            def __init__(self, pe, st, part, tag, src, early, waits):
                self.pe, self.st, self.part, self.tag, self.early, self.done = pe, st, part, tag, early, 0
                self.src = src.rearrange("p (k t) -> p k t", t=T)
                self.waits = waits

            def block(self, b, chunks, first):
                wt, _, _ = piece(self.part, f"{self.tag}_{b // 4}")
                w = wt.rearrange("p (k n) -> p k n", n=512)
                for k in chunks:
                    mm = nc.tensor.matmul(bank(b // 2)[:, (b % 2) * T:(b % 2 + 1) * T],
                                          w[:, k, (b % 4) * P:(b % 4 + 1) * P], self.src[:, k, :],
                                          start=(first and k == chunks[0] and b % 2 == 0),
                                          stop=(not first and k == chunks[-1]), skip_group_check=True)
                return mm

            def fill(self, n):
                for _ in range(n):
                    if self.done == 8:
                        return
                    if self.done == 0:
                        for w in self.waits:
                            self.pe.wait_ge(*w)
                    if self.done % 4 == 0:
                        _, landed_sem, value = piece(self.part, f"{self.tag}_{self.done // 4}")
                        self.pe.wait_ge(landed_sem, value)
                    self.block(self.done, self.early, True)
                    self.done += 1

            def finish(self, ready):
                self.fill(8)
                self.pe.wait_ge(*ready)
                late = [k for k in range(KC) if k not in self.early]
                for b in range(8):
                    mm = self.block(b, late, False)
                    if b % 2:
                        mm.then_inc(*E[self.st].step())
                        E[self.st].name(f"{self.tag}_{b // 4}_{b % 4 // 2}")
                proj_count[0] += 2

        PROJ1 = ["a_h", "a_c", "a_b", "q", "k", "v", "z", "out1_0", "out1_1"]
        PROJ2 = ["bqk", "aq", "ak", "bv", "av", "bg", "ag", "out2_0", "out2_1"]
        PROJ3 = [f"h{w}{half}" for half in range(2) for w in "fqig"] + ["out3_0", "out3_1"]

        def free_by(st, names, name, marks):
            n = names.index(name)
            return (lambda half: []) if n < 2 else (lambda half: marks(names[n - 2], half))

        m1_convin = carve(0, 12 * 260).rearrange("p (b t) -> p b t", t=260)
        m1_conv = carve(3120, 3 * HC)
        m1_ycat = carve(3120 + 3 * HC, KC * T)
        m1_sz = carve(3120 + 3 * HC + 2048, HC)
        base = 3120 + 3 * HC + 3072
        m1_ahx = carve(base, 4 * 260).rearrange("p (b t) -> p b t", t=260)
        m1_ab = carve(base + 1040, HC)
        m1_ac = carve(base + 2064, HC)
        base += 3088
        m1_mt = [carve(base, HC), carve(base + HC, HC)]
        m1_sq = m1_mt
        base += 2 * HC
        m1_AT = carve(base, HC)
        m1_vb, m1_kbg, m1_kd = (carve(base + HC * (1 + n), HC) for n in range(3))
        base += 4 * HC
        m1_S = [carve(base, 512), carve(base + 512, 512)]
        base += 1024
        m1_g = carve(base, 128)
        base += 128
        m1_expG, m1_kb, m1_DT = (carve(HC * n, HC) for n in range(3))
        m1_LT = m1_kb
        m1_X, m1_Y, m1_U = (carve(3120 + 3 * HC + 3072 + HC * n, HC) for n in range(3))
        m1_kd2 = m1_expG
        m1_u, m1_wT = m1_mt
        m1_o = m1_U
        m1_q, m1_k, m1_v = (m1_conv[:, n * HC:(n + 1) * HC] for n in range(3))
        gcol = {n: m1_g[:, 8 * i:8 * i + 8] for i, n in enumerate(
            ("beta", "g", "gc", "gl", "t0", "t1", "t2", "t3", "egc", "kdec0", "kdec1", "bg"))}

        def ht(ap):
            return ap.rearrange("p (h t) -> p h t", t=NT)

        def mixer1_tensor(pe):
            st = "mix1"
            e, s, v = E[st], S[st], V[st]
            pe.wait_ge(loaded_small, 32)
            pe.wait_ge(*v.at("ready"))
            norm_tensor(pe, st, "n")
            pe.wait_ge(*v.at("h"))
            tail = param("tail1", 64).rearrange("p (k n) -> p k n", n=8)
            for t in range(NT):
                for k in range(KC):
                    mm = nc.tensor.matmul(bank(6)[:, t * 8:t * 8 + 8], hT[:, k, t * P:(t + 1) * P], tail[:, k, :],
                                          start=(k == 0), stop=(k == KC - 1))
            mm.then_inc(*e.step())
            e.name("tail")

            def proj(name):
                project(pe, st, "one", name, free_by(st, PROJ1, name, lambda n, half: [s.at(f"{n}_{half}")]))

            for name in ("a_h", "a_c", "a_b", "q"):
                proj(name)
            pe.wait_ge(*v.at("g"))
            gv = ht(gcol["g"])
            for h in range(1):
                nc.tensor.matmul(bank(6)[:, 16:24], causal, gcol["g"], start=True, stop=True)
                mm = nc.tensor.matmul(bank(6)[:, 24:32], group_ones, gcol["g"], start=True, stop=True)
            mm.then_inc(*e.step())
            e.name("gc")
            for h in range(H4):
                for t in range(NT):
                    mm = nc.tensor.matmul(inst(bank(4, 2), h, t), gv[:, h, t:t + 1].to_broadcast([P, P]), causal,
                                          start=True, stop=True)
            mm.then_inc(*e.step())
            e.name("grow")
            proj("k")
            bv = ht(gcol["beta"])
            pe.wait_ge(*v.at("gcols"))
            for h in range(H4):
                for t in range(NT):
                    mm = nc.tensor.matmul(inst(bank(6, 2), h, t), bv[:, h, t:t + 1].to_broadcast([P, P]), eye,
                                          start=True, stop=True)
            mm.then_inc(*e.step())
            e.name("brow")
            proj("v")
            proj("z")
            pe.wait_ge(*s.at("ya_sq"))
            pe.wait_ge(*s.at("expG"))
            pe.wait_ge(*v.at("DT_raw"))
            for half in range(2):
                mm = nc.tensor.matmul(bank(4 + half), group_ones, m1_sq[0][:, half * 512:(half + 1) * 512],
                                      start=True, stop=True)
            mm.then_inc(*e.step())
            e.name("ya_sum")
            pe.wait_ge(*s.at("q_sq"))
            pe.wait_ge(*s.at("ya_ln"))
            for half in range(2):
                mm = nc.tensor.matmul(bank(4 + half), ones[:, :], m1_sq[0][:, half * 512:(half + 1) * 512],
                                      start=True, stop=True)
            mm.then_inc(*e.step())
            e.name("q_sum")
            pe.wait_ge(*s.at("k_sq"))
            pe.wait_ge(*s.at("z_0"))
            pe.wait_ge(*s.at("z_1"))
            pe.wait_ge(*s.at("v_1"))
            for half in range(2):
                mm = nc.tensor.matmul(bank(half), ones[:, :], m1_sq[1][:, half * 512:(half + 1) * 512],
                                      start=True, stop=True)
            mm.then_inc(*e.step())
            e.name("k_sum")
            pe.wait_ge(*v.at("kb"))
            for h in range(H4):
                for t in range(NT):
                    mm = nc.tensor.matmul(inst(bank(4, 2), h, t), inst(m1_k, h, t), inst(m1_kb, h, t),
                                          start=True, stop=True)
            mm.then_inc(*e.step())
            e.name("LT")
            for h in range(H4):
                for t in range(NT):
                    mm = nc.tensor.matmul(inst(bank(6, 2), h, t), inst(m1_k, h, t), inst(m1_q, h, t),
                                          start=True, stop=True)
            mm.then_inc(*e.step())
            e.name("AT")
            for h in range(H4):
                for t in range(NT):
                    mm = nc.tensor.transpose(inst(bank(0, 2), h, t), inst(m1_k, h, t), eye)
            mm.then_inc(*e.step())
            e.name("krow")
            for h in range(H4):
                for t in range(NT):
                    mm = nc.tensor.transpose(inst(bank(2, 2), h, t), inst(m1_v, h, t), eye)
            mm.then_inc(*e.step())
            e.name("vrow")
            pe.wait_ge(*v.at("Y0"))
            for h in range(H4):
                for t in range(NT):
                    mm = nc.tensor.transpose(inst(bank(4, 2), h, t), inst(m1_Y, h, t), eye)
            mm.then_inc(*e.step())
            e.name("X0")
            pe.wait_ge(*s.at("X0"))
            for n in range(1, len(LEVELS)):
                mt = m1_mt[n % 2]
                pe.wait_ge(*G[st].at(f"MT{n}"))
                if n > 1:
                    pe.wait_ge(*v.at(f"Y{n - 1}"))
                for half in range(2):
                    for j in range(4):
                        c = half * 512 + j * P
                        mm = nc.tensor.matmul(bank(4, 2)[:, c:c + P], mt[:, c:c + P], m1_X[:, c:c + P],
                                              start=True, stop=True)
                    mm.then_inc(*e.step())
                    e.name(f"U{n}_{half}")
                last = n == len(LEVELS) - 1
                if n == 1:
                    pe.wait_ge(*v.at("kvrows"))
                    pe.wait_ge(*v.at("AT"))
                for half in range(2):
                    pe.wait_ge(*s.at(f"U{n}_{half}"))
                    for j in range(4):
                        c = half * 512 + j * P
                        if not last:
                            nc.tensor.matmul(bank(6, 2)[:, c:c + P], m1_Y[:, c:c + P], m1_U[:, c:c + P],
                                             start=True, stop=True)
                        mm = nc.tensor.matmul(bank(0, 2)[:, c:c + P], m1_U[:, c:c + P], m1_Y[:, c:c + P],
                                              start=True, stop=True)
                    mm.then_inc(*e.step())
                    e.name(f"Z{n}_{half}")
            pe.wait_ge(*v.at(f"Y{len(LEVELS) - 1}"))
            for h in range(H4):
                for t in range(NT):
                    mm = nc.tensor.matmul(inst(bank(2, 2), h, t), inst(m1_Y, h, t), inst(m1_vb, h, t),
                                          start=True, stop=True)
            mm.then_inc(*e.step())
            e.name("u")
            for h in range(H4):
                for t in range(NT):
                    mm = nc.tensor.matmul(inst(bank(0, 2), h, t), inst(m1_kbg, h, t), inst(m1_Y, h, t),
                                          start=True, stop=True)
            mm.then_inc(*e.step())
            e.name("wT")
            pe.wait_ge(*s.at("wT"))
            pe.wait_ge(*v.at("u"))
            pe.wait_ge(*v.at("qd"))
            out = OutProjection(pe, st, "one", "out1", m1_ycat, range(4), [v.at("ya_out")])
            for c in range(NCH):
                t, off = c // 2, (c % 2) * CH
                if c:
                    pe.wait_ge(*v.at(f"S{c - 1}"))
                    for h in range(H4):
                        mm = nc.tensor.matmul(bank(4)[:, h * P:(h + 1) * P], inst(m1_wT, h, t),
                                              m1_S[(c - 1) % 2][:, h * P:(h + 1) * P], start=True, stop=True)
                    mm.then_inc(*e.step())
                    e.name(f"vp{c}")
                    out.fill(1)
                    pe.wait_ge(*v.at(f"vn{c}"))
                if c < NCH - 1:
                    kd = (m1_kd, m1_kd2)[c % 2]
                    for h in range(H4):
                        mm = nc.tensor.matmul(bank(5)[:, h * P:(h + 1) * P], inst(kd, h, t), inst(m1_u, h, t),
                                              start=True, stop=True)
                    mm.then_inc(*e.step())
                    e.name(f"Sp{c}")
                for h in range(H4):
                    o = bank(6, 2)[:, h * T + c * CH:h * T + (c + 1) * CH]
                    if c:
                        nc.tensor.matmul(o, m1_S[(c - 1) % 2][:, h * P:(h + 1) * P],
                                         m1_q[:, h * T + c * CH:h * T + (c + 1) * CH], start=True, stop=False)
                    mm = nc.tensor.matmul(o, inst(m1_u, h, t), inst(m1_AT, h, t)[:, off:off + CH],
                                          start=(c == 0), stop=True)
                mm.then_inc(*e.step())
                e.name(f"o{c}")
            out.fill(2)
            pe.wait_ge(*s.at("o_sq"))
            for half in range(2):
                mm = nc.tensor.matmul(bank(4 + half), ones[:, :], m1_sq[1][:, half * 512:(half + 1) * 512],
                                      start=True, stop=True)
            mm.then_inc(*e.step())
            e.name("o_sum")
            out.finish(v.at("y"))

        def mixer1_scalar(act):
            st = "mix1"
            e, s, v = E[st], S[st], V[st]
            act.dma_start(small[:, :], A["small"]).then_inc(loaded_small, 16)
            act.dma_start(consts[:, :], A["consts"]).then_inc(loaded_small, 16)
            act.preload_act_table_set(EXP_LN)
            act.wait_ge(loaded_x, 16)
            act.wait_ge(*v.at("ready"))
            norm_scalar(act, st, "n", [])
            weights_hi_of(act, st, "one", "a_h", range(4))
            tokens_hi(act, st)
            act.wait_ge(*v.at("logits"))
            nc.scalar.activation(gcol["t0"], gcol["beta"], ACT.Exp, scale=-1.0).then_inc(*s.step())
            nc.scalar.activation(gcol["t2"], gcol["t1"], ACT.Exp).then_inc(*s.step())
            act.wait_ge(*s.last())
            nc.scalar.activation(gcol["t2"], gcol["t2"], ACT.Ln, bias=1.0).then_inc(*s.step())
            nc.scalar.activation(m1_g[:, 96:100], param("a_log", 4), ACT.Exp).then_inc(*s.step())
            s.name("gates")

            def keep(name, out, func=ACT.Copy):
                b0 = 2 * (PROJ1.index(name) % 2)
                for half in range(2):
                    round_next(act, st, "one", PROJ1, name, half)
                    act.wait_ge(*e.at(f"{name}_{half}"))
                    nc.scalar.activation(out(half), bank(b0 + half).rearrange("p (b t) -> p b t", t=T),
                                         func).then_inc(*s.step())
                    s.name(f"{name}_{half}")

            def two(ap, half):
                return ap[:, half * 512:(half + 1) * 512].rearrange("p (b t) -> p b t", t=T)

            act.wait_ge(*v.at("pads"))
            keep("a_h", lambda half: m1_ahx[:, 2 * half:2 * half + 2, 2:2 + T])
            keep("a_c", lambda half: two(m1_ac, half))
            keep("a_b", lambda half: two(m1_ab, half))
            keep("q", lambda half: m1_convin[:, 2 * half:2 * half + 2, 3:3 + T])
            act.wait_ge(*v.at("ya"))
            nc.scalar.activation(m1_sq[0], m1_ycat[:, 0:HC], ACT.Square).then_inc(*s.step())
            s.name("ya_sq")
            keep("k", lambda half: m1_convin[:, 4 + 2 * half:6 + 2 * half, 3:3 + T])
            keep("v", lambda half: m1_convin[:, 8 + 2 * half:10 + 2 * half, 3:3 + T])
            act.wait_ge(*v.at("conv2"))
            act.wait_ge(*e.at("grow"))
            nc.scalar.activation(m1_expG, bank(4, 2), ACT.Exp).then_inc(*s.step())
            s.name("expG")
            act.wait_ge(*v.at("gdiff"))
            nc.scalar.activation(m1_g[:, 64:80], m1_g[:, 64:80], ACT.Exp).then_inc(*s.step())
            s.name("gexp")
            act.wait_ge(*v.at("DT_raw"))
            nc.scalar.activation(m1_DT, m1_DT, ACT.Exp).then_inc(*s.step())
            s.name("DT")
            act.wait_ge(*e.at("ya_sum"))
            nc.scalar.activation(m1_ac, bank(4, 2), ACT.Ln, bias=eps_col, scale=1.0 / CH).then_inc(*s.step())
            s.name("ya_ln")
            act.wait_ge(*s.last())
            nc.scalar.activation(m1_ac, m1_ac, ACT.Exp, scale=-0.5).then_inc(*s.step())
            s.name("ya_rstd")
            keep("z", lambda half: two(m1_sz, half), ACT.Silu)
            for n, w in enumerate("qkv"):
                nc.scalar.activation(m1_conv[:, n * HC:(n + 1) * HC], m1_conv[:, n * HC:(n + 1) * HC],
                                     ACT.Silu).then_inc(*s.step())
                s.name(f"silu_{w}")
            for n, w in enumerate("qk"):
                act.wait_ge(*s.at(f"silu_{w}"))
                if n == 0:
                    act.wait_ge(*e.at("ya_sum"))
                nc.scalar.activation(m1_sq[n], m1_conv[:, n * HC:(n + 1) * HC], ACT.Square).then_inc(*s.step())
                s.name(f"{w}_sq")
            act.preload_act_table_set(EXP_LN)
            act.wait_ge(*v.at("ya_out"))
            for n, (w, out, b) in enumerate((("q", m1_X, 4), ("k", m1_Y, 0))):
                act.wait_ge(*e.at(f"{w}_sum"))
                nc.scalar.activation(out, bank(b, 2), ACT.Ln, bias=eps_col).then_inc(*s.step())
                act.wait_ge(*s.last())
                nc.scalar.activation(out, out, ACT.Exp, scale=-0.5).then_inc(*s.step())
                s.name(f"{w}_rstd")
            act.wait_ge(*e.at("X0"))
            nc.scalar.activation(m1_X, bank(4, 2), ACT.Copy).then_inc(*s.step())
            s.name("X0")
            for n in range(1, len(LEVELS)):
                for half in range(2):
                    act.wait_ge(*e.at(f"U{n}_{half}"))
                    if n > 1:
                        act.wait_ge(*e.at(f"Z{n - 1}_{half}"))
                    nc.scalar.activation(m1_U[:, half * 512:(half + 1) * 512], bank(4 + half), ACT.Copy)\
                        .then_inc(*s.step())
                    s.name(f"U{n}_{half}")
            act.wait_ge(*e.at("wT"))
            nc.scalar.activation(m1_wT, bank(0, 2), ACT.Copy).then_inc(*s.step())
            s.name("wT")
            act.wait_ge(*e.at(f"o{NCH - 1}"))
            nc.scalar.activation(m1_o, bank(6, 2), ACT.Copy).then_inc(*s.step())
            s.name("o")
            act.wait_ge(*s.last())
            nc.scalar.activation(m1_sq[1], m1_o, ACT.Square).then_inc(*s.step())
            s.name("o_sq")
            act.wait_ge(*e.at("o_sum"))
            nc.scalar.activation(m1_X, bank(4, 2), ACT.Ln, bias=eps_col, scale=1.0 / P).then_inc(*s.step())
            act.wait_ge(*s.last())
            nc.scalar.activation(m1_X, m1_X, ACT.Exp, scale=-0.5).then_inc(*s.step())
            s.name("o_rstd")

        def mixer1_pool(pool):
            st = "mix1"
            g, v = G[st], V[st]
            for name in PROJ1[:-2]:
                weights_lo_of(pool, st, "one", name)
            for n in range(1, len(LEVELS)):
                if n == 1:
                    pool.wait_ge(*v.at("Y0"))
                else:
                    if n > 2:
                        pool.wait_ge(*E[st].at(f"U{n - 2}_1"))
                m = level_mask(len(LEVELS) - 1 - n)
                nc.gpsimd.tensor_tensor(blocks(m1_mt[n % 2]), blocks(m1_LT), spread(m), ALU.mult)\
                    .then_inc(*g.step())
                g.name(f"MT{n}")

        def mixer1_vector(dve):
            st = "mix1"
            e, s, v = E[st], S[st], V[st]
            nc.vector.memset(ones[:, :], 1.0).then_inc(*v.step())
            nc.vector.memset(eps_col, EPS).then_inc(*v.step())
            v.name("ready")
            dve.wait_ge(loaded_small, 32)
            norm_vector(dve, st, "n", param("mix_g", 8), hT, "h")
            tokens_lo(dve, st)
            dve.wait_ge(*v.last())
            nc.vector.memset(m1_convin[:, :, 0:3], 0.0).then_inc(*v.step())
            nc.vector.memset(m1_ahx[:, :, 0:2], 0.0).then_inc(*v.step())
            v.name("pads")
            dve.wait_ge(*e.at("tail"))
            lg = bank(6)[:, 0:16].rearrange("p (t n) -> p n t", n=8)
            nc.vector.tensor_copy(ht(gcol["beta"]), lg[:, 0:4, :]).then_inc(*v.step())
            nc.vector.tensor_tensor(ht(gcol["t3"]), lg[:, 4:8, :],
                                    param("dt_bias", 4).unsqueeze(2).to_broadcast([P, H4, NT]), ALU.add)\
                .then_inc(*v.step())
            dve.wait_ge(*v.last())
            nc.vector.scalar_tensor_tensor(gcol["t1"], gcol["t3"], -1.0, gcol["t3"], ALU.mult, ALU.min)\
                .then_inc(*v.step())
            v.name("logits")
            dve.wait_ge(*s.at("gates"))
            nc.vector.tensor_scalar(gcol["t0"], gcol["t0"], 1e37, 1.0, ALU.min, ALU.add).then_inc(*v.step())
            nc.vector.scalar_tensor_tensor(gcol["t3"], gcol["t3"], 0.0, gcol["t2"], ALU.max, ALU.add)\
                .then_inc(*v.step())
            dve.wait_ge(*v.last())
            nc.vector.reciprocal(gcol["beta"], gcol["t0"]).then_inc(*v.step())
            nc.vector.scalar_tensor_tensor(ht(gcol["g"]), ht(gcol["t3"]), -1.0,
                                           m1_g[:, 96:100].unsqueeze(2).to_broadcast([P, H4, NT]),
                                           ALU.mult, ALU.mult).then_inc(*v.step())
            v.name("g")
            for half in range(2):
                dve.wait_ge(*s.at(f"a_c_{half}"))
                u = m1_ahx[:, 2 * half:2 * half + 2, 2:2 + T]
                nc.vector.tensor_tensor(u, u, m1_ac[:, half * 512:(half + 1) * 512].rearrange("p (b t) -> p b t", t=T),
                                        ALU.mult).then_inc(*v.step())
            dve.wait_ge(*v.last())
            y = m1_ycat[:, 0:HC].rearrange("p (b t) -> p b t", t=T)
            for tap in range(3):
                for b in range(4):
                    w = param("conv_a", 1, tap * 4 + b)
                    if tap == 0:
                        nc.vector.tensor_scalar(y[:, b, :], m1_ahx[:, b, 0:T], w, None, ALU.mult).then_inc(*v.step())
                    else:
                        dve.wait_ge(*v.last(3))
                        nc.vector.scalar_tensor_tensor(y[:, b, :], m1_ahx[:, b, tap:tap + T], w, y[:, b, :],
                                                       ALU.mult, ALU.add).then_inc(*v.step())
            dve.wait_ge(*v.last())
            dve.wait_ge(*s.at("a_b_1"))
            nc.vector.tensor_tensor(m1_ycat[:, 0:HC], m1_ycat[:, 0:HC], m1_ab, ALU.mult).then_inc(*v.step())
            v.name("ya")
            for n, w in enumerate("qkv"):
                for half in range(2):
                    dve.wait_ge(*s.at(f"{w}_{half}"))
                for tap in range(4):
                    for b in range(4):
                        blk = 4 * n + b
                        out = m1_conv[:, blk * T:(blk + 1) * T]
                        wt = param("dn_conv", 1, tap * 12 + blk)
                        if tap == 0:
                            nc.vector.tensor_scalar(out, m1_convin[:, blk, 0:T], wt, None, ALU.mult)\
                                .then_inc(*v.step())
                        else:
                            dve.wait_ge(*v.last(3))
                            nc.vector.scalar_tensor_tensor(out, m1_convin[:, blk, tap:tap + T], wt, out,
                                                           ALU.mult, ALU.add).then_inc(*v.step())
                v.name(f"conv{n}")
                if n == 0:
                    dve.wait_ge(*e.at("gc"))
                    nc.vector.tensor_copy(m1_g[:, 16:32], bank(6)[:, 16:32]).then_inc(*v.step())
                    v.name("gcols")
            nc.vector.tensor_copy(gcol["egc"], gcol["gc"]).then_inc(*v.step())
            nc.vector.tensor_tensor(gcol["kdec0"], gcol["gl"], gcol["gc"], ALU.subtract).then_inc(*v.step())
            v.name("gdiff")
            dve.wait_ge(*s.at("expG"))
            dve.wait_ge(*v.last())
            for h in range(H4):
                for t in range(NT):
                    nc.vector.tensor_scalar(inst(m1_DT, h, t), inst(bank(4, 2), h, t), ht(gcol["gc"])[:, h, t:t + 1],
                                            0.0, ALU.subtract, ALU.min).then_inc(*v.step())
            v.name("DT_raw")
            dve.wait_ge(*s.at("gexp"))
            nc.vector.tensor_tensor(gcol["bg"], gcol["beta"], gcol["egc"], ALU.mult).then_inc(*v.step())
            nc.vector.tensor_scalar(gcol["kdec1"], gcol["kdec0"], consts[:, C_HALF + 1:C_HALF + 2], None, ALU.mult)\
                .then_inc(*v.step())
            dve.wait_ge(*v.last())
            nc.vector.tensor_scalar(gcol["kdec0"], gcol["kdec0"], consts[:, C_HALF:C_HALF + 1], None, ALU.mult)\
                .then_inc(*v.step())
            dve.wait_ge(*s.at("DT"))
            nc.vector.tensor_tensor(blocks(m1_DT), blocks(m1_DT), spread(causal), ALU.mult).then_inc(*v.step())
            dve.wait_ge(*s.at("ya_rstd"))
            for b in range(4):
                nc.vector.scalar_tensor_tensor(y[:, b, :], y[:, b, :], param("conv_a_g", 1, b),
                                               m1_ac[:, b * T:(b + 1) * T], ALU.mult, ALU.mult).then_inc(*v.step())
            v.name("ya_out")
            dve.wait_ge(*v.last())
            dve.wait_ge(*s.at("q_rstd"))
            nc.vector.scalar_tensor_tensor(m1_q, m1_q, float(P) ** -0.5, m1_X, ALU.mult, ALU.mult)\
                .then_inc(*v.step())
            dve.wait_ge(*s.at("k_rstd"))
            nc.vector.tensor_tensor(m1_k, m1_k, m1_Y, ALU.mult).then_inc(*v.step())
            dve.wait_ge(*v.last())
            dve.wait_ge(*e.at("brow"))
            nc.vector.tensor_tensor(m1_kb, m1_k, bank(6, 2), ALU.mult).then_inc(*v.step())
            v.name("kb")
            dve.wait_ge(*e.at("LT"))
            nc.vector.tensor_tensor(m1_LT, bank(4, 2), m1_DT, ALU.mult).then_inc(*v.step())
            dve.wait_ge(*v.last())
            nc.vector.tensor_tensor(blocks(m1_Y), blocks(m1_LT), spread(level_mask(len(LEVELS) - 1)), ALU.mult)\
                .then_inc(*v.step())
            dve.wait_ge(*v.last())
            nc.vector.scalar_tensor_tensor(blocks(m1_Y), blocks(m1_Y), -1.0, spread(eye), ALU.mult, ALU.add)\
                .then_inc(*v.step())
            v.name("Y0")
            dve.wait_ge(*e.at("AT"))
            nc.vector.tensor_tensor(m1_AT, bank(6, 2), m1_DT, ALU.mult).then_inc(*v.step())
            v.name("AT")

            def by_token(out, in_, col):
                nc.vector.tensor_tensor(blocks(out), blocks(in_), gcol[col].unsqueeze(2).to_broadcast([P, 8, P]),
                                        ALU.mult).then_inc(*v.step())

            nc.vector.tensor_tensor(m1_q, m1_q, m1_expG, ALU.mult).then_inc(*v.step())
            v.name("qd")
            dve.wait_ge(*v.last())
            dve.wait_ge(*e.at("krow"))
            by_token(m1_kbg, bank(0, 2), "bg")
            by_token(m1_kd, bank(0, 2), "kdec0")
            for h in range(H4):
                nc.vector.tensor_copy(m1_g[:, 100 + 4 * h:104 + 4 * h], m1_expG[:, h * T + CH - 1:(h + 1) * T:CH])\
                    .then_inc(*v.step())
            dve.wait_ge(*v.last())
            by_token(m1_kd2, bank(0, 2), "kdec1")
            dve.wait_ge(*e.at("vrow"))
            by_token(m1_vb, bank(2, 2), "beta")
            v.name("kvrows")
            for n in range(1, len(LEVELS)):
                last = n == len(LEVELS) - 1
                for half in range(2):
                    dve.wait_ge(*e.at(f"Z{n}_{half}"))
                    c = slice(half * 512, (half + 1) * 512)
                    if not last:
                        nc.vector.tensor_tensor(m1_X[:, c], m1_X[:, c], bank(6 + half), ALU.subtract)\
                            .then_inc(*v.step())
                    nc.vector.tensor_tensor(m1_Y[:, c], m1_Y[:, c], bank(half), ALU.subtract).then_inc(*v.step())
                v.name(f"Y{n}")
            dve.wait_ge(*e.at("u"))
            nc.vector.tensor_copy(m1_u, bank(2, 2)).then_inc(*v.step())
            v.name("u")
            dve.wait_ge(*v.last())
            for c in range(NCH):
                t, off = c // 2, (c % 2) * CH
                if c:
                    dve.wait_ge(*e.at(f"vp{c}"))
                    u = per_head(m1_u)[off:off + CH, :, t * P:(t + 1) * P]
                    nc.vector.tensor_tensor(u, u, bank(4)[off:off + CH, :].rearrange("p (h n) -> p h n", n=P),
                                            ALU.subtract).then_inc(*v.step())
                    v.name(f"vn{c}")
                if c < NCH - 1:
                    dve.wait_ge(*e.at(f"Sp{c}"))
                    if c > 1:
                        dve.wait_ge(*e.at(f"o{c - 1}"))
                    for h in range(H4):
                        hs = slice(h * P, (h + 1) * P)
                        if c == 0:
                            nc.vector.tensor_copy(m1_S[0][:, hs], bank(5)[:, hs]).then_inc(*v.step())
                        else:
                            nc.vector.scalar_tensor_tensor(m1_S[c % 2][:, hs], m1_S[(c - 1) % 2][:, hs],
                                                           m1_g[:, 100 + 4 * h + c:101 + 4 * h + c], bank(5)[:, hs],
                                                           ALU.mult, ALU.add).then_inc(*v.step())
                    v.name(f"S{c}")
                    dve.wait_ge(*v.last())
            dve.wait_ge(*s.at("o_rstd"))
            yb = m1_ycat[:, HC:2 * HC]
            nc.vector.scalar_tensor_tensor(yb, m1_o, param("dn_g"), m1_X, ALU.mult, ALU.mult).then_inc(*v.step())
            dve.wait_ge(*v.last())
            nc.vector.tensor_tensor(yb, yb, m1_sz, ALU.mult).then_inc(*v.step())
            v.name("y")
            add_residual(dve, st, "out1")

        def add_residual(dve, st, tag):
            for b in range(4):
                dve.wait_ge(*E[st].at(f"{tag}_{b // 2}_{b % 2}"))
                x = xT[:, 2 * b:2 * b + 2, :]
                nc.vector.tensor_tensor(x, x, bank(b).rearrange("p (b t) -> p b t", t=T), ALU.add)\
                    .then_inc(*V[st].step())
            V[st].name(f"x_{tag}")

        r_hrow = carve(2400, NT * D)
        r_base = 2400 + NT * D
        o_Xg, o_silu, o_hid, o_hidT, o_y = (r_base, r_base + 1024, r_base + 1536, r_base + 2048, r_base + 2560)
        x_Xg, x_silu, x_hid, x_hidT, x_y = (carve(o_Xg, 1024), carve(o_silu, 512), carve(o_hid, 512),
                                            carve(o_hidT, 512), carve(o_y, 1024))
        r_base += 3584
        x_pick, x_share, x_shareT = (carve(r_base + 256 * n, 256) for n in range(3))
        r_base += 768
        r_slot, r_gate = (carve(r_base + 280 * n, 280) for n in range(2))
        r_base += 560
        r_work = carve(r_base, 1024)

        HALF = PIECE // 2

        class Moe:

            def __init__(self, name, st, part, per, slots, experts, units, groups, gain, router, cell):
                self.name, self.st, self.part, self.per, self.slots = name, st, part, per, slots
                self.experts, self.units, self.groups, self.gain, self.router = experts, units, groups, gain, router
                self.n_router = experts + groups
                self.iters, self.passes = experts // per, T // slots
                self.width = experts * self.passes + 2 * per
                self.cell = trips[0:1, cell:cell + 1]
                self.sem = moe_sems[name]
                self.slot = r_slot[:, 0:NT * self.width].rearrange("p (t c) -> p t c", t=NT)
                self.gate = r_gate[:, 0:NT * self.width].rearrange("p (t c) -> p t c", t=NT)

            def trip_count(self, eng):
                return eng.value_load(self.cell, min_val=self.iters, max_val=self.iters * self.passes)

            def banks(self, u):
                return (0, 1) if u % 2 == 0 else (4, 5)

        M1 = Moe("moe1", "route1", "moe1", 2, C1, NE1, 1, 4, param("ffn_g", 8), param("router1", 288), 0)
        M2 = Moe("moe2", "route2", "moe2", 1, C2, NE2, UNITS, 0, param("ffn2_g", 8, 8), param("router2", 64), 1)

        def route_tensor(pe, m):
            st = m.st
            e, s, v = E[st], S[st], V[st]
            norm_tensor(pe, st, "n")
            pe.wait_ge(*v.at("h"))
            w = m.router.rearrange("p (k n) -> p k n", k=KC)
            for t in range(NT):
                for k in range(KC):
                    mm = nc.tensor.matmul(bank(6)[:, t * 64:t * 64 + m.n_router], hT[:, k, t * P:(t + 1) * P],
                                          w[:, k, :], start=(k == 0), stop=(k == KC - 1))
            mm.then_inc(*e.step())
            e.name("logits")
            for t in range(NT):
                for half in range(2):
                    for j in range(4):
                        mm = nc.tensor.transpose(bank(2 * t + half)[:, j * P:(j + 1) * P],
                                                 hT[:, 4 * half + j, t * P:(t + 1) * P], eye)
                    mm.then_inc(*e.step())
                    e.name(f"hrow{t}{half}")
            pe.wait_ge(*v.at("chosen"))
            n = m.experts
            A0, A1 = (r_work[:, 64 * t:64 * t + n] for t in range(NT))
            nc.tensor.matmul(bank(7)[:, 0:n], before, A0, start=True, stop=True)
            nc.tensor.matmul(bank(7)[:, 64:64 + n], ones[:, :], A0, start=True, stop=False)
            nc.tensor.matmul(bank(7)[:, 64:64 + n], before, A1, start=False, stop=True)
            nc.tensor.matmul(bank(7)[:, 128:128 + n], ones[:, :], A0, start=True, stop=False)
            nc.tensor.matmul(bank(7)[:, 128:128 + n], ones[:, :], A1, start=False, stop=True).then_inc(*e.step())
            e.name("counted")

        def route_scalar(act, m, waits):
            st = m.st
            e, s, v = E[st], S[st], V[st]
            act.preload_act_table_set(EXP_LN)
            norm_scalar(act, st, "n", waits)
            for t in range(NT):
                for half in range(2):
                    act.wait_ge(*e.at(f"hrow{t}{half}"))
                    nc.scalar.activation(r_hrow[:, t * D + half * 512:t * D + half * 512 + 512], bank(2 * t + half),
                                         ACT.Copy).then_inc(*s.step())
            s.name("hrow")
            w = r_work
            if m.groups:
                act.wait_ge(*v.at("gdiff"))
                nc.scalar.activation(w[:, 512:520], w[:, 512:520], ACT.Exp).then_inc(*s.step())
                s.name("gexp")
            act.wait_ge(*v.at("ediff"))
            nc.scalar.activation(w[:, 520:522], w[:, 520:522], ACT.Exp).then_inc(*s.step())
            s.name("eexp")

        def route_vector(dve, m):
            st = m.st
            e, s, v = E[st], S[st], V[st]
            w = r_work
            n, g = m.experts, m.groups
            norm_vector(dve, st, "n", m.gain, hT, "h")

            def pairs(at, k, stride=64):
                return w[:, at:at + NT * stride].rearrange("p (t c) -> p t c", t=NT)[:, :, 0:k]

            def do(ins):
                ins.then_inc(*v.step())
                dve.wait_ge(*v.last())

            def first_of_max(vals, top, cand, best, onehot, k):
                desc = consts[:, C_DESC:C_DESC + k].unsqueeze(1).to_broadcast([P, NT, k])
                do(nc.vector.reduce_max(top, vals, AX_X))
                do(nc.vector.tensor_tensor(cand, vals, top.unsqueeze(2).to_broadcast([P, NT, k]), ALU.is_equal))
                do(nc.vector.tensor_tensor(cand, cand, desc, ALU.mult))
                do(nc.vector.reduce_max(best, cand, AX_X))
                do(nc.vector.tensor_tensor(onehot, cand, best.unsqueeze(2).to_broadcast([P, NT, k]), ALU.is_equal))

            dve.wait_ge(*e.at("logits"))
            lg = w[:, 128:256].rearrange("p (t c) -> p t c", t=NT)
            do(nc.vector.tensor_copy(lg[:, :, 0:m.n_router],
                                     bank(6)[:, 0:128].rearrange("p (t c) -> p t c", t=NT)[:, :, 0:m.n_router]))
            ex = lg[:, :, g:g + n]
            top, best = w[:, 524:526], w[:, 526:528]
            cand = pairs(256, n)
            if g:
                oneg = pairs(384, g, 4)
                first_of_max(lg[:, :, 0:g], top, cand[:, :, 0:g], best, oneg, g)
                gd = w[:, 512:520].rearrange("p (t c) -> p t c", t=NT)
                nc.vector.tensor_tensor(gd, lg[:, :, 0:g], top.unsqueeze(2).to_broadcast([P, NT, g]), ALU.subtract)\
                    .then_inc(*v.step())
                v.name("gdiff")
                e4 = w[:, 128:256].rearrange("p (t c) -> p t c", t=NT)
                for t in range(NT):
                    lt = e4[:, t, g:g + n].rearrange("p (g c) -> p g c", g=g)
                    sel = oneg[:, t, :].unsqueeze(2).to_broadcast([P, g, n // g])
                    do(nc.vector.tensor_tensor(lt, lt, sel, ALU.mult))
                do(nc.vector.tensor_scalar(oneg, oneg, BIG, -BIG, ALU.mult, ALU.add))
                for t in range(NT):
                    lt = e4[:, t, g:g + n].rearrange("p (g c) -> p g c", g=g)
                    sel = oneg[:, t, :].unsqueeze(2).to_broadcast([P, g, n // g])
                    do(nc.vector.tensor_tensor(lt, lt, sel, ALU.add))
                dve.wait_ge(*s.at("gexp"))
                do(nc.vector.reduce_sum(w[:, 522:524], gd, AX_X))
                do(nc.vector.reciprocal(w[:, 522:524], w[:, 522:524]))
            one1, one2 = pairs(0, n), pairs(392, n, 40 if n <= 40 else 64)
            top2 = w[:, 528:530]
            first_of_max(ex, top, cand, best, one1, n)
            do(nc.vector.scalar_tensor_tensor(ex, one1, -4 * BIG, ex, ALU.mult, ALU.add))
            first_of_max(ex, top2, cand, best, one2, n)
            nc.vector.tensor_tensor(w[:, 520:522], top2, top, ALU.subtract).then_inc(*v.step())
            v.name("ediff")
            dve.wait_ge(*s.at("eexp"))
            do(nc.vector.tensor_scalar(w[:, 530:532], w[:, 520:522], 1.0, None, ALU.add))
            do(nc.vector.reciprocal(w[:, 530:532], w[:, 530:532]))
            if g:
                do(nc.vector.tensor_tensor(w[:, 530:532], w[:, 530:532], w[:, 522:524], ALU.mult))
            do(nc.vector.tensor_tensor(w[:, 532:534], w[:, 530:532], w[:, 520:522], ALU.mult))
            gt = pairs(256, n)
            do(nc.vector.memset(m.gate, 0.0))
            do(nc.vector.tensor_tensor(gt, one1, w[:, 530:532].unsqueeze(2).to_broadcast([P, NT, n]), ALU.mult))
            g2 = w[:, 600:600 + NT * n].rearrange("p (t c) -> p t c", t=NT)
            do(nc.vector.tensor_tensor(g2, one2, w[:, 532:534].unsqueeze(2).to_broadcast([P, NT, n]), ALU.mult))
            do(nc.vector.tensor_tensor(gt, gt, g2, ALU.add))
            for p in range(m.passes):
                do(nc.vector.tensor_copy(m.gate[:, :, m.per + p * n:m.per + (p + 1) * n], gt))
            do(nc.vector.tensor_tensor(one1, one1, one2, ALU.add))
            v.name("chosen")
            do(nc.vector.memset(m.slot, -1.0))
            dve.wait_ge(*e.at("counted"))
            for t in range(NT):
                do(nc.vector.scalar_tensor_tensor(w[:, 600 + t * n:600 + (t + 1) * n],
                                                  bank(7)[:, 64 * t:64 * t + n], 1.0, one1[:, t, :],
                                                  ALU.add, ALU.mult))
            for p in range(m.passes):
                do(nc.vector.tensor_scalar(m.slot[:, :, m.per + p * n:m.per + (p + 1) * n], g2,
                                           -1.0 - p * m.slots, None, ALU.add))
            do(nc.vector.reduce_max(w[:, 534:535], bank(7)[:, 128:128 + n], AX_X))
            for p in range(1, m.passes):
                do(nc.vector.tensor_scalar(w[:, 535 + p:536 + p], w[:, 534:535], float(p * m.slots), None, ALU.is_gt))
            do(nc.vector.reduce_sum(w[:, 540:541], w[:, 536:535 + m.passes], AX_X))
            nc.vector.tensor_scalar(m.cell, w[0:1, 540:541], 1.0, float(m.iters), ALU.add, ALU.mult)\
                .then_inc(*v.step())
            v.name("trips")
            dve.wait_ge(*v.last())

        def moe_tensor(pe, m):
            sem_, U, per, C = m.sem, m.units, m.per, m.slots
            e, s, v = E[m.st], S[m.st], V[m.st]

            def gather(i):
                pe.wait_ge(sem_["pick_ready"], i + 1 + 1)
                for r in range(2):
                    for k in range(4 * r, 4 * r + 4):
                        for t in range(NT):
                            mm = nc.tensor.matmul(bank(7 - r)[:, (k % 4) * P:(k % 4 + 1) * P],
                                                  r_hrow[:, t * D + k * P:t * D + (k + 1) * P],
                                                  x_pick[:, t * P:(t + 1) * P], start=(t == 0), stop=(t == NT - 1))
                    mm.then_inc(sem_["gathered"], 1)

            def landed_at(i, what, u, x):
                if m.part == "moe1":
                    sl = "gud".index(what) * 2 + x
                    return ring[:, sl, :], landed["moe1"][sl], 16 * (i + 1)
                n = MOE2_ORDER.index((what, u))
                return ring[:, n % SLOTS, :], landed["moe2"][n % SLOTS], i * (16 * TURNS2) + 16 * (1 + n // SLOTS)

            def gate_or_up(i, what, u, bank_):
                w = []
                for x in range(per):
                    tile, sem0, value = landed_at(i, what, u, x)
                    pe.wait_ge(sem0, value)
                    w.append(tile.rearrange("p (k n) -> p k n", n=512))
                for k in range(KC):
                    for x in range(per):
                        mm = nc.tensor.matmul(bank(bank_)[x * C:(x + 1) * C, :],
                                              x_Xg[:, k * P + x * C:k * P + (x + 1) * C], w[x][:, k, :],
                                              start=(k == 0), stop=(k == KC - 1))
                mm.then_inc(sem_["gate_done" if what == "g" else "up_done"], 1)

            def gate_up(i, u):
                gb, ub = m.banks(u)
                if u == 0:
                    pe.wait_ge(sem_["gathered_kept"], i * 2 + 2 + 1)
                if u == 1:
                    pe.wait_ge(sem_["spread_added"], i * 4 + 4 + 1)
                else:
                    pe.wait_ge(sem_["silu_done"], i * U + max(u - 1, 0) + 1)
                gate_or_up(i, "g", u, gb)
                if u != 1:
                    pe.wait_ge(sem_["hidden_done"], i * U + max(u - 1, 0) + 1)
                gate_or_up(i, "u", u, ub)

            def spread_back(i):
                pe.wait_ge(sem_["share_ready"], i + 1 + 1)
                pe.wait_ge(sem_["spread_added"], i * 4 + 1)
                for t in range(NT):
                    mm = nc.tensor.transpose(bank(4)[:, t * P:(t + 1) * P], x_share[:, t * P:(t + 1) * P], eye)
                mm.then_inc(sem_["shareT_done"], 1)
                pe.wait_ge(sem_["y_kept"], i + 1)
                pe.wait_ge(sem_["shareT_kept"], i + 1 + 1)
                for r in range(4):
                    if r >= 2:
                        pe.wait_ge(sem_["spread_added"], i * 4 + r - 1 + 1)
                    for j in range(2):
                        k = 2 * r + j
                        mm = nc.tensor.matmul(bank(5 - r % 2)[:, j * T:(j + 1) * T], x_y[:, k * P:(k + 1) * P],
                                              x_shareT, start=True, stop=True)
                    mm.then_inc(sem_["spread_done"], 1)

            def down(i, u):
                pe.wait_ge(sem_["hidden_done"], i * U + u + 1 + 1)
                if u == U - 1:
                    pe.wait_ge(sem_["gathered_kept"], i * 2 + 4 + 1)
                else:
                    pe.wait_ge(sem_["hiddenT_kept"], i * U + u + 1)
                for f in range(4):
                    mm = nc.tensor.transpose(bank(6)[:, f * P:(f + 1) * P], x_hid[:, f * P:(f + 1) * P], eye)
                mm.then_inc(sem_["hiddenT_done"], 1)
                w = []
                for x in range(per):
                    tile, sem0, value = landed_at(i, "d", u, x)
                    pe.wait_ge(sem0, value)
                    w.append(tile.rearrange("p (f n) -> p f n", n=D))
                if u == 0:
                    pe.wait_ge(sem_["y_kept"], i + 1)
                pe.wait_ge(sem_["hiddenT_kept"], i * U + u + 1 + 1)
                for f in range(4):
                    for half in range(2):
                        for x in range(per):
                            mm = nc.tensor.matmul(bank(2 + half)[x * C:(x + 1) * C, :],
                                                  x_hidT[:, f * P + x * C:f * P + (x + 1) * C],
                                                  w[x][:, f, half * 512:(half + 1) * 512],
                                                  start=(u == 0 and f == 0), stop=(u == U - 1 and f == 3))
                mm.then_inc(sem_["down_done"], 1)

            for w in ("gate_done", "up_done", "shareT_done", "spread_done", "gathered", "hiddenT_done", "down_done"):
                pe.sem_inc(sem_[w], 1)
            pe.wait_ge(*v.at("trips"))
            n = m.trip_count(pe)
            pe.wait_ge(*s.at("hrow"))
            pe.wait_ge(sem_["start"], 1)
            gather(0)
            with pe.Fori(0, n) as i:
                gate_up(i, 0)
                spread_back(i)
                for u in range(1, U):
                    gate_up(i, u)
                    if u < U - 1:
                        down(i, u - 1)
                if U > 1:
                    down(i, U - 2)
                if U > 1:
                    pe.wait_ge(sem_["hiddenT_kept"], i * U + U - 1 + 1)
                else:
                    pe.wait_ge(sem_["hiddenT_kept"], i + 1)
                gather(i + 1)
                down(i, U - 1)
            spread_back(n)
            return n

        def moe_scalar(act, m):
            sem_, U, per, C = m.sem, m.units, m.per, m.slots
            v = V[m.st]

            def silu(i, u):
                act.wait_ge(sem_["gate_done"], i * U + u + 1 + 1)
                act.wait_ge(sem_["hidden_done"], i * U + u + 1)
                nc.scalar.activation(x_silu, bank(m.banks(u)[0]), ACT.Silu).then_inc(sem_["silu_done"], 1)

            def keep_share(i):
                act.wait_ge(sem_["shareT_done"], i + 1 + 1)
                act.wait_ge(sem_["spread_done"], i * 4 + 1)
                nc.scalar.activation(x_shareT, bank(4)[:, 0:T], ACT.Copy).then_inc(sem_["shareT_kept"], 1)

            def keep_gathered(i):
                for r in range(2):
                    act.wait_ge(sem_["gathered"], i * 2 + 1 + r + 1)
                    nc.scalar.activation(x_Xg[:, r * 512:(r + 1) * 512], bank(7 - r), ACT.Copy)\
                        .then_inc(sem_["gathered_kept"], 1)

            def keep_hidden(i, u):
                act.wait_ge(sem_["hiddenT_done"], i * U + u + 1 + 1)
                if u == 0:
                    act.wait_ge(sem_["down_done"], i * U + 1)
                else:
                    act.wait_ge(sem_["down_done"], i * U + u + 1)
                nc.scalar.activation(x_hidT, bank(6), ACT.Copy).then_inc(sem_["hiddenT_kept"], 1)

            for w in ("silu_done", "shareT_kept", "gathered_kept", "hiddenT_kept", "y_kept"):
                act.sem_inc(sem_[w], 1)
            act.wait_ge(*v.at("trips"))
            n = m.trip_count(act)
            keep_gathered(0)
            with act.Fori(0, n) as i:
                silu(i, 0)
                keep_share(i)
                for u in range(1, U):
                    silu(i, u)
                    if u < U - 1:
                        keep_hidden(i, u - 1)
                if U > 1:
                    keep_hidden(i, U - 2)
                keep_gathered(i + 1)
                keep_hidden(i, U - 1)
                act.wait_ge(sem_["down_done"], i * U + U + 1)
                act.wait_ge(sem_["spread_done"], i * 4 + 4 + 1)
                nc.scalar.activation(x_y, bank(2, 2), ACT.Copy).then_inc(sem_["y_kept"], 1)
            keep_share(n)
            return n

        def moe_vector(dve, m):
            sem_, U, per, C = m.sem, m.units, m.per, m.slots

            def pick(i):
                for t in range(NT):
                    for x in range(per):
                        ins = nc.vector.tensor_scalar(x_pick[:, t * P + x * C:t * P + (x + 1) * C],
                                                      consts[:, C_IOTA:C_IOTA + C],
                                                      m.slot[:, t, bass.ds(i * per + (per + x), 1)], None, ALU.is_equal)
                ins.then_inc(sem_["pick_ready"], 1)

            def share(i):
                for t in range(NT):
                    for x in range(per):
                        col = bass.ds(i * per + x, 1)
                        ins = nc.vector.tensor_scalar(x_share[:, t * P + x * C:t * P + (x + 1) * C],
                                                      consts[:, C_IOTA:C_IOTA + C], m.slot[:, t, col],
                                                      m.gate[:, t, col], ALU.is_equal, ALU.mult)
                ins.then_inc(sem_["share_ready"], 1)

            def hidden(i, u):
                dve.wait_ge(sem_["silu_done"], i * U + u + 1 + 1)
                dve.wait_ge(sem_["up_done"], i * U + u + 1 + 1)
                dve.wait_ge(sem_["hiddenT_done"], i * U + u + 1)
                nc.vector.tensor_tensor(x_hid, x_silu, bank(m.banks(u)[1]), ALU.mult).then_inc(sem_["hidden_done"], 1)

            def add_spread(i):
                for r in range(4):
                    dve.wait_ge(sem_["spread_done"], i * 4 + r + 1 + 1)
                    x = xT[:, 2 * r:2 * r + 2, :]
                    nc.vector.tensor_tensor(x, x, bank(5 - r % 2).rearrange("p (b t) -> p b t", t=T), ALU.add)\
                        .then_inc(sem_["spread_added"], 1)

            for w in ("pick_ready", "share_ready", "hidden_done", "spread_added"):
                dve.sem_inc(sem_[w], 1)
            nc.vector.memset(x_y, 0.0).then_inc(sem_["start"], 1)
            pick(0)
            n = m.trip_count(dve)
            with dve.Fori(0, n) as i:
                dve.wait_ge(sem_["shareT_done"], i + 1)
                share(i)
                dve.wait_ge(sem_["gathered"], i * 2 + 2 + 1)
                pick(i + 1)
                hidden(i, 0)
                dve.wait_ge(sem_["hidden_done"], i * U + 1 + 1)
                add_spread(i)
                for u in range(1, U):
                    hidden(i, u)
            dve.wait_ge(sem_["shareT_done"], n + 1)
            share(n)
            dve.wait_ge(sem_["spread_added"], n * 4 + 1)
            add_spread(n)
            return n

        HALVES = 2 * NP2
        z_XgH, z_XgL = carve_r(o_Xg, 1024), carve_r(0, 1024)
        z_hidH, z_hidL = carve_r(o_hidT, 512), carve_r(1024, 512)
        hi_at = r_base + 1024
        HI_BUFS = 5

        def hi_buffer(j):
            b = j % HI_BUFS if j < 2 * HI_BUFS else (j - 2 * HI_BUFS) % (HI_BUFS - 1)
            return b, carve_r(hi_at + b * HALF, HALF)

        def moe2_landed(i, m):
            return landed["moe2"][m % SLOTS], i * (16 * TURNS2) + 16 * (1 + m // SLOTS)

        def moe2_products_done(i, m):
            what, u = MOE2_ORDER[m]
            return moe_sems["moe2"][{"g": "gate_done", "u": "up_done", "d": "down_done"}[what]], i * UNITS + u + 2

        def moe2_tensor(pe):
            m = M2
            sem_, U = m.sem, UNITS
            e, s, v = E[m.st], S[m.st], V[m.st]

            def gather(i):
                pe.wait_ge(sem_["pick_ready"], i + 1 + 1)
                for r in range(2):
                    for k in range(4 * r, 4 * r + 4):
                        for t in range(NT):
                            mm = nc.tensor.matmul(bank(7 - 2 * r)[:, (k % 4) * P:(k % 4 + 1) * P],
                                                  r_hrow[:, t * D + k * P:t * D + (k + 1) * P],
                                                  x_pick[:, t * P:(t + 1) * P], start=(t == 0), stop=(t == NT - 1))
                    mm.then_inc(sem_["gathered"], 1)

            def gate_or_up(i, what, u):
                m_ = MOE2_ORDER.index((what, u))
                out = bank(m.banks(u)["gu".index(what)])
                for half in range(2):
                    j = 2 * m_ + half
                    pe.wait_ge(weights_lo, i * HALVES + j + 1)
                    hi = hi_buffer(j)[1].rearrange("p (k n) -> p k n", n=512)
                    lo = ring_r[m_ % SLOTS][:, half * HALF:(half + 1) * HALF].rearrange("p (k n) -> p k n", n=512)
                    for q in range(4):
                        k = 4 * half + q
                        x = slice(k * P, (k + 1) * P)
                        mm = three(out, (z_XgH[:, x], z_XgL[:, x]), (hi[:, q, :], lo[:, q, :]), k == 0, k == KC - 1)
                mm.then_inc(sem_["gate_done" if what == "g" else "up_done"], 1)

            def share_transposed(i):
                pe.wait_ge(sem_["share_ready"], i + 1 + 1)
                pe.wait_ge(sem_["spread_added"], i * 4 + 1)
                for t in range(NT):
                    mm = nc.tensor.transpose(bank(4)[:, t * P:(t + 1) * P], x_share[:, t * P:(t + 1) * P], eye)
                mm.then_inc(sem_["shareT_done"], 1)

            def spread_back(i):
                pe.wait_ge(sem_["y_kept"], i + 1)
                pe.wait_ge(sem_["shareT_kept"], i + 1 + 1)
                for r in range(4):
                    if r >= 2:
                        pe.wait_ge(sem_["spread_added"], i * 4 + r - 1 + 1)
                    for j in range(2):
                        k = 2 * r + j
                        mm = nc.tensor.matmul(bank(5 - r % 2)[:, j * T:(j + 1) * T], x_y[:, k * P:(k + 1) * P],
                                              x_shareT, start=True, stop=True)
                    mm.then_inc(sem_["spread_done"], 1)

            def hidden_transposed(i, u):
                pe.wait_ge(sem_["hidden_done"], i * U + u + 1 + 1)
                pe.wait_ge(hiddenT_lo, i * U + u + 1)
                for f in range(4):
                    mm = nc.tensor.transpose(bank(6)[:, f * P:(f + 1) * P], x_hid[:, f * P:(f + 1) * P], eye)
                mm.then_inc(sem_["hiddenT_done"], 1)

            def down(i, u):
                m_ = MOE2_ORDER.index(("d", u))
                if u == 0:
                    pe.wait_ge(sem_["y_kept"], i + 1)
                pe.wait_ge(hiddenT_lo, i * U + u + 1 + 1)
                for half in range(2):
                    j = 2 * m_ + half
                    pe.wait_ge(weights_lo, i * HALVES + j + 1)
                    hi = hi_buffer(j)[1].rearrange("p (f n) -> p f n", n=D)
                    lo = ring_r[m_ % SLOTS][:, half * HALF:(half + 1) * HALF].rearrange("p (f n) -> p f n", n=D)
                    for q in range(2):
                        f = 2 * half + q
                        x = slice(f * P, (f + 1) * P)
                        for c in range(2):
                            n = slice(c * 512, (c + 1) * 512)
                            mm = three(bank(2 + c), (z_hidH[:, x], z_hidL[:, x]), (hi[:, q, n], lo[:, q, n]),
                                       u == 0 and f == 0, u == U - 1 and f == 3)
                mm.then_inc(sem_["down_done"], 1)

            for w in ("gate_done", "up_done", "shareT_done", "spread_done", "gathered", "hiddenT_done", "down_done"):
                pe.sem_inc(sem_[w], 1)
            pe.wait_ge(*v.at("trips"))
            n = m.trip_count(pe)
            pe.wait_ge(*s.at("hrow"))
            pe.wait_ge(sem_["start"], 1)
            gather(0)
            with pe.Fori(0, n) as i:
                pe.wait_ge(gathered_lo, i * 2 + 2 + 1)
                pe.wait_ge(sem_["silu_done"], i * U + 1)
                gate_or_up(i, "g", 0)
                share_transposed(i)
                pe.wait_ge(sem_["hidden_done"], i * U + 1)
                gate_or_up(i, "u", 0)
                spread_back(i)
                for u in range(1, U):
                    if u == 1:
                        pe.wait_ge(sem_["spread_added"], i * 4 + 4 + 1)
                    else:
                        pe.wait_ge(sem_["silu_done"], i * U + u - 1 + 1)
                    gate_or_up(i, "g", u)
                    hidden_transposed(i, u - 1)
                    if u > 1:
                        pe.wait_ge(sem_["hidden_done"], i * U + u - 1 + 1)
                    gate_or_up(i, "u", u)
                    down(i, u - 1)
                hidden_transposed(i, U - 1)
                gather(i + 1)
                down(i, U - 1)
            share_transposed(n)
            spread_back(n)

        def moe2_steps(i, split, at_step):
            for p in range(NP2):
                nxt = (i, p + 1) if p + 1 < NP2 else (i + 1, 0)
                before_, between, after_ = at_step.get(p, ([], [], []))
                for f in before_:
                    f()
                split(*nxt, 0)
                for f in between:
                    f()
                split(*nxt, 1)
                for f in after_:
                    f()

        def moe2_scalar(act):
            m = M2
            sem_, U = m.sem, UNITS
            v = V[m.st]

            def split(i, m_, half, first=False):
                j = 2 * m_ + half
                if half == 0:
                    act.wait_ge(*moe2_landed(i, m_))
                if not first:
                    users = [q for q in range(HALVES) if hi_buffer(q)[0] == hi_buffer(j)[0]]
                    at = users.index(j)
                    if at > 0:
                        act.wait_ge(*moe2_products_done(i, users[at - 1] // 2))
                    elif users[-1] >= HALVES - 4:
                        act.wait_ge(*moe2_products_done(i - 1, users[-1] // 2))
                nc.scalar.activation(hi_buffer(j)[1], ring[:, m_ % SLOTS, half * HALF:(half + 1) * HALF],
                                     ACT.Copy).then_inc(weights_hi, 1)

            def silu(i, u):
                act.wait_ge(sem_["gate_done"], i * U + u + 1 + 1)
                act.wait_ge(sem_["hidden_done"], i * U + u + 1)
                nc.scalar.activation(x_silu, bank(m.banks(u)[0]), ACT.Silu).then_inc(sem_["silu_done"], 1)

            def keep_share(i):
                act.wait_ge(sem_["shareT_done"], i + 1 + 1)
                act.wait_ge(sem_["spread_done"], i * 4 + 1)
                nc.scalar.activation(x_shareT, bank(4)[:, 0:T], ACT.Copy).then_inc(sem_["shareT_kept"], 1)

            def keep_gathered(i, r):
                act.wait_ge(sem_["gathered"], i * 2 + 1 + r + 1)
                nc.scalar.activation(z_XgH[:, r * 512:(r + 1) * 512], bank(7 - 2 * r), ACT.Copy)\
                    .then_inc(sem_["gathered_kept"], 1)

            def keep_hidden(i, u):
                act.wait_ge(sem_["hiddenT_done"], i * U + u + 1 + 1)
                act.wait_ge(sem_["down_done"], i * U + u + 1)
                nc.scalar.activation(z_hidH, bank(6), ACT.Copy).then_inc(sem_["hiddenT_kept"], 1)

            def keep_y(i):
                act.wait_ge(sem_["down_done"], i * U + U + 1)
                act.wait_ge(sem_["spread_done"], i * 4 + 4 + 1)
                nc.scalar.activation(x_y, bank(2, 2), ACT.Copy).then_inc(sem_["y_kept"], 1)

            for w in ("silu_done", "shareT_kept", "gathered_kept", "hiddenT_kept", "y_kept"):
                act.sem_inc(sem_[w], 1)
            for half in range(2):
                split(0, 0, half, first=True)
            act.wait_ge(*v.at("trips"))
            n = m.trip_count(act)
            for r in range(2):
                keep_gathered(0, r)
            with act.Fori(0, n) as i:
                work = {1: ([], [lambda: keep_share(i), lambda: silu(i, 0)], [])}
                for u in range(1, U):
                    work[3 * u] = ([], [lambda u=u: keep_hidden(i, u - 1), lambda u=u: silu(i, u)], [])
                work[NP2 - 1] = ([lambda: keep_hidden(i, U - 1)],
                                 [lambda: keep_gathered(i + 1, 0), lambda: keep_gathered(i + 1, 1)],
                                 [lambda: keep_y(i)])
                moe2_steps(i, split, work)
            keep_share(n)
            return n

        def moe2_vector(dve):
            m = M2
            sem_, U = m.sem, UNITS

            def split(i, m_, half):
                j = 2 * m_ + half
                dve.wait_ge(weights_hi, i * HALVES + j + 1)
                at = slice(half * HALF, (half + 1) * HALF)
                nc.vector.tensor_tensor(ring_r[m_ % SLOTS][:, at], ring[:, m_ % SLOTS, at],
                                        hi_buffer(j)[1].bitcast(F32), ALU.subtract).then_inc(weights_lo, 1)

            def pick(i):
                for t in range(NT):
                    ins = nc.vector.tensor_scalar(x_pick[:, t * P:(t + 1) * P], consts[:, C_IOTA:C_IOTA + P],
                                                  m.slot[:, t, bass.ds(i + 1, 1)], None, ALU.is_equal)
                ins.then_inc(sem_["pick_ready"], 1)

            def share(i):
                dve.wait_ge(sem_["shareT_done"], i + 1)
                for t in range(NT):
                    ins = nc.vector.tensor_scalar(x_share[:, t * P:(t + 1) * P], consts[:, C_IOTA:C_IOTA + P],
                                                  m.slot[:, t, bass.ds(i, 1)], m.gate[:, t, bass.ds(i, 1)],
                                                  ALU.is_equal, ALU.mult)
                ins.then_inc(sem_["share_ready"], 1)

            def hidden(i, u):
                dve.wait_ge(sem_["silu_done"], i * U + u + 1 + 1)
                dve.wait_ge(sem_["up_done"], i * U + u + 1 + 1)
                dve.wait_ge(sem_["hiddenT_done"], i * U + u + 1)
                nc.vector.tensor_tensor(x_hid, x_silu, bank(m.banks(u)[1]), ALU.mult).then_inc(sem_["hidden_done"], 1)

            def rest_of_hidden(i, u):
                dve.wait_ge(sem_["hiddenT_kept"], i * U + u + 1 + 1)
                nc.vector.tensor_tensor(z_hidL, bank(6), z_hidH.bitcast(F32), ALU.subtract).then_inc(hiddenT_lo, 1)

            def rest_of_gathered(i, r):
                dve.wait_ge(sem_["gathered_kept"], i * 2 + r + 1 + 1)
                x = slice(r * 512, (r + 1) * 512)
                nc.vector.tensor_tensor(z_XgL[:, x], bank(7 - 2 * r), z_XgH[:, x].bitcast(F32), ALU.subtract)\
                    .then_inc(gathered_lo, 1)

            def add_spread(i):
                for r in range(4):
                    dve.wait_ge(sem_["spread_done"], i * 4 + r + 1 + 1)
                    x = xT[:, 2 * r:2 * r + 2, :]
                    nc.vector.tensor_tensor(x, x, bank(5 - r % 2).rearrange("p (b t) -> p b t", t=T), ALU.add)\
                        .then_inc(sem_["spread_added"], 1)

            def next_pick(i):
                dve.wait_ge(sem_["gathered"], i * 2 + 2 + 1)
                pick(i + 1)

            for w in ("pick_ready", "share_ready", "hidden_done", "spread_added"):
                dve.sem_inc(sem_[w], 1)
            dve.sem_inc(gathered_lo, 1)
            dve.sem_inc(hiddenT_lo, 1)
            nc.vector.memset(x_y, 0.0).then_inc(sem_["start"], 1)
            pick(0)
            for half in range(2):
                split(0, 0, half)
            n = m.trip_count(dve)
            for r in range(2):
                rest_of_gathered(0, r)
            with dve.Fori(0, n) as i:
                work = {0: ([lambda: share(i)], [], []),
                        1: ([], [lambda: next_pick(i)], []),
                        2: ([lambda: add_spread(i), lambda: hidden(i, 0)], [], [])}
                for u in range(1, U):
                    work[3 * u] = ([], [lambda u=u: rest_of_hidden(i, u - 1)], [])
                    work[3 * u + 1] = ([], [lambda u=u: hidden(i, u)], [])
                work[NP2 - 1] = ([lambda: rest_of_hidden(i, U - 1)],
                                 [lambda: rest_of_gathered(i + 1, 0), lambda: rest_of_gathered(i + 1, 1)], [])
                moe2_steps(i, split, work)
            share(n)
            dve.wait_ge(sem_["spread_added"], n * 4 + 1)
            add_spread(n)

        c_w = [carve(0, HC), carve(HC, HC)]
        c_qt, c_kt, c_AT = (carve(HC * n, HC) for n in (2, 3, 4))
        c_kd = [carve(HC * 5, HC), carve(HC * 6, HC)]
        c_S = [carve(HC * 7, 512), carve(HC * 7 + 512, 512)]
        y_cat = carve(HC * 8, KC * T)
        c_small = carve(HC * 20, 128)
        c_decay = c_small[:, 0:16]
        c_retk = c_small[:, 16:24]
        c_lb, c_omlb = c_small[:, 24:32], c_small[:, 32:40]
        NL = len(LEVELS)

        class Gated:
            def __init__(self, st, tag, nb, q, k, g, v, gate, y, gain):
                self.st, self.tag, self.nb = st, tag, nb
                self.q, self.k, self.g, self.v, self.gate, self.y, self.gain = q, k, g, v, gate, y, gain
                self.N = nb * T
                self.w = [w[:, 0:self.N] for w in c_w]
                self.kt = c_kt[:, 0:self.N]
                self.padded = nb == 2

        def parity(ap, par):
            return ap.rearrange("p (b r t) -> p b r t", r=2, t=T)[:, :, par, :]

        def scores(pe, x, name, k, q, b0):
            for h in range(H4):
                for t in range(NT):
                    kb = k[:, (h if x.nb == 4 else h // 2) * T + t * P:(h if x.nb == 4 else h // 2) * T + t * P + P]
                    mm = nc.tensor.matmul(inst(bank(b0, 2), h, t), kb, inst(q, h, t), start=True, stop=True)
            mm.then_inc(*E[x.st].step())
            E[x.st].name(x.tag + name)

        def gated_tensor_round(pe, x, n):
            v, tag = V[x.st], x.tag
            b0 = 4 + 2 * (n % 2)
            if n == 0:
                pe.wait_ge(*v.at(tag + "ready"))
                scores(pe, x, "r0", x.k, c_qt if x.padded else x.q, b0)
            else:
                pe.wait_ge(*v.at(f"{tag}q{n}"))
                pe.wait_ge(*G[x.st].at(f"{tag}k{n}"))
                if n >= 2:
                    pe.wait_ge(*v.at(f"{tag}taken{n - 2}"))
                scores(pe, x, f"r{n}", x.kt, c_qt, b0)

        def gated_scalar_round(act, x, n):
            s, v = S[x.st], V[x.st]
            w = x.w[n % 2]
            act.wait_ge(*v.at(f"{x.tag}d{n}"))
            nc.scalar.activation(w, w, ACT.Abs).then_inc(*s.step())
            act.wait_ge(*s.last())
            nc.scalar.activation(w, w, ACT.Exp, scale=-1.0).then_inc(*s.step())
            s.name(f"{x.tag}w{n}")

        def gated_pool_round(pool, x, n):
            pool.wait_ge(*S[x.st].at(f"{x.tag}w{n}"))
            if n >= 2:
                pool.wait_ge(*E[x.st].at(f"{x.tag}r{n - 1}"))
            nc.gpsimd.tensor_tensor(x.kt, x.k, x.w[n % 2], ALU.mult).then_inc(*G[x.st].step())
            G[x.st].name(f"{x.tag}k{n}")

        def gated_difference(dve, x, n):
            v = V[x.st]
            size = LEVELS[n - 1]
            g = x.g.rearrange("p (b i) -> p b i", i=2 * size)
            if n >= 3:
                dve.wait_ge(*G[x.st].at(f"{x.tag}k{n - 2}"))
            nc.vector.tensor_tensor(x.w[n % 2].rearrange("p (b i) -> p b i", i=2 * size), g,
                                    g[:, :, size - 1:size].to_broadcast([P, x.N // (2 * size), 2 * size]),
                                    ALU.subtract).then_inc(*v.step())
            v.name(f"{x.tag}d{n}")

        def scaled_queries(dve, x, w, scale=1.0):
            v = V[x.st]
            if x.padded:
                for par in range(2):
                    ins = nc.vector.scalar_tensor_tensor(
                        parity(c_qt, par), x.q.rearrange("p (b t) -> p b t", t=T),
                        consts[:, C_HALF + par:C_HALF + par + 1], w.rearrange("p (b t) -> p b t", t=T),
                        ALU.mult, ALU.mult).then_inc(*v.step())
            else:
                nc.vector.tensor_tensor(c_qt, x.q, w, ALU.mult).then_inc(*v.step())

        def gated_vector_round(dve, x, n):
            e, s, v = E[x.st], S[x.st], V[x.st]
            tag = x.tag
            if n < NL:
                if n >= 1:
                    dve.wait_ge(*v.last())
                gated_difference(dve, x, n + 1)
            if n >= 1:
                dve.wait_ge(*s.at(f"{tag}w{n}"))
                if n >= 2 or x.padded:
                    dve.wait_ge(*e.at(f"{tag}r{n - 1}"))
                scaled_queries(dve, x, x.w[n % 2])
                v.name(f"{tag}q{n}")
                take_scores(dve, x, n - 1)

        def take_scores(dve, x, n):
            e, v = E[x.st], V[x.st]
            b0 = 4 + 2 * (n % 2)
            dve.wait_ge(*e.at(f"{x.tag}r{n}"))
            if n == 0:
                nc.vector.tensor_tensor(blocks(c_AT), blocks(bank(b0, 2)), spread(eye), ALU.mult).then_inc(*v.step())
            else:
                mask = level_mask(n - 1).bitcast(I32).unsqueeze(1).to_broadcast([P, 8, P])
                nc.vector.copy_predicated(blocks(c_AT), mask, blocks(bank(b0, 2))).then_inc(*v.step())
            v.name(f"{x.tag}taken{n}")
            dve.wait_ge(*v.last())

        def gated_vector_end(dve, x):
            e, s, v = E[x.st], S[x.st], V[x.st]
            tag = x.tag
            take_scores(dve, x, NL)
            dve.wait_ge(*G[x.st].at(f"{tag}k{NL}"))
            chunks = x.g.rearrange("p (b i) -> p b i", i=CH)
            nc.vector.tensor_tensor(x.w[0].rearrange("p (b i) -> p b i", i=CH), chunks,
                                    chunks[:, :, CH - 1:CH].to_broadcast([P, x.N // CH, CH]),
                                    ALU.subtract).then_inc(*v.step())
            v.name(tag + "last")
            dve.wait_ge(*s.at(tag + "eg"))
            scaled_queries(dve, x, x.w[1])
            v.name(tag + "qd")
            nc.vector.tensor_copy(c_decay[:, 0:4 * x.nb], x.w[1][:, CH - 1::CH]).then_inc(*v.step())
            dve.wait_ge(*v.last())

        def gated_scalar_end(act, x):
            s, v = S[x.st], V[x.st]
            tag = x.tag
            act.wait_ge(*v.at(tag + "last"))
            nc.scalar.activation(x.w[1], x.g, ACT.Exp).then_inc(*s.step())
            s.name(tag + "eg")
            nc.scalar.activation(x.w[0], x.w[0], ACT.Abs).then_inc(*s.step())
            act.wait_ge(*s.last())
            nc.scalar.activation(x.w[0], x.w[0], ACT.Exp, scale=-1.0).then_inc(*s.step())
            s.name(tag + "el")
            for b in range(x.N // 512):
                act.wait_ge(*E[x.st].at(f"{tag}kr{b}"))
                for half in range(2):
                    nc.scalar.activation(c_kd[half][:, b * 512:(b + 1) * 512], bank(4 + b), ACT.Copy,
                                         scale=consts[:, C_HALF + half:C_HALF + half + 1]).then_inc(*s.step())
            s.name(tag + "kd")

        def gated_pool_end(pool, x):
            pool.wait_ge(*S[x.st].at(x.tag + "el"))
            nc.gpsimd.tensor_tensor(x.kt, x.k, x.w[0], ALU.mult).then_inc(*G[x.st].step())
            G[x.st].name(x.tag + "kl")

        def gated_tensor_end(pe, x, out=None):
            e, v = E[x.st], V[x.st]
            pe.wait_ge(*G[x.st].at(x.tag + "kl"))
            pe.wait_ge(*v.at(f"{x.tag}taken{NL}"))
            k_rows(pe, x, x.kt)
            attend_tensor(pe, x, out)

        def k_rows(pe, x, k):
            e = E[x.st]
            for b in range(x.N // 512):
                for j in range(4):
                    mm = nc.tensor.transpose(bank(4 + b)[:, j * P:(j + 1) * P],
                                             k[:, b * 512 + j * P:b * 512 + (j + 1) * P], eye)
                mm.then_inc(*e.step())
                e.name(f"{x.tag}kr{b}")

        def attend_tensor(pe, x, out=None):
            e, s, v, tag = E[x.st], S[x.st], V[x.st], x.tag
            pe.wait_ge(*s.at(tag + "kd"))
            pe.wait_ge(*s.at(tag + "v"))
            pe.wait_ge(*v.at(tag + "qd"))

            def value(h, t):
                return x.v[:, t * 512 + h * P:t * 512 + (h + 1) * P]

            def add_to_state(c):
                t = c // 2
                if c >= 2:
                    pe.wait_ge(*v.at(f"{tag}S{c - 2}"))
                for h in range(H4):
                    kd = inst(c_kd[c % 2], h if x.nb == 4 else h // 2, t)
                    mm = nc.tensor.matmul(bank(4 + c % 2)[:, h * P:(h + 1) * P], kd, value(h, t),
                                          start=True, stop=True)
                mm.then_inc(*e.step())
                e.name(f"{tag}Sp{c}")

            add_to_state(0)
            for c in range(NCH):
                t, off = c // 2, (c % 2) * CH
                if c < NCH - 2:
                    add_to_state(c + 1)
                if out:
                    out.fill(1)
                if c:
                    pe.wait_ge(*v.at(f"{tag}S{c - 1}"))
                for h in range(H4):
                    o = bank(6, 2)[:, h * T + c * CH:h * T + (c + 1) * CH]
                    if c:
                        nc.tensor.matmul(o, c_S[(c - 1) % 2][:, h * P:(h + 1) * P],
                                         c_qt[:, h * T + c * CH:h * T + (c + 1) * CH], start=True, stop=False)
                    mm = nc.tensor.matmul(o, value(h, t), inst(c_AT, h, t)[:, off:off + CH],
                                          start=(c == 0), stop=True)
                mm.then_inc(*e.step())
                e.name(f"{tag}o{c}")
            if out:
                out.fill(2)
            pe.wait_ge(*s.at(tag + "osq"))
            for half in range(2):
                mm = nc.tensor.matmul(bank(4 + half), ones[:, :], c_w[0][:, half * 512:(half + 1) * 512],
                                      start=True, stop=True)
            mm.then_inc(*e.step())
            e.name(tag + "osum")

        def attend_vector(dve, x, decay):
            e, s, v, tag = E[x.st], S[x.st], V[x.st], x.tag
            for c in range(NCH - 1):
                dve.wait_ge(*e.at(f"{tag}Sp{c}"))
                if c > 1:
                    dve.wait_ge(*e.at(f"{tag}o{c - 1}"))
                for h in range(H4):
                    hs = slice(h * P, (h + 1) * P)
                    if c == 0:
                        nc.vector.tensor_copy(c_S[0][:, hs], bank(4)[:, hs]).then_inc(*v.step())
                    else:
                        nc.vector.scalar_tensor_tensor(c_S[c % 2][:, hs], c_S[(c - 1) % 2][:, hs], decay(h, c),
                                                       bank(4 + c % 2)[:, hs], ALU.mult, ALU.add)\
                            .then_inc(*v.step())
                v.name(f"{tag}S{c}")
                dve.wait_ge(*v.last())
            dve.wait_ge(*s.at(tag + "orstd"))
            nc.vector.scalar_tensor_tensor(x.y, c_AT, x.gain, c_w[1], ALU.mult, ALU.mult).then_inc(*v.step())
            dve.wait_ge(*v.last())
            dve.wait_ge(*s.at(tag + "gate"))
            nc.vector.tensor_tensor(x.y, x.y, x.gate, ALU.mult).then_inc(*v.step())
            v.name(tag + "y")
            dve.wait_ge(*v.last())

        def attend_scalar(act, x):
            e, s, tag = E[x.st], S[x.st], x.tag
            act.wait_ge(*e.at(f"{tag}o{NCH - 1}"))
            nc.scalar.activation(c_AT, bank(6, 2), ACT.Copy).then_inc(*s.step())
            act.wait_ge(*s.last())
            nc.scalar.activation(c_w[0], c_AT, ACT.Square).then_inc(*s.step())
            s.name(tag + "osq")
            act.wait_ge(*e.at(tag + "osum"))
            nc.scalar.activation(c_w[1], bank(4, 2), ACT.Ln, bias=eps_col, scale=1.0 / P).then_inc(*s.step())
            act.wait_ge(*s.last())
            nc.scalar.activation(c_w[1], c_w[1], ACT.Exp, scale=-0.5).then_inc(*s.step())
            s.name(tag + "orstd")

        def keep_banks(act, st, name, names, base, out, func=ACT.Copy, scale=1.0, blocks_=True, waits=()):
            e, s = E[st], S[st]
            b0 = 2 * ((base + names.index(name)) % 2)
            for w in waits:
                act.wait_ge(*w)
            for half in range(2):
                round_next(act, st, "two", names, name, half)
                act.wait_ge(*e.at(f"{name}_{half}"))
                nc.scalar.activation(out(half), bank(b0 + half), func, scale=scale).then_inc(*s.step())
                s.name(f"{name}_{half}")

        def halves(ap):
            return lambda half: ap[:, half * 512:(half + 1) * 512]

        B2 = len(PROJ1)
        a_q, a_k, a_v, a_gate, b_v, b_gate = (carve(tail_at + HC * n, HC) for n in range(6))
        b_q, b_k, b_g = (carve(tail_at + HC * 6 + 512 * n, 512) for n in range(3))
        a_cos, a_sin = (carve(tail_at + HC * 6 + 1536 + T * n, T) for n in range(2))
        a_ang, a_turn = (carve(tail_at + HC * 8 + T * n, T) for n in (1, 2))
        b_low = carve(tail_at + HC * 9, T)
        GLA = Gated("mix2", "b", 2, b_q, b_k, b_g, b_v, b_gate, y_cat[:, HC:2 * HC], param("gla_g"))
        RET = Gated("mix2", "a", 4, a_q, a_k, None, a_v, a_gate, y_cat[:, 0:HC], param("ret_g"))

        def mixer2_tensor(pe):
            st = "mix2"
            e, s, v = E[st], S[st], V[st]
            norm_tensor(pe, st, "f")
            norm_tensor(pe, st, "n")
            pe.wait_ge(*v.at("h"))
            tail = param("tail2", 128).rearrange("p (k n) -> p k n", n=16)
            for k in range(KC):
                mm = nc.tensor.matmul(bank(6)[0:16, 0:T], tail[:, k, :], hT[:, k, :], start=(k == 0), stop=(k == KC - 1))
            mm.then_inc(*e.step())
            e.name("low")

            def proj(name, rows_=False):
                (project_rows if rows_ else project)(
                    pe, st, "two", name, free_by(st, PROJ2, name, lambda n, half: [s.at(f"{n}_{half}")]))

            proj("bqk")
            pe.wait_ge(*s.at("low"))
            for b in range(2):
                mm = nc.tensor.matmul(bank(7)[:, b * T:(b + 1) * T], param("gla_w", 256)[0:16, b * P:(b + 1) * P],
                                      b_low[0:16, :], start=True, stop=True)
            mm.then_inc(*e.step())
            e.name("z")
            proj("aq")
            gated_tensor_round(pe, GLA, 0)
            proj("ak")
            gated_tensor_round(pe, GLA, 1)
            proj("bv", True)
            gated_tensor_round(pe, GLA, 2)
            proj("av", True)
            gated_tensor_round(pe, GLA, 3)
            proj("bg")
            gated_tensor_round(pe, GLA, 4)
            proj("ag")
            gated_tensor_round(pe, GLA, 5)
            gated_tensor_round(pe, GLA, 6)
            gated_tensor_end(pe, GLA)
            pe.wait_ge(*s.at("ag_1"))
            for half in range(2):
                mm = nc.tensor.matmul(bank(half), consts[:, C_ROT:C_ROT + P], a_q[:, half * 512:(half + 1) * 512],
                                      start=True, stop=True)
            mm.then_inc(*e.step())
            e.name("rotq")
            for half in range(2):
                mm = nc.tensor.matmul(bank(2 + half), consts[:, C_ROT:C_ROT + P], a_k[:, half * 512:(half + 1) * 512],
                                      start=True, stop=True)
            mm.then_inc(*e.step())
            e.name("rotk")
            pe.wait_ge(*v.at("rotated"))
            pe.wait_ge(*v.at("by"))
            scores(pe, RET, "r0", a_k, a_q, 6)
            out = OutProjection(pe, st, "two", "out2", y_cat, range(4, 8), [])
            out.fill(2)
            pe.wait_ge(*s.at("borstd"))
            k_rows(pe, RET, a_k)
            pe.wait_ge(*v.at("ataken"))
            attend_tensor(pe, RET, out)
            out.finish(v.at("ay"))

        def mixer2_scalar(act, waits):
            st = "mix2"
            e, s, v = E[st], S[st], V[st]
            act.preload_act_table_set(EXP_LN)
            for w in waits:
                act.wait_ge(*w)
            weights_hi_of(act, st, "two", "bqk", range(4))
            norm_scalar(act, st, "f", [])
            norm_scalar(act, st, "n", [v.at("x")])
            tokens_hi(act, st)
            act.wait_ge(*e.at("low"))
            nc.scalar.activation(b_low[0:16, :], bank(6)[0:16, 0:T], ACT.Copy).then_inc(*s.step())
            s.name("low")

            def keep(name, out, **kw):
                keep_banks(act, st, name, PROJ2, B2, out, **kw)

            for half, (name, out, scale) in enumerate((("bqk_0", b_q, 64 ** -0.5), ("bqk_1", b_k, 1.0))):
                round_next(act, st, "two", PROJ2, "bqk", half)
                act.wait_ge(*e.at(name))
                nc.scalar.activation(out, bank(2 * (B2 % 2) + half), ACT.Copy, scale=scale).then_inc(*s.step())
                s.name(name)
            act.wait_ge(*v.at("z"))
            nc.scalar.activation(c_qt[:, 0:512], c_qt[:, 0:512], ACT.Exp).then_inc(*s.step())
            act.wait_ge(*s.last())
            nc.scalar.activation(c_qt[:, 0:512], c_qt[:, 0:512], ACT.Ln, bias=1.0).then_inc(*s.step())
            s.name("softplus")
            gated_scalar_round(act, GLA, 1)
            keep("aq", halves(a_q))
            gated_scalar_round(act, GLA, 2)
            keep("ak", halves(a_k), scale=float(P) ** -0.5)
            gated_scalar_round(act, GLA, 3)
            keep("bv", halves(b_v))
            s.name("bv")
            gated_scalar_round(act, GLA, 4)
            keep("av", halves(a_v))
            s.name("av")
            gated_scalar_round(act, GLA, 5)
            gated_scalar_round(act, GLA, 6)
            keep("bg", halves(b_gate), func=ACT.Silu)
            s.name("bgate")
            keep("ag", halves(a_gate), func=ACT.Silu)
            s.name("agate")
            act.wait_ge(*v.at("angles"))
            nc.scalar.activation(a_sin, a_ang, ACT.Sin).then_inc(*s.step())
            nc.scalar.activation(a_cos, a_turn, ACT.Sin).then_inc(*s.step())
            s.name("sincos")
            act.preload_act_table_set(EXP_LN)
            gated_scalar_end(act, GLA)
            attend_scalar(act, GLA)
            for b in range(2):
                act.wait_ge(*e.at(f"akr{b}"))
                for half in range(2):
                    for h in (2 * b, 2 * b + 1):
                        nc.scalar.activation(c_kd[half][:, h * T:(h + 1) * T],
                                             bank(4 + b)[:, (h % 2) * T:(h % 2 + 1) * T], ACT.Copy,
                                             scale=c_retk[:, half * 4 + h:half * 4 + h + 1]).then_inc(*s.step())
            s.name("akd")
            attend_scalar(act, RET)

        def mixer2_pool(pool):
            names = PROJ2[:-2]
            for name in names[:3]:
                weights_lo_of(pool, "mix2", "two", name)
            for n in range(1, NL + 1):
                gated_pool_round(pool, GLA, n)
                if n + 2 < len(names):
                    weights_lo_of(pool, "mix2", "two", names[n + 2])
            gated_pool_end(pool, GLA)

        def mixer2_vector(dve):
            st = "mix2"
            e, s, v = E[st], S[st], V[st]
            norm_vector(dve, st, "f", param("final_g", 8), xT, "x")
            dve.wait_ge(*v.last())
            norm_vector(dve, st, "n", param("mix2_g", 8), hT, "h")
            tokens_lo(dve, st)

            def do(ins):
                ins.then_inc(*v.step())
                dve.wait_ge(*v.last())

            dve.wait_ge(loaded_positions, 16)
            do(nc.vector.tensor_copy(a_ang, a_pos))
            do(nc.vector.tensor_scalar(a_ang, a_ang, consts[:, C_FREQ:C_FREQ + 1], None, ALU.mult))
            magic = float(3 << 22)
            do(nc.vector.tensor_scalar(a_turn, a_ang, float(1 / (2 * np.pi)), magic, ALU.mult, ALU.add))
            do(nc.vector.tensor_scalar(a_turn, a_turn, -magic, None, ALU.add))
            for part in (6.28125, 0.0019340515136718750, 2 * np.pi - 6.28125 - 0.0019340515136718750):
                do(nc.vector.scalar_tensor_tensor(a_ang, a_turn, -float(part), a_ang, ALU.mult, ALU.add))
            limit = 3.1415925
            do(nc.vector.tensor_scalar(a_ang, a_ang, limit, -limit, ALU.min, ALU.max))
            do(nc.vector.scalar_tensor_tensor(a_turn, a_ang, -1.0, a_ang, ALU.mult, ALU.min))
            nc.vector.tensor_scalar(a_turn, a_turn, float(np.pi / 2), None, ALU.add).then_inc(*v.step())
            v.name("angles")
            for half in range(2):
                do(nc.vector.tensor_scalar(c_retk[:, half * 4:half * 4 + 4], consts[:, C_RETK:C_RETK + 4],
                                           consts[:, C_HALF + half:C_HALF + half + 1], None, ALU.mult))
            v.name("retk")
            dve.wait_ge(*e.at("z"))
            for b in range(2):
                do(nc.vector.tensor_scalar(b_g[:, b * T:(b + 1) * T], bank(7)[:, b * T:(b + 1) * T],
                                           param("gla_b", 1, b), None, ALU.add))
            nc.vector.scalar_tensor_tensor(c_qt[:, 0:512], b_g, -1.0, b_g, ALU.mult, ALU.min).then_inc(*v.step())
            v.name("z")
            dve.wait_ge(*s.at("softplus"))
            do(nc.vector.scalar_tensor_tensor(b_g, b_g, 0.0, c_qt[:, 0:512], ALU.min, ALU.subtract))
            do(nc.vector.tensor_scalar(b_g, b_g, 1.0 / 16.0, None, ALU.mult))
            cumulate(dve, GLA)
            dve.wait_ge(*v.last())
            dve.wait_ge(*s.at("bqk_1"))
            for par in range(2):
                nc.vector.tensor_scalar(parity(c_qt, par), b_q.rearrange("p (b t) -> p b t", t=T),
                                        consts[:, C_HALF + par:C_HALF + par + 1], None, ALU.mult)\
                    .then_inc(*v.step())
            v.name("bready")
            for n in range(NL + 1):
                gated_vector_round(dve, GLA, n)
            gated_vector_end(dve, GLA)
            attend_vector(dve, GLA, lambda h, c: c_decay[:, (h // 2) * 4 + c:(h // 2) * 4 + c + 1])
            dve.wait_ge(*s.at("sincos"))
            for x, b0, name in ((a_q, 0, "rotq"), (a_k, 2, "rotk")):
                dve.wait_ge(*e.at(name))
                do(nc.vector.tensor_tensor(per_head(x), per_head(x), a_cos.unsqueeze(1).to_broadcast([P, H4, T]),
                                           ALU.mult))
                do(nc.vector.tensor_tensor(per_head(c_kt), per_head(bank(b0, 2)),
                                           a_sin.unsqueeze(1).to_broadcast([P, H4, T]), ALU.mult))
                do(nc.vector.tensor_tensor(x, x, c_kt, ALU.add))
            v.name("rotated")
            dve.wait_ge(*e.at("ar0"))
            for h in range(H4):
                at = c_AT[:, h * T:(h + 1) * T].rearrange("p (t i) -> p t i", i=P)
                mask = consts[:, C_RET + h * P:C_RET + (h + 1) * P].unsqueeze(1).to_broadcast([P, NT, P])
                nc.vector.tensor_tensor(at, bank(6, 2)[:, h * T:(h + 1) * T].rearrange("p (t i) -> p t i", i=P),
                                        mask, ALU.mult).then_inc(*v.step())
            v.name("ataken")
            qdec = consts[:, C_RETQ:C_RETQ + H4 * CH].rearrange("p (h i) -> p h i", h=H4)
            for c in range(NCH):
                cs = slice(c * CH, (c + 1) * CH)
                nc.vector.tensor_tensor(per_head(c_qt)[:, :, cs], per_head(a_q)[:, :, cs], qdec, ALU.mult)\
                    .then_inc(*v.step())
            v.name("aqd")
            attend_vector(dve, RET, lambda h, c: CHUNK_DECAY[h])
            for n in range(2):
                ffn_weights_lo(dve, n)
            add_residual(dve, st, "out2")

        def cumulate(dve, x):
            v = V[x.st]
            for c in range(x.N // CH):
                g = x.g[:, c * CH:(c + 1) * CH]
                nc.vector.tensor_tensor_scan(g, ones[:, 0:CH], g, 0.0, ALU.mult, ALU.add).then_inc(*v.step())

        f_silu = [carve(2400 + 512 * n, 512) for n in range(2)]
        f_hid = [carve(3424 + 512 * n, 512) for n in range(2)]
        f_hi_at = ARENA_CUTS[0] + ARENA_CUTS[1]
        f_hid_hi = [carve_r(512 * n, 512) for n in range(2)]
        f_hid_lo = [carve_r(1024 + 512 * n, 512) for n in range(2)]
        F_UNITS = [("g", 0), ("u", 0)]
        for c in range(1, FFC):
            F_UNITS += [("g", c), ("u", c), ("d", c - 1)]
        F_UNITS.append(("d", FFC - 1))
        F_HI = 4

        def ffn_unit(n):
            what, c = F_UNITS[n]
            name = f"ffn_d{c}" if what == "d" else f"ffn_gu{c}"
            slot = slot_of("two", name)
            _, landed_sem, value = piece("two", name)
            hi = carve_r(f_hi_at + (n % F_HI) * HALF, HALF)
            if what == "d":
                views = [x.rearrange("p (f n) -> p f n", n=D)
                         for x in (ring[:, slot, 0:HALF], ring_r[slot][:, 0:HALF], hi)]
            else:
                a = "gu".index(what)
                views = [x.rearrange("p (k a n) -> p k a n", a=2, n=256)[:, :, a, :]
                         for x in (ring[:, slot, :], ring_r[slot][:, :])]
                views.append(hi.rearrange("p (k n) -> p k n", n=256))
            return (*views, (landed_sem, value), f"{name}_{1 if what == 'd' else a}")

        def ffn_tensor(pe):
            st = "ffn"
            e, s, v = E[st], S[st], V[st]
            norm_tensor(pe, st, "n")
            pe.wait_ge(*v.at("tok_lo"))

            def gate_or_up(n, a, c):
                _, lo, hi, _, name = ffn_unit(n)
                for j in range(2):
                    for k in range(KC):
                        x = slice(j * P, (j + 1) * P)
                        mm = three(bank(2 * (c % 2) + a)[:, j * T:(j + 1) * T], (hi[:, k, x], lo[:, k, x]),
                                   (tok[0][:, k, :], tok[1][:, k, :]), k == 0, k == KC - 1)
                mm.then_inc(*e.step())
                e.name(name)

            def down(n, c):
                _, lo, hi, _, name = ffn_unit(n)
                pe.wait_ge(*v.at(f"hid_lo{c}"))
                for f in range(2):
                    y = slice(f * T, (f + 1) * T)
                    for d in range(KC):
                        x = slice(d * P, (d + 1) * P)
                        mm = three(bank(4 + d // 2)[:, (d % 2) * T:(d % 2 + 1) * T], (hi[:, f, x], lo[:, f, x]),
                                   (f_hid_hi[c % 2][:, y], f_hid_lo[c % 2][:, y]),
                                   c == 0 and f == 0 and d % 2 == 0, c == FFC - 1 and f == 1,
                                   skip_group_check=True)
                mm.then_inc(*e.step())
                e.name(name)

            for n, (what, c) in enumerate(F_UNITS):
                pe.wait_ge(*v.at(f"w_lo{n}"))
                if what == "d":
                    down(n, c)
                else:
                    if what == "g" and c >= 2:
                        pe.wait_ge(*v.at(f"hid{c - 2}"))
                    gate_or_up(n, "gu".index(what), c)

        def ffn_steps(split, after):
            for n in range(2, len(F_UNITS) + 2):
                if n < len(F_UNITS):
                    split(n)
                after(*F_UNITS[n - 2])

        def ffn_scalar(act):
            st = "ffn"
            e, s, v = E[st], S[st], V[st]

            def split(n):
                src, _, hi, landed_at, _ = ffn_unit(n)
                act.wait_ge(*landed_at)
                if n >= F_HI:
                    act.wait_ge(*e.at(ffn_unit(n - F_HI)[4]))
                nc.scalar.activation(hi, src, ACT.Copy).then_inc(*s.step())
                s.name(f"w_hi{n}")

            def hidden_hi(c):
                act.wait_ge(*v.at(f"hid{c}"))
                if c >= 2:
                    act.wait_ge(*e.at(f"ffn_d{c - 2}_1"))
                nc.scalar.activation(f_hid_hi[c % 2], f_hid[c % 2], ACT.Copy).then_inc(*s.step())
                s.name(f"hid_hi{c}")

            def after(what, c):
                if what == "g":
                    act.wait_ge(*e.at(f"ffn_gu{c}_0"))
                    if c >= 2:
                        act.wait_ge(*v.at(f"hid{c - 2}"))
                    nc.scalar.activation(f_silu[c % 2], bank(2 * (c % 2)), ACT.Silu).then_inc(*s.step())
                    s.name(f"silu{c}")
                    if c:
                        hidden_hi(c - 1)
                elif what == "u" and c == FFC - 1:
                    hidden_hi(c)

            act.wait_ge(*V["mix2"].at("ay"))
            for n in range(2):
                split(n)
            norm_scalar(act, st, "n", [V["mix2"].at("x_out2")])
            tokens_hi(act, st)
            ffn_steps(split, after)

        def ffn_weights_lo(dve, n):
            src, lo, hi, _, _ = ffn_unit(n)
            dve.wait_ge(*S["ffn"].at(f"w_hi{n}"))
            nc.vector.tensor_tensor(lo, src, hi.bitcast(F32), ALU.subtract).then_inc(*V["ffn"].step())
            V["ffn"].name(f"w_lo{n}")

        def ffn_vector(dve):
            st = "ffn"
            e, s, v = E[st], S[st], V[st]
            norm_vector(dve, st, "n", param("ffn2_g", 8), hT, "h")
            tokens_lo(dve, st)

            def hidden_lo(c):
                dve.wait_ge(*s.at(f"hid_hi{c}"))
                if c >= 2:
                    dve.wait_ge(*e.at(f"ffn_d{c - 2}_1"))
                nc.vector.tensor_tensor(f_hid_lo[c % 2], f_hid[c % 2], f_hid_hi[c % 2].bitcast(F32), ALU.subtract)\
                    .then_inc(*v.step())
                v.name(f"hid_lo{c}")

            def after(what, c):
                if what == "u":
                    dve.wait_ge(*s.at(f"silu{c}"))
                    dve.wait_ge(*e.at(f"ffn_gu{c}_1"))
                    if c >= 2:
                        dve.wait_ge(*v.at(f"hid_lo{c - 2}"))
                    nc.vector.tensor_tensor(f_hid[c % 2], f_silu[c % 2], bank(2 * (c % 2) + 1), ALU.mult)\
                        .then_inc(*v.step())
                    v.name(f"hid{c}")
                if what == "g" and c:
                    hidden_lo(c - 1)
                elif what == "u" and c == FFC - 1:
                    hidden_lo(c)

            ffn_steps(lambda n: ffn_weights_lo(dve, n), after)
            dve.wait_ge(*e.at(f"ffn_d{FFC - 1}_1"))
            for b in range(4):
                x = xT[:, 2 * b:2 * b + 2, :]
                nc.vector.tensor_tensor(x, x, bank(4 + b).rearrange("p (b t) -> p b t", t=T), ALU.add)\
                    .then_inc(*v.step())
            v.name("x")

        B3 = len(PROJ1) + len(PROJ2)
        HG = []
        for half in range(2):
            g_, k_, q_, v_, gate_ = (carve(tail_at + HC * (5 * half + n), HC) for n in range(5))
            HG.append(Gated("hgrn", f"h{half}", 4, q_, k_, g_, v_, gate_, y_cat[:, half * HC:(half + 1) * HC],
                            param("hgrn_g")))

        def hgrn_tensor(pe):
            st = "hgrn"
            e, s, v = E[st], S[st], V[st]
            norm_tensor(pe, st, "n")
            pe.wait_ge(*v.at("h"))

            def proj(name):
                (project_rows if name[1] == "i" else project)(
                    pe, st, "two", name, free_by(st, PROJ3, name, lambda n, half: [s.at(f"{n}_{half}")]))

            for what in "fqig":
                proj(f"h{what}0")
            for n, what in enumerate("fqig"):
                gated_tensor_round(pe, HG[0], 2 * n)
                proj(f"h{what}1")
                if 2 * n + 1 <= NL:
                    gated_tensor_round(pe, HG[0], 2 * n + 1)
            gated_tensor_end(pe, HG[0])
            out = OutProjection(pe, st, "two", "out3", y_cat, range(4), [v.at("h0y"), s.at("hg1_1")])
            for n in range(NL + 1):
                gated_tensor_round(pe, HG[1], n)
                if n >= 2:
                    out.fill(1)
            gated_tensor_end(pe, HG[1], out)
            out.finish(v.at("h1y"))

        def hgrn_scalar(act):
            st = "hgrn"
            e, s, v = E[st], S[st], V[st]
            act.preload_act_table_set(EXP_LN)
            weights_hi_of(act, st, "two", "hf0", range(4))
            norm_scalar(act, st, "n", [V["ffn"].at("x")])
            tokens_hi(act, st)
            act.wait_ge(*v.at("lbdiff"))
            nc.scalar.activation(c_small[:, 40:56], c_small[:, 40:56], ACT.Exp).then_inc(*s.step())
            s.name("lbexp")

            def keep(half, what, out, **kw):
                keep_banks(act, st, f"h{what}{half}", PROJ3, B3, out, **kw)

            def first(half):
                x = HG[half]
                keep(half, "f", halves(x.k), func=ACT.Exp, scale=-1.0)
                act.wait_ge(*v.at(f"h{half}f"))
                nc.scalar.activation(x.g, x.g, ACT.Ln).then_inc(*s.step())
                s.name(f"h{half}ln")

            first(0)
            keep(0, "q", halves(HG[0].q), func=ACT.Silu)
            keep(0, "i", halves(HG[0].v))
            s.name("h0v")
            keep(0, "g", halves(HG[0].gate), func=ACT.Silu)
            s.name("h0gate")
            act.preload_act_table_set(EXP_LN)
            gated_scalar_round(act, HG[0], 1)
            first(1)
            gated_scalar_round(act, HG[0], 2)
            gated_scalar_round(act, HG[0], 3)
            keep(1, "q", halves(HG[1].q))
            gated_scalar_round(act, HG[0], 4)
            gated_scalar_round(act, HG[0], 5)
            keep(1, "i", halves(HG[1].v))
            s.name("h1v")
            gated_scalar_round(act, HG[0], 6)
            keep(1, "g", halves(HG[1].gate))
            nc.scalar.activation(HG[1].q, HG[1].q, ACT.Silu).then_inc(*s.step())
            s.name("hq1_1b")
            act.wait_ge(*s.at("hg1_1"))
            nc.scalar.activation(HG[1].gate, HG[1].gate, ACT.Silu).then_inc(*s.step())
            s.name("h1gate")
            act.preload_act_table_set(EXP_LN)
            gated_scalar_end(act, HG[0])
            attend_scalar(act, HG[0])
            for n in range(1, NL + 1):
                gated_scalar_round(act, HG[1], n)
            gated_scalar_end(act, HG[1])
            attend_scalar(act, HG[1])

        def hgrn_pool(pool):
            names = PROJ3[:-2]
            for name in names[:5]:
                weights_lo_of(pool, "hgrn", "two", name)
            for half in range(2):
                for n in range(1, NL + 1):
                    gated_pool_round(pool, HG[half], n)
                    if half == 0 and n % 2 and n < 6:
                        weights_lo_of(pool, "hgrn", "two", names[5 + n // 2])
                gated_pool_end(pool, HG[half])

        def hgrn_vector(dve):
            st = "hgrn"
            e, s, v = E[st], S[st], V[st]

            def do(ins):
                ins.then_inc(*v.step())
                dve.wait_ge(*v.last())

            lb = param("lb", 16)
            l0, l1 = c_small[:, 40:48], c_small[:, 48:56]
            m = c_small[:, 56:64]
            dve.wait_ge(*V["ffn"].at("x"))
            do(nc.vector.tensor_tensor(m, lb[:, 0:8], lb[:, 8:16], ALU.max))
            do(nc.vector.tensor_tensor(l0, lb[:, 0:8], m, ALU.subtract))
            do(nc.vector.tensor_tensor(l1, lb[:, 8:16], m, ALU.subtract))
            v.name("lbdiff")
            norm_vector(dve, st, "n", param("mix2_g", 8, 8), hT, "h")
            tokens_lo(dve, st)
            dve.wait_ge(*s.at("lbexp"))
            do(nc.vector.tensor_tensor(m, l0, l1, ALU.add))
            do(nc.vector.reciprocal(m, m))
            do(nc.vector.tensor_tensor(l0, l0, m, ALU.mult))
            do(nc.vector.tensor_tensor(l1, l1, m, ALU.mult))
            do(nc.vector.tensor_tensor(l1, l1, l0, ALU.add))
            do(nc.vector.tensor_tensor(c_lb, l1, l0, ALU.subtract))
            do(nc.vector.tensor_scalar(c_omlb, c_lb, -1.0, 1.0, ALU.mult, ALU.add))
            do(nc.vector.tensor_scalar(c_lb, c_lb, 1e-19, None, ALU.max))

            def first(half):
                x = HG[half]
                dve.wait_ge(*s.at(f"hf{half}_1"))
                do(nc.vector.tensor_scalar(x.k, x.k, BIG, None, ALU.min))
                do(nc.vector.tensor_scalar(x.g, x.k, 1.0, None, ALU.add))
                do(nc.vector.reciprocal(x.g, x.g))
                for h in range(H4):
                    hs = slice(h * T, (h + 1) * T)
                    n = half * H4 + h
                    nc.vector.scalar_tensor_tensor(x.k[:, hs], x.k[:, hs], c_omlb[:, n:n + 1], x.g[:, hs],
                                                   ALU.mult, ALU.mult).then_inc(*v.step())
                dve.wait_ge(*v.last())
                for h in range(H4):
                    hs = slice(h * T, (h + 1) * T)
                    n = half * H4 + h
                    nc.vector.tensor_scalar(x.g[:, hs], x.g[:, hs], c_omlb[:, n:n + 1], c_lb[:, n:n + 1],
                                            ALU.mult, ALU.add).then_inc(*v.step())
                v.name(f"h{half}f")

            def second(half):
                x = HG[half]
                dve.wait_ge(*s.at(f"h{half}ln"))
                cumulate(dve, x)
                dve.wait_ge(*v.last())
                dve.wait_ge(*s.at("hq0_1" if half == 0 else "hq1_1b"))
                do(nc.vector.tensor_scalar(x.q, x.q, float(P) ** -0.5, None, ALU.mult))
                v.name(f"h{half}ready")

            first(0)
            second(0)
            gated_vector_round(dve, HG[0], 0)
            first(1)
            for n in range(1, NL + 1):
                gated_vector_round(dve, HG[0], n)
            gated_vector_end(dve, HG[0])

            def decay(h, c):
                return c_decay[:, h * 4 + c:h * 4 + c + 1]

            attend_vector(dve, HG[0], decay)
            second(1)
            for n in range(NL + 1):
                gated_vector_round(dve, HG[1], n)
            gated_vector_end(dve, HG[1])
            attend_vector(dve, HG[1], decay)
            add_residual(dve, st, "out3")

        def final_tensor(pe):
            norm_tensor(pe, "final", "n")

        def final_scalar(act, waits):
            act.preload_act_table_set(EXP_LN)
            norm_scalar(act, "final", "n", waits)

        def final_vector(dve):
            norm_vector(dve, "final", "n", param("final2_g", 8), hT, "h")

        @block.tensor
        def _(pe):
            mixer1_tensor(pe)
            if upto == 1:
                return
            route_tensor(pe, M1)
            moe_tensor(pe, M1)
            if upto == 2:
                return
            mixer2_tensor(pe)
            if upto == 3:
                return
            ffn_tensor(pe)
            if upto == 4:
                return
            hgrn_tensor(pe)
            if upto == 5:
                return
            route_tensor(pe, M2)
            moe2_tensor(pe)
            final_tensor(pe)

        @block.scalar
        def _(act):
            mixer1_scalar(act)
            if upto == 1:
                return
            route_scalar(act, M1, [V["mix1"].at("x_out1")])
            n = moe_scalar(act, M1)
            if upto == 2:
                return
            mixer2_scalar(act, [(moe_sems["moe1"]["spread_added"], n * 4 + 5)])
            if upto == 3:
                return
            ffn_scalar(act)
            if upto == 4:
                return
            hgrn_scalar(act)
            if upto == 5:
                return
            route_scalar(act, M2, [V["hgrn"].at("x_out3")])
            n = moe2_scalar(act)
            final_scalar(act, [(moe_sems["moe2"]["spread_added"], n * 4 + 5)])

        @block.gpsimd
        def _(pool):
            mixer1_pool(pool)
            if upto < 3:
                return
            mixer2_pool(pool)
            if upto < 5:
                return
            hgrn_pool(pool)

        @block.vector
        def _(dve):
            mixer1_vector(dve)
            if upto == 1:
                return
            route_vector(dve, M1)
            moe_vector(dve, M1)
            if upto == 2:
                return
            mixer2_vector(dve)
            if upto == 3:
                return
            ffn_vector(dve)
            if upto == 4:
                return
            hgrn_vector(dve)
            if upto == 5:
                return
            route_vector(dve, M2)
            moe2_vector(dve)
            final_vector(dve)
    return found


_BIG = ["w_in", "w_out", "w_gate", "w_up", "w_down", "ab_w_in_2", "ab_w_out_2", "ffn_w_gate_2", "ffn_w_up_2",
        "ffn_w_down_2", "c_w_in_2", "c_w_out_2", "moe_w_gate_2", "moe_w_up_2", "moe_w_down_2"]


def laid_out(inputs):
    a = {k: np.asarray(v) for k, v in inputs.items()}

    def columns(v):
        v = v.reshape(-1, v.shape[-1] // P, P)
        return v.transpose(2, 0, 1).reshape(P, -1)

    def matrix(w):
        return w.reshape(KC, P, -1).transpose(1, 0, 2).reshape(P, -1)

    def every(v):
        return np.broadcast_to(v.reshape(1, -1), (P, v.size))

    gla_w = np.zeros((P, 256), np.float32)
    gla_w[:16] = a["gla_w_a2_2"][0]
    parts = {
        "mix_g": columns(a["mix_norm_g"]), "ffn_g": columns(a["ffn_norm_g"]), "final_g": columns(a["final_norm_g"]),
        "mix2_g": columns(a["norm_mix_g_2"]), "ffn2_g": columns(a["norm_ffn_g_2"]),
        "final2_g": columns(a["final_norm_g_2"]), "conv_a": columns(a["conv_a_w"][0]),
        "conv_a_g": columns(a["conv_a_norm_g"]), "dn_conv": columns(a["dn_conv_w"][0]),
        "dn_g": columns(a["dn_norm_g"]), "ret_g": columns(a["ret_norm_g_2"]), "gla_g": columns(a["gla_norm_g_2"]),
        "hgrn_g": columns(a["hgrn_norm_g_2"]), "lb": columns(a["hgrn_lb_logits_2"]),
        "gla_b": columns(a["gla_b_a2_2"]), "a_log": every(a["dn_a_log"]), "dt_bias": every(a["dn_dt_bias"]),
        "router1": matrix(np.concatenate([a["router_group_w"][0], a["router_expert_w"][0]], axis=1)),
        "router2": matrix(a["moe_router_2"][0]), "tail1": matrix(a["w_in"][0][:, 3584:]),
        "tail2": matrix(a["ab_w_in_2"][0][:, 3584:]), "gla_w": gla_w,
    }
    out = {name: np.ascontiguousarray(a[name]) for name in _BIG}
    out["small"] = np.ascontiguousarray(np.concatenate([parts[n] for n, _ in _SMALL], axis=1))
    out["consts"] = constants()
    out["xT"] = np.ascontiguousarray(a["x"][0].reshape(T, KC, P).transpose(2, 1, 0))
    out["positions"] = np.ascontiguousarray(np.broadcast_to(a["positions_2"].reshape(1, T), (P, T)))
    return out


def write_out(nc, known, arrays, upto=99):
    A = {n: nc.dram_tensor(f"in_{n}", a.shape, mybir.dt.from_np(a.dtype), kind="ExternalInput").ap()
         for n, a in arrays.items()}
    A["out"] = nc.dram_tensor("out_0", (P, KC, T), F32, kind="ExternalOutput").ap()
    return program(nc, known, A, upto)


def kernel(**inputs):
    import concourse.bacc as _bacc
    from concourse.bass_utils import run_bass_kernel_spmd as _run

    arrays = laid_out(inputs)
    core = {"target_bir_lowering": False, "num_devices": 1, "dynamic_dma_scratch_size": 1024}
    known = write_out(_bacc.Bacc("TRN2", **core), {}, arrays)
    nc = _bacc.Bacc("TRN2", **core)
    write_out(nc, known, arrays)
    r = _run(nc, [{f"in_{n}": a for n, a in arrays.items()}], core_ids=[0])
    out = r.results[0]["out_0"]
    return out.transpose(2, 1, 0).reshape(1, T, D)
```

```python
from contextlib import ExitStack

import concourse.bass as bass
from concourse import mybir
import numpy as np

F32 = mybir.dt.float32
F32R = mybir.dt.float32r
I32 = mybir.dt.int32
ALU = mybir.AluOpType
ACT = mybir.ActivationFunctionType
AX_X = mybir.AxisListType.X
EXP_LN = "natural_log_exp_and_others"

P = 128
T = 256
NT = T // P
D = 1024
KC = D // P
CH = 64
NCH = T // CH
H4 = 4
HC = H4 * T
PIECE = 4096
SLOTS = 7
DENSE_SLOTS = 5
TOKENS, HIS = 5, 6
LEVELS = (32, 16, 8, 4, 2, 1)
EPS = 1e-6
BIG = 1e30

C_EYE, C_GROUP, C_CAUSAL, C_BEFORE, C_IOTA, C_ROT = (n * P for n in range(6))
C_LEVEL = 6 * P
C_RET = C_LEVEL + len(LEVELS) * P
C_RETQ = C_RET + H4 * P
C_RETK = C_RETQ + H4 * CH
C_HALF = C_RETK + H4
C_FREQ = C_HALF + 2
C_DESC = C_FREQ + 1
C_SMALL_END = C_DESC + 32
CONSTS = C_SMALL_END

_SMALL = [("mix_g", 8), ("ffn_g", 8), ("final_g", 8), ("mix2_g", 16), ("ffn2_g", 16), ("final2_g", 8),
          ("conv_a", 12), ("conv_a_g", 4), ("dn_conv", 48), ("dn_g", 1), ("ret_g", 1), ("gla_g", 1),
          ("hgrn_g", 1), ("lb", 16), ("gla_b", 2), ("a_log", 4), ("dt_bias", 4), ("router1", 288),
          ("router2", 64), ("tail1", 64), ("tail2", 128), ("gla_w", 256)]
SMALL = {}
_at = 0
for _name, _n in _SMALL:
    SMALL[_name] = _at
    _at += _n
SMALLS = _at

LOG_GAMMA = np.log1p(-np.exp2(-5.0 - np.arange(4, dtype=np.float32))).astype(np.float32)
CHUNK_DECAY = [float(x) for x in np.exp(CH * LOG_GAMMA)]


def constants():
    p, f = np.arange(P)[:, None], np.arange(P)[None, :]
    same = p // CH == f // CH
    c = np.zeros((P, CONSTS), np.float32)
    c[:, C_EYE:C_EYE + P] = p == f
    c[:, C_GROUP:C_GROUP + P] = same
    c[:, C_CAUSAL:C_CAUSAL + P] = same & (p <= f)
    c[:, C_BEFORE:C_BEFORE + P] = p < f
    c[:, C_IOTA:C_IOTA + P] = f
    c[:, C_ROT:C_ROT + P] = np.where(p == f + 64, -1.0, 0.0) + np.where(p == f - 64, 1.0, 0.0)
    for n, s in enumerate(LEVELS):
        both = p // (2 * s) == f // (2 * s)
        c[:, C_LEVEL + n * P:C_LEVEL + (n + 1) * P] = both & (p % (2 * s) < s) & (f % (2 * s) >= s)
    for h in range(H4):
        rel = (f - p).astype(np.float32)
        c[:, C_RET + h * P:C_RET + (h + 1) * P] = np.where(same & (p <= f), np.exp(np.minimum(rel, P) * LOG_GAMMA[h]), 0)
        c[:, C_RETQ + h * CH:C_RETQ + (h + 1) * CH] = np.exp((np.arange(CH, dtype=np.float32) + 1) * LOG_GAMMA[h])
        c[:, C_RETK + h] = np.exp((CH - 1.0 - np.arange(P) % CH) * LOG_GAMMA[h])
    c[:, C_HALF] = np.arange(P) < CH
    c[:, C_HALF + 1] = np.arange(P) >= CH
    c[:, C_FREQ] = np.float32(10000.0) ** (-(np.arange(P) % 64 * 2).astype(np.float32) / 128)
    c[:, C_DESC:C_DESC + 32] = 32 - np.arange(32)
    return c


class Steps:

    def __init__(self, sem, label, known, found):
        self.sem, self.label, self.known, self.found, self.n = sem, label, known, found, 0

    def step(self):
        self.n += 1
        return self.sem, 1

    def name(self, what):
        assert (self.label, what) not in self.found, (self.label, what)
        self.found[self.label, what] = self.n

    def at(self, what):
        return self.sem, self.known[self.label, what] if self.known else 1

    def last(self, back=0):
        return self.sem, self.n - back


def program(nc, known, A):
    found = {}
    ctx = ExitStack()
    with ctx:
        def sb(name, shape, dt=F32):
            return ctx.enter_context(nc.sbuf_tensor(name, shape, dt))

        def sem(name):
            return ctx.enter_context(nc.semaphore(name))

        def steps(label):
            return Steps(sem(label), label, known, found)

        def two_views(name, shape, cuts):
            with ExitStack() as parts:
                rounded = [parts.enter_context(nc.sbuf_tensor(f"{name}_r{n}", [P, size], F32R))
                           for n, size in enumerate(cuts)]
            return sb(name, shape), rounded

        ring, ring_r = two_views("ring", [P, SLOTS, PIECE], [PIECE] * SLOTS)
        xT = sb("xT", [P, KC, T])
        hT = sb("hT", [P, KC, T])
        consts = sb("consts", [P, CONSTS])
        small = sb("small", [P, SMALLS])
        ones = sb("ones", [P, P])
        zero1 = sb("zero1", [P, 4])
        ARENA = 20700
        ARENA_CUTS = [2400, 7984, 10240]
        arena, arena_r = two_views("arena", [P, ARENA], ARENA_CUTS)
        trips = sb("trips", [P, 2], I32)
        psum = ctx.enter_context(nc.psum_tensor("psum", [P, 8, 512], F32))

        eye = consts[:, C_EYE:C_EYE + P]
        group_ones = consts[:, C_GROUP:C_GROUP + P]
        causal = consts[:, C_CAUSAL:C_CAUSAL + P]
        before = consts[:, C_BEFORE:C_BEFORE + P]

        def level_mask(n):
            return consts[:, C_LEVEL + n * P:C_LEVEL + (n + 1) * P]

        def param(name, n=1, at=0):
            return small[:, SMALL[name] + at:SMALL[name] + at + n]

        def carve(at, n):
            assert at + n <= ARENA
            return arena[:, at:at + n]

        def carve_r(at, n):
            part = 0
            while at >= ARENA_CUTS[part]:
                at -= ARENA_CUTS[part]
                part += 1
            assert at + n <= ARENA_CUTS[part]
            return arena_r[part][:, at:at + n]

        def bank(b, n=1):
            return psum[:, b:b + n, :].rearrange("p b c -> p (b c)")

        def per_head(ap):
            return ap.rearrange("p (h t) -> p h t", h=H4)

        def inst(ap, h, t):
            return ap[:, h * T + t * P:h * T + t * P + P]

        def spread(mask, n=8):
            return mask.unsqueeze(1).to_broadcast([P, n, P])

        def blocks(ap):
            return ap.rearrange("p (n i) -> p n i", i=P)

        loaded_small = sem("loaded_small")
        loaded_consts = sem("loaded_consts")
        loaded_x = sem("loaded_x")
        landed = {part: [sem(f"{part}_landed_{s}") for s in range(SLOTS)]
                  for part in ("one", "moe1", "two", "moe2")}
        loaded_positions = sem("loaded_positions")
        out_written = sem("out_written")
        stages = ("mix1", "route1", "mix2", "ffn", "hgrn", "route2", "final")
        V = {s: steps(f"{s}_vector") for s in stages}
        S = {s: steps(f"{s}_scalar") for s in stages}
        E = {s: steps(f"{s}_tensor") for s in stages}
        G = {s: steps(f"{s}_pool") for s in stages}
        moe_sems = {}
        for m in ("moe1", "moe2"):
            moe_sems[m] = {w: sem(f"{m}_{w}") for w in (
                "gate_done", "up_done", "silu_done", "hidden_done", "hiddenT_done", "hiddenT_kept",
                "down_done", "y_kept", "shareT_done", "shareT_kept", "spread_done", "spread_added",
                "gathered", "gathered_kept", "pick_ready", "share_ready", "start")}
        gathered_lo, hiddenT_lo = sem("moe2_gathered_lo"), sem("moe2_hiddenT_lo")
        weights_hi, weights_lo = sem("moe2_weights_hi"), sem("moe2_weights_lo")

        def cols(w, c0, n=512):
            return w[:, c0:c0 + n].rearrange("(k p) n -> p k n", p=P), KC, n

        def rows(w, r0, k):
            return w[r0:r0 + k * P, :].rearrange("(k p) n -> p k n", p=P), k, D

        w_in, w_out = A["w_in"][0], A["w_out"][0]
        ab_in, ab_out = A["ab_w_in_2"][0], A["ab_w_out_2"][0]
        c_in, c_out = A["c_w_in_2"][0], A["c_w_out_2"][0]
        ffn_g, ffn_u, ffn_d = A["ffn_w_gate_2"][0], A["ffn_w_up_2"][0], A["ffn_w_down_2"][0]
        FF = ffn_g.shape[1]
        FFC = FF // 256
        ONE = [("q", cols(w_in, 1536)), ("k", cols(w_in, 2048)), ("v", cols(w_in, 2560)),
               ("a_h", cols(w_in, 0)), ("a_c", cols(w_in, 1024)), ("a_b", cols(w_in, 512)),
               ("z", cols(w_in, 3072)), ("out1_0", cols(w_out, 0)), ("out1_1", cols(w_out, 512))]
        TWO = [("bqk", cols(ab_in, 2048)), ("bv", cols(ab_in, 2560)), ("aq", cols(ab_in, 0)),
               ("ak", cols(ab_in, 512)), ("bg", cols(ab_in, 3072)), ("av", cols(ab_in, 1024)),
               ("ag", cols(ab_in, 1536)), ("out2_0", cols(ab_out, 0)), ("out2_1", cols(ab_out, 512))]
        for c in range(FFC):
            TWO.append((f"ffn_gu{c}", (cols(ffn_g, c * 256, 256), cols(ffn_u, c * 256, 256))))
            if c:
                TWO.append((f"ffn_d{c - 1}", rows(ffn_d, (c - 1) * 256, 2)))
        TWO.append((f"ffn_d{FFC - 1}", rows(ffn_d, (FFC - 1) * 256, 2)))
        for half in range(2):
            for what, at in (("f", 1024), ("q", 0), ("i", 2048), ("g", 3072)):
                TWO.append((f"h{what}{half}", cols(c_in, at + half * 512)))
        TWO += [("out3_0", cols(c_out, 0)), ("out3_1", cols(c_out, 512))]
        order = {"one": [n for n, _ in ONE], "two": [n for n, _ in TWO]}

        def piece(part, name):
            n = order[part].index(name)
            before_ = [order[part][m] for m in range(n % DENSE_SLOTS, n + 1, DENSE_SLOTS)]
            slot = slot_of(part, name)
            return (ring[:, slot, :], landed[part][slot],
                    sum(32 if x.startswith("ffn_gu") else 16 for x in before_))

        def slot_of(part, name):
            return order[part].index(name) % DENSE_SLOTS

        def last_in(part, slot):
            return [name for name in order[part] if slot_of(part, name) == slot][-1]

        def piece_used(name):
            stage = ("mix1" if name in order["one"] else "ffn" if name.startswith("ffn") else
                     "hgrn" if name[0] == "h" or name.startswith("out3") else "mix2")
            return E[stage].at(f"{name}_1")

        NE1, NE2, FF1, FF2 = 32, 8, 512, 3584
        PAIRS = NE1 // 2
        UNITS = FF2 // 512
        C1, C2 = 64, 128
        PASSES1, PASSES2 = T // C1, T // C2
        wg1, wu1, wd1 = A["w_gate"][0], A["w_up"][0], A["w_down"][0]
        wg2, wu2, wd2 = A["moe_w_gate_2"][0], A["moe_w_up_2"][0], A["moe_w_down_2"][0]
        MOE2_ORDER = [("g", 0), ("u", 0)]
        for u in range(1, UNITS):
            MOE2_ORDER += [("g", u), ("u", u), ("d", u - 1)]
        MOE2_ORDER += [("d", UNITS - 1)]
        NP2 = len(MOE2_ORDER)
        TURNS2 = NP2 // SLOTS
        assert NP2 % SLOTS == 0

        tail_at = HC * 10
        a_pos = carve(tail_at + HC * 8, T).bitcast(I32)
        block = ctx.enter_context(nc.Block())

        @block.sync
        def _(sp):
            sp.dma_start(xT[:, :, :], A["xT"]).then_inc(loaded_x, 16)
            sp.dma_start(small[:, :], A["small"]).then_inc(loaded_small, 16)

            def send(view, slot, landed_sem):
                src, k, n = view
                sp.dma_start(ring[:, slot, 0:k * n].rearrange("p (k n) -> p k n", n=n), src)\
                    .then_inc(landed_sem, 16)

            def send_part(part, pieces, wait_before=None, after_first=None):
                for n, (name, view) in enumerate(pieces):
                    if n == DENSE_SLOTS and after_first:
                        after_first()
                    if part == "one" and n == 1:
                        sp.dma_start(consts[:, :], A["consts"]).then_inc(loaded_consts, 16)
                    slot = slot_of(part, name)
                    if n >= DENSE_SLOTS:
                        sp.wait_ge(*piece_used(pieces[n - DENSE_SLOTS][0]))
                    elif wait_before is not None:
                        wait_before(slot)
                    if name.startswith("ffn_gu"):
                        for half, (src, k, w) in enumerate(view):
                            sp.dma_start(ring[:, slot, :].rearrange("p (k a n) -> p k a n", a=2, n=256)[:, :, half, :],
                                         src).then_inc(landed[part][slot], 16)
                    else:
                        send(view, slot, landed[part][slot])

            send_part("one", ONE)


            def moe1_piece(expert, s):
                w, k, n = ((wg1, KC, FF1), (wu1, KC, FF1), (wd1, 4, D))[s // 2]
                return w[bass.ds(expert, 1), :, :].rearrange("e (k p) n -> p (e k) n", p=P), k, n

            for s in (0, 1, 4, 5, 2, 3):
                sp.wait_ge(*piece_used(last_in("one", s) if s < DENSE_SLOTS else "z"))
                w, k, n = ((wg1, KC, FF1), (wu1, KC, FF1), (wd1, 4, D))[s // 2]
                send((w[s % 2].rearrange("(k p) n -> p k n", p=P), k, n), s, landed["moe1"][s])
            sp.wait_ge(*V["route1"].at("trips"))
            trips1 = sp.value_load(trips[0:1, 0:1], min_val=PAIRS, max_val=PAIRS * PASSES1)
            pair_reg = sp.alloc_register("pair")
            with sp.Fori(1, trips1) as i:
                sp.reg_alu(pair_reg, i, PAIRS - 1, op=ALU.bitwise_and)
                pair = sp.snap(pair_reg, min_val=0, max_val=PAIRS - 1)
                expert = [sp.snap(pair * 2 + x, min_val=x, max_val=NE1 - 2 + x) for x in range(2)]
                for s in range(6):
                    sp.wait_ge(moe_sems["moe1"][("gate_done", "up_done", "down_done")[s // 2]], i + 1)
                    send(moe1_piece(expert[s % 2], s), s, landed["moe1"][s])

            def after_moe1(slot):
                if slot < 6:
                    sp.wait_ge(moe_sems["moe1"][("gate_done", "up_done", "down_done")[slot // 2]], trips1 + 1)

            def positions():
                sp.wait_ge(moe_sems["moe1"]["spread_added"], trips1 * 4 + 5)
                sp.dma_start(a_pos, A["positions"]).then_inc(loaded_positions, 16)

            send_part("two", TWO, after_moe1, positions)

            def moe2_piece(e, m):
                what, u = MOE2_ORDER[m]
                if what == "d":
                    return (wd2[bass.ds(e, 1), u * 512:(u + 1) * 512, :] if not isinstance(e, int)
                            else wd2[e:e + 1, u * 512:(u + 1) * 512, :]).rearrange("e (k p) n -> p (e k) n", p=P), 4, D
                w = wg2 if what == "g" else wu2
                return (w[bass.ds(e, 1), :, u * 512:(u + 1) * 512] if not isinstance(e, int)
                        else w[e:e + 1, :, u * 512:(u + 1) * 512]).rearrange("e (k p) n -> p (e k) n", p=P), KC, 512

            def moe2_used(i, m):
                what, u = MOE2_ORDER[m - SLOTS]
                sem_ = moe_sems["moe2"][{"g": "gate_done", "u": "up_done", "d": "down_done"}[what]]
                return sem_, i * UNITS + (u + 2 - (UNITS if m < SLOTS else 0))

            for m in (1, 2, 3, 5, 6, 4, 0, *range(SLOTS, NP2)):
                slot = m % SLOTS
                if m < SLOTS:
                    sp.wait_ge(*piece_used(last_in("two", slot) if slot < DENSE_SLOTS else "hg1"))
                else:
                    sp.wait_ge(*moe2_used(0, m))
                send(moe2_piece(0, m), slot, landed["moe2"][slot])
            sp.wait_ge(*V["route2"].at("trips"))
            trips2 = sp.value_load(trips[0:1, 1:2], min_val=NE2, max_val=NE2 * PASSES2)
            expert_reg = sp.alloc_register("expert")
            with sp.Fori(1, trips2) as i:
                sp.reg_alu(expert_reg, i, NE2 - 1, op=ALU.bitwise_and)
                e = sp.snap(expert_reg, min_val=0, max_val=NE2 - 1)
                for m in range(NP2):
                    sp.wait_ge(*moe2_used(i, m))
                    send(moe2_piece(e, m), m % SLOTS, landed["moe2"][m % SLOTS])
            sp.wait_ge(*moe2_used(trips2, 0))
            send(moe2_piece(0, 0), 0, landed["moe2"][0])

            for half, name in enumerate(("h_first", "h")):
                sp.wait_ge(*V["final"].at(name))
                ks = slice(4 * half, 4 * half + 4)
                sp.dma_start(A["out"][:, ks, :], hT[:, ks, :]).then_inc(out_written, 16)
            sp.wait_ge(out_written, 32)

        SQ = carve(0, KC * T)
        RSTD = carve(KC * T, T)

        def norm_scalar(act, st, tag, waits):
            s = S[st]
            for half in range(2):
                if waits:
                    act.wait_ge(*waits[half])
                sq = SQ[:, half * 1024:(half + 1) * 1024]
                nc.scalar.activation(sq.rearrange("p (k t) -> p k t", t=T), xT[:, half * 4:half * 4 + 4, :],
                                     ACT.Square).then_inc(*s.step())
                s.name(f"{tag}_sq{half}")
            act.wait_ge(*E[st].at(f"{tag}_sum"))
            nc.scalar.activation(RSTD, bank(7)[:, 0:T], ACT.Ln, bias=eps_col, scale=1.0 / D).then_inc(*s.step())
            act.wait_ge(*s.last())
            nc.scalar.activation(RSTD, RSTD, ACT.Exp, scale=-0.5).then_inc(*s.step())
            s.name(f"{tag}_rstd")

        def norm_tensor(pe, st, tag, waits=()):
            for w in waits:
                pe.wait_ge(*w)
            for k in range(KC):
                if k % 4 == 0:
                    pe.wait_ge(*S[st].at(f"{tag}_sq{k // 4}"))
                mm = nc.tensor.matmul(bank(7)[:, 0:T], ones[:, :], SQ[:, k * T:(k + 1) * T],
                                      start=(k == 0), stop=(k == KC - 1))
            mm.then_inc(*E[st].step())
            E[st].name(f"{tag}_sum")

        def norm_vector(v, st, tag, gain, out, name, waits=()):
            v.wait_ge(*S[st].at(f"{tag}_rstd"))
            for w in waits:
                v.wait_ge(*w)
            for k in range(KC):
                nc.vector.scalar_tensor_tensor(out[:, k, :], xT[:, k, :], gain[:, k:k + 1], RSTD,
                                               ALU.mult, ALU.mult).then_inc(*V[st].step())
                if k == 3:
                    V[st].name(f"{name}_first")
            V[st].name(name)

        eps_col = zero1[:, 0:1]

        proj_count = [0]

        def three(out, a, b, start, stop, **kw):
            (ah, al), (bh, bl) = a, b
            nc.tensor.matmul(out, ah, bh, start=start, stop=False, **kw)
            nc.tensor.matmul(out, ah, bl, start=False, stop=False, **kw)
            return nc.tensor.matmul(out, al, bh, start=False, stop=stop, **kw)

        tok = [ring_r[TOKENS][:, n * KC * T:(n + 1) * KC * T].rearrange("p (k t) -> p k t", t=T) for n in range(2)]
        w_hi = ring_r[HIS][:, :].rearrange("p (k n) -> p k n", n=512)

        def tokens_hi(act, st, tag="h"):
            for half in range(2):
                act.wait_ge(*V[st].at(tag if half else f"{tag}_first"))
                ks = slice(4 * half, 4 * half + 4)
                nc.scalar.activation(tok[0][:, ks, :], hT[:, ks, :], ACT.Copy).then_inc(*S[st].step())
                S[st].name(f"tok_hi{half}")

        def round_next(act, st, part, names, name, half):
            after = names[names.index(name) + 1]
            if not after.startswith("out"):
                weights_hi_of(act, st, part, after, (2 * half, 2 * half + 1), before=name)

        def tokens_lo(dve, st):
            for half in range(2):
                dve.wait_ge(*S[st].at(f"tok_hi{half}"))
                ks = slice(4 * half, 4 * half + 4)
                nc.vector.tensor_tensor(tok[1][:, ks, :], hT[:, ks, :], tok[0][:, ks, :].bitcast(F32), ALU.subtract)\
                    .then_inc(*V[st].step())
                V[st].name(f"tok_lo{half}")

        def weights_hi_of(act, st, part, name, quarters, before=None):
            _, landed_sem, value = piece(part, name)
            w = ring[:, slot_of(part, name), :].rearrange("p (k n) -> p k n", n=512)
            act.wait_ge(landed_sem, value)
            for q in quarters:
                if before is not None:
                    act.wait_ge(*E[st].at(f"{before}_q{q}"))
                c = slice(q * P, (q + 1) * P)
                nc.scalar.activation(w_hi[:, :, c], w[:, :, c], ACT.Copy).then_inc(*S[st].step())
                S[st].name(f"{name}_hi{q}")

        def weights_lo_of(pool, st, part, name, quarters=range(4)):
            w = ring[:, slot_of(part, name), :].rearrange("p (k n) -> p k n", n=512)
            lo = ring_r[slot_of(part, name)][:, :].rearrange("p (k n) -> p k n", n=512)
            for q in quarters:
                pool.wait_ge(*S[st].at(f"{name}_hi{q}"))
                c = slice(q * P, (q + 1) * P)
                nc.gpsimd.tensor_tensor(lo[:, :, c], w[:, :, c], w_hi[:, :, c].bitcast(F32), ALU.subtract)\
                    .then_inc(*G[st].step())
                G[st].name(f"{name}_lo{q}")

        def project(pe, st, part, name, free, quarters=range(4)):
            lo = ring_r[slot_of(part, name)][:, :].rearrange("p (k n) -> p k n", n=512)
            b0 = 2 * (proj_count[0] % 2)
            proj_count[0] += 3 in quarters
            for q in quarters:
                half, j = q // 2, q % 2
                if j == 0:
                    for wait in free(half):
                        pe.wait_ge(*wait)
                pe.wait_ge(*G[st].at(f"{name}_lo{q}"))
                c = slice(q * P, (q + 1) * P)
                for k in range(KC):
                    if q == quarters[0] and k % 4 == 0:
                        pe.wait_ge(*V[st].at(f"tok_lo{k // 4}"))
                    mm = three(bank(b0 + half)[:, j * T:(j + 1) * T], (w_hi[:, k, c], lo[:, k, c]),
                               (tok[0][:, k, :], tok[1][:, k, :]), k == 0, k == KC - 1)
                mm.then_inc(*E[st].step())
                E[st].name(f"{name}_q{q}")
                if j == 1:
                    E[st].name(f"{name}_{half}")
            return b0

        def project_rows(pe, st, part, name, free, quarters=range(4)):
            lo = ring_r[slot_of(part, name)][:, :].rearrange("p (k n) -> p k n", n=512)
            b0 = 2 * (proj_count[0] % 2)
            proj_count[0] += 3 in quarters
            pe.wait_ge(*V[st].at("tok_lo1"))
            for half in sorted({q // 2 for q in quarters}):
                pe.wait_ge(*G[st].at(f"{name}_lo{2 * half + 1}"))
                c = slice(half * 256, (half + 1) * 256)
                for t in range(NT):
                    if half == 0:
                        for wait in free(t):
                            pe.wait_ge(*wait)
                    ts = slice(t * P, (t + 1) * P)
                    for k in range(KC):
                        mm = three(bank(b0 + t)[:, c], (tok[0][:, k, ts], tok[1][:, k, ts]),
                                   (w_hi[:, k, c], lo[:, k, c]), k == 0, k == KC - 1)
                    mm.then_inc(*E[st].step())
                    if half == 1:
                        E[st].name(f"{name}_{t}")
                for q in (2 * half, 2 * half + 1):
                    E[st].name(f"{name}_q{q}")
            return b0

        class ProjectionFill:

            def __init__(self, proj, name):
                self.proj, self.name, self.done = proj, name, 0

            def fill(self, n):
                for _ in range(n):
                    if self.done < 4:
                        self.proj(self.name, (self.done,))
                        self.done += 1

        class OutProjection:

            def __init__(self, pe, st, part, tag, src, early, waits):
                self.pe, self.st, self.part, self.tag, self.early, self.done = pe, st, part, tag, early, 0
                self.src = src.rearrange("p (k t) -> p k t", t=T)
                self.waits = waits

            def block(self, b, chunks, first):
                wt, _, _ = piece(self.part, f"{self.tag}_{b // 4}")
                w = wt.rearrange("p (k n) -> p k n", n=512)
                for k in chunks:
                    mm = nc.tensor.matmul(bank(b // 2)[:, (b % 2) * T:(b % 2 + 1) * T],
                                          w[:, k, (b % 4) * P:(b % 4 + 1) * P], self.src[:, k, :],
                                          start=(first and k == chunks[0] and b % 2 == 0),
                                          stop=(not first and k == chunks[-1]), skip_group_check=True)
                return mm

            def fill(self, n):
                for _ in range(n):
                    if self.done == 8:
                        return
                    if self.done == 0:
                        for w in self.waits:
                            self.pe.wait_ge(*w)
                    if self.done % 4 == 0:
                        _, landed_sem, value = piece(self.part, f"{self.tag}_{self.done // 4}")
                        self.pe.wait_ge(landed_sem, value)
                    self.block(self.done, self.early, True)
                    self.done += 1

            def finish(self, ready):
                self.fill(8)
                self.pe.wait_ge(*ready)
                late = [k for k in range(KC) if k not in self.early]
                for b in range(8):
                    mm = self.block(b, late, False)
                    if b % 2:
                        mm.then_inc(*E[self.st].step())
                        E[self.st].name(f"{self.tag}_{b // 4}_{b % 4 // 2}")
                proj_count[0] += 2

        PROJ1 = ["q", "k", "v", "a_h", "a_c", "a_b", "z", "out1_0", "out1_1"]
        PROJ2 = ["bqk", "bv", "aq", "ak", "bg", "av", "ag", "out2_0", "out2_1"]
        PROJ3 = [f"h{w}{half}" for half in range(2) for w in "fqig"] + ["out3_0", "out3_1"]

        def free_by(st, names, name, marks):
            n = names.index(name)
            return (lambda half: []) if n < 2 else (lambda half: marks(names[n - 2], half))

        m1_convin = carve(0, 12 * 260).rearrange("p (b t) -> p b t", t=260)
        m1_conv = carve(3120, 3 * HC)
        m1_ycat = carve(3120 + 3 * HC, KC * T)
        m1_sz = carve(3120 + 3 * HC + 2048, HC)
        base = 3120 + 3 * HC + 3072
        m1_ahx = carve(base, 4 * 260).rearrange("p (b t) -> p b t", t=260)
        m1_ab = carve(base + 1040, HC)
        m1_ac = carve(base + 2064, HC)
        base += 3088
        m1_mt = [carve(base, HC), carve(base + HC, HC)]
        m1_sq = m1_mt
        base += 2 * HC
        m1_AT = carve(base, HC)
        m1_vb, m1_kbg, m1_kd = (carve(base + HC * (1 + n), HC) for n in range(3))
        base += 4 * HC
        m1_S = [carve(base, 512), carve(base + 512, 512)]
        base += 1024
        m1_g = carve(base, 128)
        base += 128
        m1_expG, m1_kb, m1_DT = (carve(HC * n, HC) for n in range(3))
        m1_LT = m1_kb
        m1_X, m1_Y, m1_U = (carve(3120 + 3 * HC + 3072 + HC * n, HC) for n in range(3))
        m1_kd2 = m1_expG
        m1_u, m1_wT = m1_mt
        m1_q, m1_k, m1_v = (m1_conv[:, n * HC:(n + 1) * HC] for n in range(3))
        gcol = {n: m1_g[:, 8 * i:8 * i + 8] for i, n in enumerate(
            ("beta", "g", "gc", "gl", "t0", "t1", "t2", "t3", "egc", "kdec0", "kdec1", "bg"))}

        def ht(ap):
            return ap.rearrange("p (h t) -> p h t", t=NT)

        def mixer1_tensor(pe):
            st = "mix1"
            e, s, v = E[st], S[st], V[st]
            pe.wait_ge(*v.at("ready"))
            norm_tensor(pe, st, "n")
            pe.wait_ge(*v.at("h"))
            pe.wait_ge(loaded_small, 16)
            tail = param("tail1", 64).rearrange("p (k n) -> p k n", n=8)
            for t in range(NT):
                for k in range(KC):
                    mm = nc.tensor.matmul(bank(6)[:, t * 8:t * 8 + 8], hT[:, k, t * P:(t + 1) * P], tail[:, k, :],
                                          start=(k == 0), stop=(k == KC - 1))
            mm.then_inc(*e.step())
            e.name("tail")

            def proj(name, quarters=range(4)):
                project(pe, st, "one", name, free_by(st, PROJ1, name, lambda n, half: [s.at(f"{n}_{half}")]),
                        quarters)

            for name in "qk":
                proj(name)
            pe.wait_ge(loaded_consts, 16)
            pe.wait_ge(*v.at("g"))
            gv = ht(gcol["g"])
            nc.tensor.matmul(bank(6)[:, 16:24], causal, gcol["g"], start=True, stop=True)
            nc.tensor.matmul(bank(6)[:, 24:32], group_ones, gcol["g"], start=True, stop=True).then_inc(*e.step())
            e.name("gc")
            for h in range(H4):
                for t in range(NT):
                    mm = nc.tensor.matmul(inst(bank(4, 2), h, t), gv[:, h, t:t + 1].to_broadcast([P, P]), causal,
                                          start=True, stop=True)
            mm.then_inc(*e.step())
            e.name("grow")
            for name in ("v", "a_h", "a_c"):
                proj(name)
            pe.wait_ge(*s.at("expG"))
            pe.wait_ge(*v.at("DT_raw"))
            for n, w in enumerate("qk"):
                pe.wait_ge(*s.at(f"{w}_sq"))
                for half in range(2):
                    mm = nc.tensor.matmul(bank(4 + 2 * n + half), ones[:, :], m1_sq[n][:, half * 512:(half + 1) * 512],
                                          start=True, stop=True)
                mm.then_inc(*e.step())
                e.name(f"{w}_sum")
            proj("a_b", (0, 1))
            bv = ht(gcol["beta"])
            pe.wait_ge(*s.at("q_rstd"))
            for h in range(H4):
                for t in range(NT):
                    mm = nc.tensor.matmul(inst(bank(4, 2), h, t), bv[:, h, t:t + 1].to_broadcast([P, P]), eye,
                                          start=True, stop=True)
            mm.then_inc(*e.step())
            e.name("brow")
            proj("a_b", (2, 3))
            pe.wait_ge(*v.at("kb"))
            for h in range(H4):
                for t in range(NT):
                    mm = nc.tensor.matmul(inst(bank(6, 2), h, t), inst(m1_k, h, t), inst(m1_kb, h, t),
                                          start=True, stop=True)
            mm.then_inc(*e.step())
            e.name("LT")
            for h in range(H4):
                for t in range(NT):
                    mm = nc.tensor.matmul(inst(bank(4, 2), h, t), inst(m1_k, h, t), inst(m1_q, h, t),
                                          start=True, stop=True)
            mm.then_inc(*e.step())
            e.name("AT")
            proj("z", (0, 1))
            pe.wait_ge(*s.at("ya_sq"))
            for half in range(2):
                mm = nc.tensor.matmul(bank(2 + half), group_ones, m1_sq[0][:, half * 512:(half + 1) * 512],
                                      start=True, stop=True)
            mm.then_inc(*e.step())
            e.name("ya_sum")
            proj("z", (2, 3))
            pe.wait_ge(*s.at("z_1"))
            pe.wait_ge(*s.at("ya_ln"))
            for h in range(H4):
                for t in range(NT):
                    mm = nc.tensor.transpose(inst(bank(0, 2), h, t), inst(m1_k, h, t), eye)
            mm.then_inc(*e.step())
            e.name("krow")
            for h in range(H4):
                for t in range(NT):
                    mm = nc.tensor.transpose(inst(bank(2, 2), h, t), inst(m1_v, h, t), eye)
            mm.then_inc(*e.step())
            e.name("vrow")
            pe.wait_ge(*v.at("Y0"))
            pe.wait_ge(*v.at("AT"))
            for h in range(H4):
                for t in range(NT):
                    mm = nc.tensor.transpose(inst(bank(4, 2), h, t), inst(m1_Y, h, t), eye)
            mm.then_inc(*e.step())
            e.name("X0")
            pe.wait_ge(*s.at("X0"))
            for n in range(1, len(LEVELS)):
                mt = m1_mt[n % 2]
                pe.wait_ge(*G[st].at(f"MT{n}"))
                if n > 1:
                    pe.wait_ge(*v.at(f"Y{n - 1}"))
                for half in range(2):
                    for j in range(4):
                        c = half * 512 + j * P
                        mm = nc.tensor.matmul(bank(4, 2)[:, c:c + P], mt[:, c:c + P], m1_X[:, c:c + P],
                                              start=True, stop=True)
                    mm.then_inc(*e.step())
                    e.name(f"U{n}_{half}")
                last = n == len(LEVELS) - 1
                if n == 1:
                    pe.wait_ge(*v.at("kvrows"))
                    pe.wait_ge(*v.at("AT"))
                for half in range(2):
                    pe.wait_ge(*s.at(f"U{n}_{half}"))
                    for j in range(4):
                        c = half * 512 + j * P
                        if not last:
                            nc.tensor.matmul(bank(6, 2)[:, c:c + P], m1_Y[:, c:c + P], m1_U[:, c:c + P],
                                             start=True, stop=True)
                        mm = nc.tensor.matmul(bank(0, 2)[:, c:c + P], m1_U[:, c:c + P], m1_Y[:, c:c + P],
                                              start=True, stop=True)
                    mm.then_inc(*e.step())
                    e.name(f"Z{n}_{half}")
            pe.wait_ge(*v.at(f"Y{len(LEVELS) - 1}"))
            for h in range(H4):
                for t in range(NT):
                    mm = nc.tensor.matmul(inst(bank(2, 2), h, t), inst(m1_Y, h, t), inst(m1_vb, h, t),
                                          start=True, stop=True)
            mm.then_inc(*e.step())
            e.name("u")
            for h in range(H4):
                for t in range(NT):
                    mm = nc.tensor.matmul(inst(bank(0, 2), h, t), inst(m1_kbg, h, t), inst(m1_Y, h, t),
                                          start=True, stop=True)
            mm.then_inc(*e.step())
            e.name("wT")
            pe.wait_ge(*s.at("wT"))
            pe.wait_ge(*v.at("u"))
            pe.wait_ge(*v.at("qd"))
            out = OutProjection(pe, st, "one", "out1", m1_ycat, range(4), [v.at("ya_out")])
            for c in range(NCH):
                t, off = c // 2, (c % 2) * CH
                if c:
                    pe.wait_ge(*v.at(f"S{c - 1}"))
                    for h in range(H4):
                        mm = nc.tensor.matmul(bank(4)[:, h * P:(h + 1) * P], inst(m1_wT, h, t),
                                              m1_S[(c - 1) % 2][:, h * P:(h + 1) * P], start=True, stop=True)
                    mm.then_inc(*e.step())
                    e.name(f"vp{c}")
                    out.fill(1)
                    pe.wait_ge(*v.at(f"vn{c}"))
                if c < NCH - 1:
                    kd = (m1_kd, m1_kd2)[c % 2]
                    for h in range(H4):
                        mm = nc.tensor.matmul(bank(5)[:, h * P:(h + 1) * P], inst(kd, h, t), inst(m1_u, h, t),
                                              start=True, stop=True)
                    mm.then_inc(*e.step())
                    e.name(f"Sp{c}")
                for h in range(H4):
                    o = bank(6, 2)[:, h * T + c * CH:h * T + (c + 1) * CH]
                    if c:
                        nc.tensor.matmul(o, m1_S[(c - 1) % 2][:, h * P:(h + 1) * P],
                                         m1_q[:, h * T + c * CH:h * T + (c + 1) * CH], start=True, stop=False)
                    mm = nc.tensor.matmul(o, inst(m1_u, h, t), inst(m1_AT, h, t)[:, off:off + CH],
                                          start=(c == 0), stop=True)
                mm.then_inc(*e.step())
                e.name(f"o{c}")
            out.fill(2)
            pe.wait_ge(*s.at("o_sq"))
            for half in range(2):
                mm = nc.tensor.matmul(bank(4 + half), ones[:, :], m1_sq[1][:, half * 512:(half + 1) * 512],
                                      start=True, stop=True)
            mm.then_inc(*e.step())
            e.name("o_sum")
            out.finish(v.at("y"))

        def mixer1_scalar(act):
            st = "mix1"
            e, s, v = E[st], S[st], V[st]
            act.preload_act_table_set(EXP_LN)
            act.wait_ge(loaded_x, 16)
            act.wait_ge(loaded_small, 16)
            act.wait_ge(*v.at("ready"))
            norm_scalar(act, st, "n", [])
            weights_hi_of(act, st, "one", "q", range(4))
            tokens_hi(act, st)
            act.wait_ge(*v.at("logits"))
            nc.scalar.activation(gcol["t0"], gcol["beta"], ACT.Exp, scale=-1.0).then_inc(*s.step())
            nc.scalar.activation(gcol["t2"], gcol["t1"], ACT.Exp).then_inc(*s.step())
            act.wait_ge(*s.last())
            nc.scalar.activation(gcol["t2"], gcol["t2"], ACT.Ln, bias=1.0).then_inc(*s.step())
            nc.scalar.activation(m1_g[:, 96:100], param("a_log", 4), ACT.Exp).then_inc(*s.step())
            s.name("gates")

            def keep(name, out, func=ACT.Copy, rounded=0):
                b0 = 2 * (PROJ1.index(name) % 2)
                for half in range(2):
                    if half >= rounded:
                        round_next(act, st, "one", PROJ1, name, half)
                    act.wait_ge(*e.at(f"{name}_{half}"))
                    nc.scalar.activation(out(half), bank(b0 + half).rearrange("p (b t) -> p b t", t=T),
                                         func).then_inc(*s.step())
                    s.name(f"{name}_{half}")

            def two(ap, half):
                return ap[:, half * 512:(half + 1) * 512].rearrange("p (b t) -> p b t", t=T)

            act.wait_ge(*v.at("pads"))
            for n, w in enumerate("qkv"):
                keep(w, lambda half: m1_convin[:, 4 * n + 2 * half:4 * n + 2 * half + 2, 3:3 + T])
            round_next(act, st, "one", PROJ1, "a_h", 0)
            act.wait_ge(*v.at("conv2"))
            act.wait_ge(*e.at("grow"))
            nc.scalar.activation(m1_expG, bank(4, 2), ACT.Exp).then_inc(*s.step())
            s.name("expG")
            for n, w in enumerate("qkv"):
                nc.scalar.activation(m1_conv[:, n * HC:(n + 1) * HC], m1_conv[:, n * HC:(n + 1) * HC],
                                     ACT.Silu).then_inc(*s.step())
                s.name(f"silu_{w}")
            keep("a_h", lambda half: m1_ahx[:, 2 * half:2 * half + 2, 2:2 + T], rounded=1)
            act.preload_act_table_set(EXP_LN)
            for n, w in enumerate("qk"):
                act.wait_ge(*s.at(f"silu_{w}"))
                nc.scalar.activation(m1_sq[n], m1_conv[:, n * HC:(n + 1) * HC], ACT.Square).then_inc(*s.step())
                s.name(f"{w}_sq")
            act.wait_ge(*v.at("gdiff"))
            nc.scalar.activation(m1_g[:, 64:80], m1_g[:, 64:80], ACT.Exp).then_inc(*s.step())
            s.name("gexp")
            act.wait_ge(*v.at("DT_raw"))
            nc.scalar.activation(m1_DT, m1_DT, ACT.Exp).then_inc(*s.step())
            s.name("DT")
            keep("a_c", lambda half: two(m1_ac, half))
            for n, (w, out) in enumerate((("q", m1_AT), ("k", m1_vb))):
                act.wait_ge(*e.at(f"{w}_sum"))
                nc.scalar.activation(out, bank(4 + 2 * n, 2), ACT.Ln, bias=eps_col).then_inc(*s.step())
                act.wait_ge(*s.last())
                nc.scalar.activation(out, out, ACT.Exp, scale=-0.5).then_inc(*s.step())
                s.name(f"{w}_rstd")
            keep("a_b", lambda half: two(m1_ab, half))
            act.wait_ge(*v.at("ya"))
            nc.scalar.activation(m1_sq[0], m1_ycat[:, 0:HC], ACT.Square).then_inc(*s.step())
            s.name("ya_sq")
            act.wait_ge(*e.at("ya_sum"))
            nc.scalar.activation(m1_ac, bank(2, 2), ACT.Ln, bias=eps_col, scale=1.0 / CH).then_inc(*s.step())
            s.name("ya_ln")
            act.wait_ge(*s.last())
            nc.scalar.activation(m1_ac, m1_ac, ACT.Exp, scale=-0.5).then_inc(*s.step())
            s.name("ya_rstd")
            keep("z", lambda half: two(m1_sz, half), ACT.Silu)
            act.preload_act_table_set(EXP_LN)
            act.wait_ge(*e.at("X0"))
            nc.scalar.activation(m1_X, bank(4, 2), ACT.Copy).then_inc(*s.step())
            s.name("X0")
            for n in range(1, len(LEVELS)):
                for half in range(2):
                    act.wait_ge(*e.at(f"U{n}_{half}"))
                    if n > 1:
                        act.wait_ge(*e.at(f"Z{n - 1}_{half}"))
                    nc.scalar.activation(m1_U[:, half * 512:(half + 1) * 512], bank(4 + half), ACT.Copy)\
                        .then_inc(*s.step())
                    s.name(f"U{n}_{half}")
            act.wait_ge(*e.at("wT"))
            nc.scalar.activation(m1_wT, bank(0, 2), ACT.Copy).then_inc(*s.step())
            s.name("wT")
            act.wait_ge(*e.at(f"o{NCH - 1}"))
            nc.scalar.activation(m1_sq[1], bank(6, 2), ACT.Square).then_inc(*s.step())
            s.name("o_sq")
            act.wait_ge(*e.at("o_sum"))
            nc.scalar.activation(m1_X, bank(4, 2), ACT.Ln, bias=eps_col, scale=1.0 / P).then_inc(*s.step())
            act.wait_ge(*s.last())
            nc.scalar.activation(m1_X, m1_X, ACT.Exp, scale=-0.5).then_inc(*s.step())
            s.name("o_rstd")

        def mixer1_pool(pool):
            st = "mix1"
            g, v = G[st], V[st]
            pool.wait_ge(loaded_consts, 16)
            for name in PROJ1[:-2]:
                weights_lo_of(pool, st, "one", name)
            for n in range(1, len(LEVELS)):
                if n == 1:
                    pool.wait_ge(*v.at("Y0"))
                else:
                    if n > 2:
                        pool.wait_ge(*E[st].at(f"U{n - 2}_1"))
                m = level_mask(len(LEVELS) - 1 - n)
                nc.gpsimd.tensor_tensor(blocks(m1_mt[n % 2]), blocks(m1_LT), spread(m), ALU.mult)\
                    .then_inc(*g.step())
                g.name(f"MT{n}")

        def mixer1_vector(dve):
            st = "mix1"
            e, s, v = E[st], S[st], V[st]
            nc.vector.memset(ones[:, :], 1.0).then_inc(*v.step())
            nc.vector.memset(eps_col, EPS).then_inc(*v.step())
            v.name("ready")
            dve.wait_ge(loaded_small, 16)
            norm_vector(dve, st, "n", param("mix_g", 8), hT, "h")
            tokens_lo(dve, st)
            dve.wait_ge(*v.last())
            dve.wait_ge(loaded_consts, 16)
            nc.vector.memset(m1_convin[:, :, 0:3], 0.0).then_inc(*v.step())
            nc.vector.memset(m1_ahx[:, :, 0:2], 0.0).then_inc(*v.step())
            v.name("pads")
            dve.wait_ge(*e.at("tail"))
            lg = bank(6)[:, 0:16].rearrange("p (t n) -> p n t", n=8)
            nc.vector.tensor_copy(ht(gcol["beta"]), lg[:, 0:4, :]).then_inc(*v.step())
            nc.vector.tensor_tensor(ht(gcol["t3"]), lg[:, 4:8, :],
                                    param("dt_bias", 4).unsqueeze(2).to_broadcast([P, H4, NT]), ALU.add)\
                .then_inc(*v.step())
            dve.wait_ge(*v.last())
            nc.vector.scalar_tensor_tensor(gcol["t1"], gcol["t3"], -1.0, gcol["t3"], ALU.mult, ALU.min)\
                .then_inc(*v.step())
            v.name("logits")
            dve.wait_ge(*s.at("gates"))
            nc.vector.tensor_scalar(gcol["t0"], gcol["t0"], 1e37, 1.0, ALU.min, ALU.add).then_inc(*v.step())
            nc.vector.scalar_tensor_tensor(gcol["t3"], gcol["t3"], 0.0, gcol["t2"], ALU.max, ALU.add)\
                .then_inc(*v.step())
            dve.wait_ge(*v.last())
            nc.vector.reciprocal(gcol["beta"], gcol["t0"]).then_inc(*v.step())
            nc.vector.scalar_tensor_tensor(ht(gcol["g"]), ht(gcol["t3"]), -1.0,
                                           m1_g[:, 96:100].unsqueeze(2).to_broadcast([P, H4, NT]),
                                           ALU.mult, ALU.mult).then_inc(*v.step())
            v.name("g")
            for n, w in enumerate("qkv"):
                for half in range(2):
                    dve.wait_ge(*s.at(f"{w}_{half}"))
                for tap in range(4):
                    for b in range(4):
                        blk = 4 * n + b
                        out = m1_conv[:, blk * T:(blk + 1) * T]
                        wt = param("dn_conv", 1, tap * 12 + blk)
                        if tap == 0:
                            nc.vector.tensor_scalar(out, m1_convin[:, blk, 0:T], wt, None, ALU.mult)\
                                .then_inc(*v.step())
                        else:
                            dve.wait_ge(*v.last(3))
                            nc.vector.scalar_tensor_tensor(out, m1_convin[:, blk, tap:tap + T], wt, out,
                                                           ALU.mult, ALU.add).then_inc(*v.step())
                v.name(f"conv{n}")
                if n == 0:
                    dve.wait_ge(*e.at("gc"))
                    nc.vector.tensor_copy(m1_g[:, 16:32], bank(6)[:, 16:32]).then_inc(*v.step())
                    v.name("gcols")
            nc.vector.tensor_copy(gcol["egc"], gcol["gc"]).then_inc(*v.step())
            nc.vector.tensor_tensor(gcol["kdec0"], gcol["gl"], gcol["gc"], ALU.subtract).then_inc(*v.step())
            v.name("gdiff")
            dve.wait_ge(*s.at("expG"))
            dve.wait_ge(*v.last())
            for h in range(H4):
                for t in range(NT):
                    nc.vector.tensor_scalar(inst(m1_DT, h, t), inst(bank(4, 2), h, t), ht(gcol["gc"])[:, h, t:t + 1],
                                            0.0, ALU.subtract, ALU.min).then_inc(*v.step())
            v.name("DT_raw")
            dve.wait_ge(*s.at("gexp"))
            nc.vector.tensor_tensor(gcol["bg"], gcol["beta"], gcol["egc"], ALU.mult).then_inc(*v.step())
            nc.vector.tensor_scalar(gcol["kdec1"], gcol["kdec0"], consts[:, C_HALF + 1:C_HALF + 2], None, ALU.mult)\
                .then_inc(*v.step())
            dve.wait_ge(*v.last())
            nc.vector.tensor_scalar(gcol["kdec0"], gcol["kdec0"], consts[:, C_HALF:C_HALF + 1], None, ALU.mult)\
                .then_inc(*v.step())
            dve.wait_ge(*s.at("DT"))
            nc.vector.tensor_tensor(blocks(m1_DT), blocks(m1_DT), spread(causal), ALU.mult).then_inc(*v.step())
            dve.wait_ge(*s.at("q_rstd"))
            nc.vector.scalar_tensor_tensor(m1_q, m1_q, float(P) ** -0.5, m1_AT, ALU.mult, ALU.mult)\
                .then_inc(*v.step())
            dve.wait_ge(*s.at("k_rstd"))
            nc.vector.tensor_tensor(m1_k, m1_k, m1_vb, ALU.mult).then_inc(*v.step())
            dve.wait_ge(*v.last())
            dve.wait_ge(*e.at("brow"))
            nc.vector.tensor_tensor(m1_kb, m1_k, bank(4, 2), ALU.mult).then_inc(*v.step())
            v.name("kb")
            for half in range(2):
                dve.wait_ge(*s.at(f"a_c_{half}"))
                u = m1_ahx[:, 2 * half:2 * half + 2, 2:2 + T]
                nc.vector.tensor_tensor(u, u, m1_ac[:, half * 512:(half + 1) * 512].rearrange("p (b t) -> p b t", t=T),
                                        ALU.mult).then_inc(*v.step())
            dve.wait_ge(*v.last())
            y = m1_ycat[:, 0:HC].rearrange("p (b t) -> p b t", t=T)
            for tap in range(3):
                for b in range(4):
                    w = param("conv_a", 1, tap * 4 + b)
                    if tap == 0:
                        nc.vector.tensor_scalar(y[:, b, :], m1_ahx[:, b, 0:T], w, None, ALU.mult).then_inc(*v.step())
                    else:
                        dve.wait_ge(*v.last(3))
                        nc.vector.scalar_tensor_tensor(y[:, b, :], m1_ahx[:, b, tap:tap + T], w, y[:, b, :],
                                                       ALU.mult, ALU.add).then_inc(*v.step())
            dve.wait_ge(*v.last())
            dve.wait_ge(*s.at("a_b_1"))
            nc.vector.tensor_tensor(m1_ycat[:, 0:HC], m1_ycat[:, 0:HC], m1_ab, ALU.mult).then_inc(*v.step())
            v.name("ya")
            dve.wait_ge(*e.at("LT"))
            nc.vector.tensor_tensor(m1_LT, bank(6, 2), m1_DT, ALU.mult).then_inc(*v.step())
            dve.wait_ge(*e.at("AT"))
            nc.vector.tensor_tensor(m1_AT, bank(4, 2), m1_DT, ALU.mult).then_inc(*v.step())
            v.name("AT")
            dve.wait_ge(*v.last())
            nc.vector.tensor_tensor(m1_q, m1_q, m1_expG, ALU.mult).then_inc(*v.step())
            v.name("qd")
            dve.wait_ge(*s.at("ya_rstd"))
            for b in range(4):
                nc.vector.scalar_tensor_tensor(y[:, b, :], y[:, b, :], param("conv_a_g", 1, b),
                                               m1_ac[:, b * T:(b + 1) * T], ALU.mult, ALU.mult).then_inc(*v.step())
            v.name("ya_out")
            dve.wait_ge(*v.last())
            nc.vector.tensor_tensor(blocks(m1_Y), blocks(m1_LT), spread(level_mask(len(LEVELS) - 1)), ALU.mult)\
                .then_inc(*v.step())
            dve.wait_ge(*v.last())
            nc.vector.scalar_tensor_tensor(blocks(m1_Y), blocks(m1_Y), -1.0, spread(eye), ALU.mult, ALU.add)\
                .then_inc(*v.step())
            v.name("Y0")

            def by_token(out, in_, col):
                nc.vector.tensor_tensor(blocks(out), blocks(in_), gcol[col].unsqueeze(2).to_broadcast([P, 8, P]),
                                        ALU.mult).then_inc(*v.step())

            dve.wait_ge(*v.last())
            dve.wait_ge(*e.at("krow"))
            by_token(m1_kbg, bank(0, 2), "bg")
            by_token(m1_kd, bank(0, 2), "kdec0")
            for h in range(H4):
                nc.vector.tensor_copy(m1_g[:, 100 + 4 * h:104 + 4 * h], m1_expG[:, h * T + CH - 1:(h + 1) * T:CH])\
                    .then_inc(*v.step())
            dve.wait_ge(*v.last())
            by_token(m1_kd2, bank(0, 2), "kdec1")
            dve.wait_ge(*e.at("vrow"))
            by_token(m1_vb, bank(2, 2), "beta")
            v.name("kvrows")
            for n in range(1, len(LEVELS)):
                last = n == len(LEVELS) - 1
                for half in range(2):
                    dve.wait_ge(*e.at(f"Z{n}_{half}"))
                    c = slice(half * 512, (half + 1) * 512)
                    if not last:
                        nc.vector.tensor_tensor(m1_X[:, c], m1_X[:, c], bank(6 + half), ALU.subtract)\
                            .then_inc(*v.step())
                    nc.vector.tensor_tensor(m1_Y[:, c], m1_Y[:, c], bank(half), ALU.subtract).then_inc(*v.step())
                v.name(f"Y{n}")
            dve.wait_ge(*e.at("u"))
            nc.vector.tensor_copy(m1_u, bank(2, 2)).then_inc(*v.step())
            v.name("u")
            dve.wait_ge(*v.last())
            for c in range(NCH):
                t, off = c // 2, (c % 2) * CH
                if c:
                    dve.wait_ge(*e.at(f"vp{c}"))
                    u = per_head(m1_u)[off:off + CH, :, t * P:(t + 1) * P]
                    nc.vector.tensor_tensor(u, u, bank(4)[off:off + CH, :].rearrange("p (h n) -> p h n", n=P),
                                            ALU.subtract).then_inc(*v.step())
                    v.name(f"vn{c}")
                if c < NCH - 1:
                    dve.wait_ge(*e.at(f"Sp{c}"))
                    if c > 1:
                        dve.wait_ge(*e.at(f"o{c - 1}"))
                    for h in range(H4):
                        hs = slice(h * P, (h + 1) * P)
                        if c == 0:
                            nc.vector.tensor_copy(m1_S[0][:, hs], bank(5)[:, hs]).then_inc(*v.step())
                        else:
                            nc.vector.scalar_tensor_tensor(m1_S[c % 2][:, hs], m1_S[(c - 1) % 2][:, hs],
                                                           m1_g[:, 100 + 4 * h + c:101 + 4 * h + c], bank(5)[:, hs],
                                                           ALU.mult, ALU.add).then_inc(*v.step())
                    v.name(f"S{c}")
                    dve.wait_ge(*v.last())
            dve.wait_ge(*s.at("o_rstd"))
            yb = m1_ycat[:, HC:2 * HC]
            nc.vector.scalar_tensor_tensor(yb, bank(6, 2), param("dn_g"), m1_X, ALU.mult, ALU.mult).then_inc(*v.step())
            dve.wait_ge(*v.last())
            nc.vector.tensor_tensor(yb, yb, m1_sz, ALU.mult).then_inc(*v.step())
            v.name("y")
            add_residual(dve, st, "out1")

        def add_residual(dve, st, tag):
            for b in range(4):
                dve.wait_ge(*E[st].at(f"{tag}_{b // 2}_{b % 2}"))
                x = xT[:, 2 * b:2 * b + 2, :]
                nc.vector.tensor_tensor(x, x, bank(b).rearrange("p (b t) -> p b t", t=T), ALU.add)\
                    .then_inc(*V[st].step())
                if b == 1:
                    V[st].name(f"x_{tag}_first")
            V[st].name(f"x_{tag}")

        r_hrow = carve(2400, NT * D)
        r_base = 2400 + NT * D
        o_Xg, o_silu, o_hid, o_hidT, o_y = (r_base, r_base + 1024, r_base + 1536, r_base + 2048, r_base + 2560)
        x_Xg, x_silu, x_hid, x_hidT, x_y = (carve(o_Xg, 1024), carve(o_silu, 512), carve(o_hid, 512),
                                            carve(o_hidT, 512), carve(o_y, 1024))
        r_base += 3584
        x_pick, x_share, x_shareT = (carve(r_base + 256 * n, 256) for n in range(3))
        r_base += 768
        r_slot, r_gate = (carve(r_base + 280 * n, 280) for n in range(2))
        r_base += 560
        r_work = carve(r_base, 1024)

        HALF = PIECE // 2

        class Moe:

            def __init__(self, name, st, part, per, slots, experts, units, groups, gain, router, cell):
                self.name, self.st, self.part, self.per, self.slots = name, st, part, per, slots
                self.experts, self.units, self.groups, self.gain, self.router = experts, units, groups, gain, router
                self.n_router = experts + groups
                self.iters, self.passes = experts // per, T // slots
                self.width = experts * self.passes + 2 * per
                self.cell = trips[0:1, cell:cell + 1]
                self.sem = moe_sems[name]
                self.slot = r_slot[:, 0:NT * self.width].rearrange("p (t c) -> p t c", t=NT)
                self.gate = r_gate[:, 0:NT * self.width].rearrange("p (t c) -> p t c", t=NT)

            def trip_count(self, eng):
                return eng.value_load(self.cell, min_val=self.iters, max_val=self.iters * self.passes)

            def banks(self, u):
                return (0, 1) if u % 2 == 0 else (4, 5)

        M1 = Moe("moe1", "route1", "moe1", 2, C1, NE1, 1, 4, param("ffn_g", 8), param("router1", 288), 0)
        M2 = Moe("moe2", "route2", "moe2", 1, C2, NE2, UNITS, 0, param("ffn2_g", 8, 8), param("router2", 64), 1)

        def route_tensor(pe, m):
            st = m.st
            e, s, v = E[st], S[st], V[st]
            norm_tensor(pe, st, "n")
            pe.wait_ge(*v.at("h"))
            w = m.router.rearrange("p (k n) -> p k n", k=KC)
            for t in range(NT):
                for k in range(KC):
                    mm = nc.tensor.matmul(bank(6)[:, t * 64:t * 64 + m.n_router], hT[:, k, t * P:(t + 1) * P],
                                          w[:, k, :], start=(k == 0), stop=(k == KC - 1))
            mm.then_inc(*e.step())
            e.name("logits")
            for t in range(NT):
                for half in range(2):
                    for j in range(4):
                        mm = nc.tensor.transpose(bank(2 * t + half)[:, j * P:(j + 1) * P],
                                                 hT[:, 4 * half + j, t * P:(t + 1) * P], eye)
                    mm.then_inc(*e.step())
                    e.name(f"hrow{t}{half}")
            pe.wait_ge(*v.at("chosen"))
            n = m.experts
            A0, A1 = (r_work[:, 64 * t:64 * t + n] for t in range(NT))
            nc.tensor.matmul(bank(7)[:, 0:n], before, A0, start=True, stop=True)
            nc.tensor.matmul(bank(7)[:, 64:64 + n], ones[:, :], A0, start=True, stop=False)
            nc.tensor.matmul(bank(7)[:, 64:64 + n], before, A1, start=False, stop=True)
            nc.tensor.matmul(bank(7)[:, 128:128 + n], ones[:, :], A0, start=True, stop=False)
            nc.tensor.matmul(bank(7)[:, 128:128 + n], ones[:, :], A1, start=False, stop=True).then_inc(*e.step())
            e.name("counted")

        def route_scalar(act, m, waits):
            st = m.st
            e, s, v = E[st], S[st], V[st]
            act.preload_act_table_set(EXP_LN)
            norm_scalar(act, st, "n", waits)
            for t in range(NT):
                for half in range(2):
                    act.wait_ge(*e.at(f"hrow{t}{half}"))
                    nc.scalar.activation(r_hrow[:, t * D + half * 512:t * D + half * 512 + 512], bank(2 * t + half),
                                         ACT.Copy).then_inc(*s.step())
            s.name("hrow")
            w = r_work
            if m.groups:
                act.wait_ge(*v.at("gdiff"))
                nc.scalar.activation(w[:, 512:520], w[:, 512:520], ACT.Exp).then_inc(*s.step())
                s.name("gexp")
            act.wait_ge(*v.at("ediff"))
            nc.scalar.activation(w[:, 520:522], w[:, 520:522], ACT.Exp).then_inc(*s.step())
            s.name("eexp")

        def route_vector(dve, m):
            st = m.st
            e, s, v = E[st], S[st], V[st]
            w = r_work
            n, g = m.experts, m.groups
            norm_vector(dve, st, "n", m.gain, hT, "h")

            def pairs(at, k, stride=64):
                return w[:, at:at + NT * stride].rearrange("p (t c) -> p t c", t=NT)[:, :, 0:k]

            def do(ins):
                ins.then_inc(*v.step())
                dve.wait_ge(*v.last())

            def first_of_max(vals, top, cand, best, onehot, k):
                desc = consts[:, C_DESC:C_DESC + k].unsqueeze(1).to_broadcast([P, NT, k])
                do(nc.vector.reduce_max(top, vals, AX_X))
                do(nc.vector.tensor_tensor(cand, vals, top.unsqueeze(2).to_broadcast([P, NT, k]), ALU.is_equal))
                do(nc.vector.tensor_tensor(cand, cand, desc, ALU.mult))
                do(nc.vector.reduce_max(best, cand, AX_X))
                do(nc.vector.tensor_tensor(onehot, cand, best.unsqueeze(2).to_broadcast([P, NT, k]), ALU.is_equal))

            dve.wait_ge(*e.at("logits"))
            lg = w[:, 128:256].rearrange("p (t c) -> p t c", t=NT)
            do(nc.vector.tensor_copy(lg[:, :, 0:m.n_router],
                                     bank(6)[:, 0:128].rearrange("p (t c) -> p t c", t=NT)[:, :, 0:m.n_router]))
            ex = lg[:, :, g:g + n]
            top, best = w[:, 524:526], w[:, 526:528]
            cand = pairs(256, n)
            if g:
                oneg = pairs(384, g, 4)
                first_of_max(lg[:, :, 0:g], top, cand[:, :, 0:g], best, oneg, g)
                gd = w[:, 512:520].rearrange("p (t c) -> p t c", t=NT)
                nc.vector.tensor_tensor(gd, lg[:, :, 0:g], top.unsqueeze(2).to_broadcast([P, NT, g]), ALU.subtract)\
                    .then_inc(*v.step())
                v.name("gdiff")
                e4 = w[:, 128:256].rearrange("p (t c) -> p t c", t=NT)
                for t in range(NT):
                    lt = e4[:, t, g:g + n].rearrange("p (g c) -> p g c", g=g)
                    sel = oneg[:, t, :].unsqueeze(2).to_broadcast([P, g, n // g])
                    do(nc.vector.tensor_tensor(lt, lt, sel, ALU.mult))
                do(nc.vector.tensor_scalar(oneg, oneg, BIG, -BIG, ALU.mult, ALU.add))
                for t in range(NT):
                    lt = e4[:, t, g:g + n].rearrange("p (g c) -> p g c", g=g)
                    sel = oneg[:, t, :].unsqueeze(2).to_broadcast([P, g, n // g])
                    do(nc.vector.tensor_tensor(lt, lt, sel, ALU.add))
                dve.wait_ge(*s.at("gexp"))
                do(nc.vector.reduce_sum(w[:, 522:524], gd, AX_X))
                do(nc.vector.reciprocal(w[:, 522:524], w[:, 522:524]))
            one1, one2 = pairs(0, n), pairs(392, n, 40 if n <= 40 else 64)
            top2 = w[:, 528:530]
            first_of_max(ex, top, cand, best, one1, n)
            do(nc.vector.scalar_tensor_tensor(ex, one1, -4 * BIG, ex, ALU.mult, ALU.add))
            first_of_max(ex, top2, cand, best, one2, n)
            nc.vector.tensor_tensor(w[:, 520:522], top2, top, ALU.subtract).then_inc(*v.step())
            v.name("ediff")
            dve.wait_ge(*s.at("eexp"))
            do(nc.vector.tensor_scalar(w[:, 530:532], w[:, 520:522], 1.0, None, ALU.add))
            do(nc.vector.reciprocal(w[:, 530:532], w[:, 530:532]))
            if g:
                do(nc.vector.tensor_tensor(w[:, 530:532], w[:, 530:532], w[:, 522:524], ALU.mult))
            do(nc.vector.tensor_tensor(w[:, 532:534], w[:, 530:532], w[:, 520:522], ALU.mult))
            gt = pairs(256, n)
            do(nc.vector.memset(m.gate, 0.0))
            do(nc.vector.tensor_tensor(gt, one1, w[:, 530:532].unsqueeze(2).to_broadcast([P, NT, n]), ALU.mult))
            g2 = w[:, 600:600 + NT * n].rearrange("p (t c) -> p t c", t=NT)
            do(nc.vector.tensor_tensor(g2, one2, w[:, 532:534].unsqueeze(2).to_broadcast([P, NT, n]), ALU.mult))
            do(nc.vector.tensor_tensor(gt, gt, g2, ALU.add))
            for p in range(m.passes):
                do(nc.vector.tensor_copy(m.gate[:, :, m.per + p * n:m.per + (p + 1) * n], gt))
            do(nc.vector.tensor_tensor(one1, one1, one2, ALU.add))
            v.name("chosen")
            do(nc.vector.memset(m.slot, -1.0))
            dve.wait_ge(*e.at("counted"))
            for t in range(NT):
                do(nc.vector.scalar_tensor_tensor(w[:, 600 + t * n:600 + (t + 1) * n],
                                                  bank(7)[:, 64 * t:64 * t + n], 1.0, one1[:, t, :],
                                                  ALU.add, ALU.mult))
            for p in range(m.passes):
                do(nc.vector.tensor_scalar(m.slot[:, :, m.per + p * n:m.per + (p + 1) * n], g2,
                                           -1.0 - p * m.slots, None, ALU.add))
            do(nc.vector.reduce_max(w[:, 534:535], bank(7)[:, 128:128 + n], AX_X))
            for p in range(1, m.passes):
                do(nc.vector.tensor_scalar(w[:, 535 + p:536 + p], w[:, 534:535], float(p * m.slots), None, ALU.is_gt))
            do(nc.vector.reduce_sum(w[:, 540:541], w[:, 536:535 + m.passes], AX_X))
            nc.vector.tensor_scalar(m.cell, w[0:1, 540:541], 1.0, float(m.iters), ALU.add, ALU.mult)\
                .then_inc(*v.step())
            v.name("trips")
            dve.wait_ge(*v.last())

        def moe_tensor(pe, m):
            sem_, per, C = m.sem, m.per, m.slots
            s, v = S[m.st], V[m.st]

            def gather(i):
                pe.wait_ge(sem_["pick_ready"], i + 2)
                for r in range(2):
                    for k in range(4 * r, 4 * r + 4):
                        for t in range(NT):
                            mm = nc.tensor.matmul(bank(7 - r)[:, (k % 4) * P:(k % 4 + 1) * P],
                                                  r_hrow[:, t * D + k * P:t * D + (k + 1) * P],
                                                  x_pick[:, t * P:(t + 1) * P], start=(t == 0), stop=(t == NT - 1))
                    mm.then_inc(sem_["gathered"], 1)

            def weights(i, what, x):
                slot = "gud".index(what) * 2 + x
                pe.wait_ge(landed["moe1"][slot], 16 * (i + 1))
                return ring[:, slot, :]

            def gate_or_up(i, what, bank_):
                w = [weights(i, what, x).rearrange("p (k n) -> p k n", n=512) for x in range(per)]
                for k in range(KC):
                    for x in range(per):
                        mm = nc.tensor.matmul(bank(bank_)[x * C:(x + 1) * C, :],
                                              x_Xg[:, k * P + x * C:k * P + (x + 1) * C], w[x][:, k, :],
                                              start=(k == 0), stop=(k == KC - 1))
                mm.then_inc(sem_["gate_done" if what == "g" else "up_done"], 1)

            def gate_up(i):
                pe.wait_ge(sem_["gathered_kept"], i * 2 + 3)
                pe.wait_ge(sem_["silu_done"], i + 1)
                gate_or_up(i, "g", 0)
                pe.wait_ge(sem_["hidden_done"], i + 1)
                gate_or_up(i, "u", 1)

            def spread_back(i):
                pe.wait_ge(sem_["share_ready"], i + 2)
                pe.wait_ge(sem_["spread_added"], i * 4 + 1)
                for t in range(NT):
                    mm = nc.tensor.transpose(bank(4)[:, t * P:(t + 1) * P], x_share[:, t * P:(t + 1) * P], eye)
                mm.then_inc(sem_["shareT_done"], 1)
                pe.wait_ge(sem_["y_kept"], i + 1)
                pe.wait_ge(sem_["shareT_kept"], i + 2)
                for r in range(4):
                    if r >= 2:
                        pe.wait_ge(sem_["spread_added"], i * 4 + r)
                    for j in range(2):
                        k = 2 * r + j
                        mm = nc.tensor.matmul(bank(5 - r % 2)[:, j * T:(j + 1) * T], x_y[:, k * P:(k + 1) * P],
                                              x_shareT, start=True, stop=True)
                    mm.then_inc(sem_["spread_done"], 1)

            def down(i):
                pe.wait_ge(sem_["hidden_done"], i + 2)
                pe.wait_ge(sem_["gathered_kept"], i * 2 + 5)
                for f in range(4):
                    mm = nc.tensor.transpose(bank(6)[:, f * P:(f + 1) * P], x_hid[:, f * P:(f + 1) * P], eye)
                mm.then_inc(sem_["hiddenT_done"], 1)
                w = [weights(i, "d", x).rearrange("p (f n) -> p f n", n=D) for x in range(per)]
                pe.wait_ge(sem_["y_kept"], i + 1)
                pe.wait_ge(sem_["hiddenT_kept"], i + 2)
                for f in range(4):
                    for half in range(2):
                        for x in range(per):
                            mm = nc.tensor.matmul(bank(2 + half)[x * C:(x + 1) * C, :],
                                                  x_hidT[:, f * P + x * C:f * P + (x + 1) * C],
                                                  w[x][:, f, half * 512:(half + 1) * 512],
                                                  start=(f == 0), stop=(f == 3))
                mm.then_inc(sem_["down_done"], 1)

            for w in ("gate_done", "up_done", "shareT_done", "spread_done", "gathered", "hiddenT_done", "down_done"):
                pe.sem_inc(sem_[w], 1)
            pe.wait_ge(*v.at("trips"))
            n = m.trip_count(pe)
            pe.wait_ge(*s.at("hrow"))
            gather(0)
            pe.wait_ge(sem_["start"], 1)
            with pe.Fori(0, n) as i:
                gate_up(i)
                spread_back(i)
                pe.wait_ge(sem_["hiddenT_kept"], i + 1)
                gather(i + 1)
                down(i)
            spread_back(n)
            return n

        def moe_scalar(act, m):
            sem_ = m.sem
            v = V[m.st]

            def silu(i):
                act.wait_ge(sem_["gate_done"], i + 2)
                act.wait_ge(sem_["hidden_done"], i + 1)
                nc.scalar.activation(x_silu, bank(0), ACT.Silu).then_inc(sem_["silu_done"], 1)

            def keep_share(i):
                act.wait_ge(sem_["shareT_done"], i + 2)
                act.wait_ge(sem_["spread_done"], i * 4 + 1)
                nc.scalar.activation(x_shareT, bank(4)[:, 0:T], ACT.Copy).then_inc(sem_["shareT_kept"], 1)

            def keep_gathered(i):
                for r in range(2):
                    act.wait_ge(sem_["gathered"], i * 2 + 2 + r)
                    nc.scalar.activation(x_Xg[:, r * 512:(r + 1) * 512], bank(7 - r), ACT.Copy)\
                        .then_inc(sem_["gathered_kept"], 1)

            def keep_hidden(i):
                act.wait_ge(sem_["hiddenT_done"], i + 2)
                act.wait_ge(sem_["down_done"], i + 1)
                nc.scalar.activation(x_hidT, bank(6), ACT.Copy).then_inc(sem_["hiddenT_kept"], 1)

            for w in ("silu_done", "shareT_kept", "gathered_kept", "hiddenT_kept", "y_kept"):
                act.sem_inc(sem_[w], 1)
            act.wait_ge(*v.at("trips"))
            n = m.trip_count(act)
            keep_gathered(0)
            with act.Fori(0, n) as i:
                silu(i)
                keep_share(i)
                keep_gathered(i + 1)
                keep_hidden(i)
                act.wait_ge(sem_["down_done"], i + 2)
                act.wait_ge(sem_["spread_done"], i * 4 + 5)
                nc.scalar.activation(x_y, bank(2, 2), ACT.Copy).then_inc(sem_["y_kept"], 1)
            keep_share(n)
            return n

        def moe_vector(dve, m):
            sem_, per, C = m.sem, m.per, m.slots

            def pick(i):
                for t in range(NT):
                    for x in range(per):
                        ins = nc.vector.tensor_scalar(x_pick[:, t * P + x * C:t * P + (x + 1) * C],
                                                      consts[:, C_IOTA:C_IOTA + C],
                                                      m.slot[:, t, bass.ds(i * per + (per + x), 1)], None, ALU.is_equal)
                ins.then_inc(sem_["pick_ready"], 1)

            def share(i):
                for t in range(NT):
                    for x in range(per):
                        col = bass.ds(i * per + x, 1)
                        ins = nc.vector.tensor_scalar(x_share[:, t * P + x * C:t * P + (x + 1) * C],
                                                      consts[:, C_IOTA:C_IOTA + C], m.slot[:, t, col],
                                                      m.gate[:, t, col], ALU.is_equal, ALU.mult)
                ins.then_inc(sem_["share_ready"], 1)

            def hidden(i):
                dve.wait_ge(sem_["silu_done"], i + 2)
                dve.wait_ge(sem_["up_done"], i + 2)
                dve.wait_ge(sem_["hiddenT_done"], i + 1)
                nc.vector.tensor_tensor(x_hid, x_silu, bank(1), ALU.mult).then_inc(sem_["hidden_done"], 1)

            def add_spread(i):
                for r in range(4):
                    dve.wait_ge(sem_["spread_done"], i * 4 + r + 2)
                    x = xT[:, 2 * r:2 * r + 2, :]
                    nc.vector.tensor_tensor(x, x, bank(5 - r % 2).rearrange("p (b t) -> p b t", t=T), ALU.add)\
                        .then_inc(sem_["spread_added"], 1)

            for w in ("pick_ready", "share_ready", "hidden_done", "spread_added"):
                dve.sem_inc(sem_[w], 1)
            pick(0)
            nc.vector.memset(x_y, 0.0).then_inc(sem_["start"], 1)
            n = m.trip_count(dve)
            with dve.Fori(0, n) as i:
                dve.wait_ge(sem_["shareT_done"], i + 1)
                share(i)
                dve.wait_ge(sem_["gathered"], i * 2 + 3)
                pick(i + 1)
                hidden(i)
                add_spread(i)
            dve.wait_ge(sem_["shareT_done"], n + 1)
            share(n)
            dve.wait_ge(sem_["spread_added"], n * 4 + 1)
            add_spread(n)
            return n

        HALVES = 2 * NP2
        z_XgH, z_XgL = carve_r(o_Xg, 1024), carve_r(0, 1024)
        z_hidH, z_hidL = carve_r(o_hidT, 512), carve_r(1024, 512)
        hi_at = r_base + 1024
        HI_BUFS = 5

        def hi_buffer(j):
            b = j % HI_BUFS if j < 2 * HI_BUFS else (j - 2 * HI_BUFS) % (HI_BUFS - 1)
            return b, carve_r(hi_at + b * HALF, HALF)

        def moe2_landed(i, m):
            return landed["moe2"][m % SLOTS], i * (16 * TURNS2) + 16 * (1 + m // SLOTS)

        def moe2_products_done(i, m):
            what, u = MOE2_ORDER[m]
            return moe_sems["moe2"][{"g": "gate_done", "u": "up_done", "d": "down_done"}[what]], i * UNITS + u + 2

        def moe2_tensor(pe):
            m = M2
            sem_, U = m.sem, UNITS
            e, s, v = E[m.st], S[m.st], V[m.st]

            def gather(i):
                pe.wait_ge(sem_["pick_ready"], i + 2)
                for r in range(2):
                    for k in range(4 * r, 4 * r + 4):
                        for t in range(NT):
                            mm = nc.tensor.matmul(bank(7 - 2 * r)[:, (k % 4) * P:(k % 4 + 1) * P],
                                                  r_hrow[:, t * D + k * P:t * D + (k + 1) * P],
                                                  x_pick[:, t * P:(t + 1) * P], start=(t == 0), stop=(t == NT - 1))
                    mm.then_inc(sem_["gathered"], 1)

            def gate_or_up(i, what, u):
                m_ = MOE2_ORDER.index((what, u))
                out = bank(m.banks(u)["gu".index(what)])
                for half in range(2):
                    j = 2 * m_ + half
                    pe.wait_ge(weights_lo, i * HALVES + j + 1)
                    hi = hi_buffer(j)[1].rearrange("p (k n) -> p k n", n=512)
                    lo = ring_r[m_ % SLOTS][:, half * HALF:(half + 1) * HALF].rearrange("p (k n) -> p k n", n=512)
                    for q in range(4):
                        k = 4 * half + q
                        x = slice(k * P, (k + 1) * P)
                        mm = three(out, (z_XgH[:, x], z_XgL[:, x]), (hi[:, q, :], lo[:, q, :]), k == 0, k == KC - 1)
                mm.then_inc(sem_["gate_done" if what == "g" else "up_done"], 1)

            def share_transposed(i):
                pe.wait_ge(sem_["share_ready"], i + 2)
                pe.wait_ge(sem_["spread_added"], i * 4 + 1)
                for t in range(NT):
                    mm = nc.tensor.transpose(bank(4)[:, t * P:(t + 1) * P], x_share[:, t * P:(t + 1) * P], eye)
                mm.then_inc(sem_["shareT_done"], 1)

            def spread_back(i):
                pe.wait_ge(sem_["y_kept"], i + 1)
                pe.wait_ge(sem_["shareT_kept"], i + 2)
                for r in range(4):
                    if r >= 2:
                        pe.wait_ge(sem_["spread_added"], i * 4 + r)
                    for j in range(2):
                        k = 2 * r + j
                        mm = nc.tensor.matmul(bank(5 - r % 2)[:, j * T:(j + 1) * T], x_y[:, k * P:(k + 1) * P],
                                              x_shareT, start=True, stop=True)
                    mm.then_inc(sem_["spread_done"], 1)

            def hidden_transposed(i, u):
                pe.wait_ge(sem_["hidden_done"], i * U + u + 2)
                pe.wait_ge(hiddenT_lo, i * U + u + 1)
                for f in range(4):
                    mm = nc.tensor.transpose(bank(6)[:, f * P:(f + 1) * P], x_hid[:, f * P:(f + 1) * P], eye)
                mm.then_inc(sem_["hiddenT_done"], 1)

            def down(i, u):
                m_ = MOE2_ORDER.index(("d", u))
                if u == 0:
                    pe.wait_ge(sem_["y_kept"], i + 1)
                pe.wait_ge(hiddenT_lo, i * U + u + 2)
                for half in range(2):
                    j = 2 * m_ + half
                    pe.wait_ge(weights_lo, i * HALVES + j + 1)
                    hi = hi_buffer(j)[1].rearrange("p (f n) -> p f n", n=D)
                    lo = ring_r[m_ % SLOTS][:, half * HALF:(half + 1) * HALF].rearrange("p (f n) -> p f n", n=D)
                    for q in range(2):
                        f = 2 * half + q
                        x = slice(f * P, (f + 1) * P)
                        for c in range(2):
                            n = slice(c * 512, (c + 1) * 512)
                            mm = three(bank(2 + c), (z_hidH[:, x], z_hidL[:, x]), (hi[:, q, n], lo[:, q, n]),
                                       u == 0 and f == 0, u == U - 1 and f == 3)
                mm.then_inc(sem_["down_done"], 1)

            for w in ("gate_done", "up_done", "shareT_done", "spread_done", "gathered", "hiddenT_done", "down_done"):
                pe.sem_inc(sem_[w], 1)
            pe.wait_ge(*v.at("trips"))
            n = m.trip_count(pe)
            pe.wait_ge(*s.at("hrow"))
            gather(0)
            pe.wait_ge(sem_["start"], 1)
            with pe.Fori(0, n) as i:
                pe.wait_ge(gathered_lo, i * 2 + 3)
                pe.wait_ge(sem_["silu_done"], i * U + 1)
                gate_or_up(i, "g", 0)
                share_transposed(i)
                pe.wait_ge(sem_["hidden_done"], i * U + 1)
                gate_or_up(i, "u", 0)
                spread_back(i)
                for u in range(1, U):
                    if u == 1:
                        pe.wait_ge(sem_["spread_added"], i * 4 + 5)
                    else:
                        pe.wait_ge(sem_["silu_done"], i * U + u)
                    gate_or_up(i, "g", u)
                    hidden_transposed(i, u - 1)
                    if u > 1:
                        pe.wait_ge(sem_["hidden_done"], i * U + u)
                    gate_or_up(i, "u", u)
                    down(i, u - 1)
                hidden_transposed(i, U - 1)
                gather(i + 1)
                down(i, U - 1)
            share_transposed(n)
            spread_back(n)

        def moe2_steps(i, split, at_step):
            for p in range(NP2):
                nxt = (i, p + 1) if p + 1 < NP2 else (i + 1, 0)
                before_, between, after_ = at_step.get(p, ([], [], []))
                for f in before_:
                    f()
                split(*nxt, 0)
                for f in between:
                    f()
                split(*nxt, 1)
                for f in after_:
                    f()

        def moe2_scalar(act):
            m = M2
            sem_, U = m.sem, UNITS
            v = V[m.st]

            def split(i, m_, half, first=False):
                j = 2 * m_ + half
                if half == 0:
                    act.wait_ge(*moe2_landed(i, m_))
                if not first:
                    users = [q for q in range(HALVES) if hi_buffer(q)[0] == hi_buffer(j)[0]]
                    at = users.index(j)
                    if at > 0:
                        act.wait_ge(*moe2_products_done(i, users[at - 1] // 2))
                    elif users[-1] >= HALVES - 4:
                        act.wait_ge(*moe2_products_done(i - 1, users[-1] // 2))
                nc.scalar.activation(hi_buffer(j)[1], ring[:, m_ % SLOTS, half * HALF:(half + 1) * HALF],
                                     ACT.Copy).then_inc(weights_hi, 1)

            def silu(i, u):
                act.wait_ge(sem_["gate_done"], i * U + u + 2)
                act.wait_ge(sem_["hidden_done"], i * U + u + 1)
                nc.scalar.activation(x_silu, bank(m.banks(u)[0]), ACT.Silu).then_inc(sem_["silu_done"], 1)

            def keep_share(i):
                act.wait_ge(sem_["shareT_done"], i + 2)
                act.wait_ge(sem_["spread_done"], i * 4 + 1)
                nc.scalar.activation(x_shareT, bank(4)[:, 0:T], ACT.Copy).then_inc(sem_["shareT_kept"], 1)

            def keep_gathered(i, r):
                act.wait_ge(sem_["gathered"], i * 2 + 2 + r)
                nc.scalar.activation(z_XgH[:, r * 512:(r + 1) * 512], bank(7 - 2 * r), ACT.Copy)\
                    .then_inc(sem_["gathered_kept"], 1)

            def keep_hidden(i, u):
                act.wait_ge(sem_["hiddenT_done"], i * U + u + 2)
                act.wait_ge(sem_["down_done"], i * U + u + 1)
                nc.scalar.activation(z_hidH, bank(6), ACT.Copy).then_inc(sem_["hiddenT_kept"], 1)

            def keep_y(i):
                act.wait_ge(sem_["down_done"], i * U + U + 1)
                act.wait_ge(sem_["spread_done"], i * 4 + 5)
                nc.scalar.activation(x_y, bank(2, 2), ACT.Copy).then_inc(sem_["y_kept"], 1)

            for w in ("silu_done", "shareT_kept", "gathered_kept", "hiddenT_kept", "y_kept"):
                act.sem_inc(sem_[w], 1)
            for half in range(2):
                split(0, 0, half, first=True)
            act.wait_ge(*v.at("trips"))
            n = m.trip_count(act)
            for r in range(2):
                keep_gathered(0, r)
            with act.Fori(0, n) as i:
                work = {1: ([], [lambda: keep_share(i), lambda: silu(i, 0)], [])}
                for u in range(1, U):
                    work[3 * u] = ([], [lambda u=u: keep_hidden(i, u - 1), lambda u=u: silu(i, u)], [])
                work[NP2 - 1] = ([lambda: keep_hidden(i, U - 1)],
                                 [lambda: keep_gathered(i + 1, 0), lambda: keep_gathered(i + 1, 1)],
                                 [lambda: keep_y(i)])
                moe2_steps(i, split, work)
            keep_share(n)
            return n

        def moe2_vector(dve):
            m = M2
            sem_, U = m.sem, UNITS

            def split(i, m_, half):
                j = 2 * m_ + half
                dve.wait_ge(weights_hi, i * HALVES + j + 1)
                at = slice(half * HALF, (half + 1) * HALF)
                nc.vector.tensor_tensor(ring_r[m_ % SLOTS][:, at], ring[:, m_ % SLOTS, at],
                                        hi_buffer(j)[1].bitcast(F32), ALU.subtract).then_inc(weights_lo, 1)

            def pick(i):
                for t in range(NT):
                    ins = nc.vector.tensor_scalar(x_pick[:, t * P:(t + 1) * P], consts[:, C_IOTA:C_IOTA + P],
                                                  m.slot[:, t, bass.ds(i + 1, 1)], None, ALU.is_equal)
                ins.then_inc(sem_["pick_ready"], 1)

            def share(i):
                dve.wait_ge(sem_["shareT_done"], i + 1)
                for t in range(NT):
                    ins = nc.vector.tensor_scalar(x_share[:, t * P:(t + 1) * P], consts[:, C_IOTA:C_IOTA + P],
                                                  m.slot[:, t, bass.ds(i, 1)], m.gate[:, t, bass.ds(i, 1)],
                                                  ALU.is_equal, ALU.mult)
                ins.then_inc(sem_["share_ready"], 1)

            def hidden(i, u):
                dve.wait_ge(sem_["silu_done"], i * U + u + 2)
                dve.wait_ge(sem_["up_done"], i * U + u + 2)
                dve.wait_ge(sem_["hiddenT_done"], i * U + u + 1)
                nc.vector.tensor_tensor(x_hid, x_silu, bank(m.banks(u)[1]), ALU.mult).then_inc(sem_["hidden_done"], 1)

            def rest_of_hidden(i, u):
                dve.wait_ge(sem_["hiddenT_kept"], i * U + u + 2)
                nc.vector.tensor_tensor(z_hidL, bank(6), z_hidH.bitcast(F32), ALU.subtract).then_inc(hiddenT_lo, 1)

            def rest_of_gathered(i, r):
                dve.wait_ge(sem_["gathered_kept"], i * 2 + r + 2)
                x = slice(r * 512, (r + 1) * 512)
                nc.vector.tensor_tensor(z_XgL[:, x], bank(7 - 2 * r), z_XgH[:, x].bitcast(F32), ALU.subtract)\
                    .then_inc(gathered_lo, 1)

            def add_spread(i):
                for r in range(4):
                    dve.wait_ge(sem_["spread_done"], i * 4 + r + 2)
                    x = xT[:, 2 * r:2 * r + 2, :]
                    nc.vector.tensor_tensor(x, x, bank(5 - r % 2).rearrange("p (b t) -> p b t", t=T), ALU.add)\
                        .then_inc(sem_["spread_added"], 1)

            def next_pick(i):
                dve.wait_ge(sem_["gathered"], i * 2 + 3)
                pick(i + 1)

            for w in ("pick_ready", "share_ready", "hidden_done", "spread_added"):
                dve.sem_inc(sem_[w], 1)
            dve.sem_inc(gathered_lo, 1)
            dve.sem_inc(hiddenT_lo, 1)
            pick(0)
            nc.vector.memset(x_y, 0.0).then_inc(sem_["start"], 1)
            for half in range(2):
                split(0, 0, half)
            n = m.trip_count(dve)
            for r in range(2):
                rest_of_gathered(0, r)
            with dve.Fori(0, n) as i:
                work = {0: ([lambda: share(i)], [], []),
                        1: ([], [lambda: next_pick(i)], []),
                        2: ([lambda: add_spread(i), lambda: hidden(i, 0)], [], [])}
                for u in range(1, U):
                    work[3 * u] = ([], [lambda u=u: rest_of_hidden(i, u - 1)], [])
                    work[3 * u + 1] = ([], [lambda u=u: hidden(i, u)], [])
                work[NP2 - 1] = ([lambda: rest_of_hidden(i, U - 1)],
                                 [lambda: rest_of_gathered(i + 1, 0), lambda: rest_of_gathered(i + 1, 1)], [])
                moe2_steps(i, split, work)
            share(n)
            dve.wait_ge(sem_["spread_added"], n * 4 + 1)
            add_spread(n)

        c_w = [carve(0, HC), carve(HC, HC)]
        c_qt, c_kt, c_AT = (carve(HC * n, HC) for n in (2, 3, 4))
        c_kd = [carve(HC * 5, HC), carve(HC * 6, HC)]
        c_S = [carve(HC * 7, 512), carve(HC * 7 + 512, 512)]
        y_cat = carve(HC * 8, KC * T)
        c_small = carve(HC * 20, 128)
        c_decay = c_small[:, 0:16]
        c_retk = c_small[:, 16:24]
        c_lb, c_omlb = c_small[:, 24:32], c_small[:, 32:40]
        NL = len(LEVELS)

        class Gated:
            def __init__(self, st, tag, nb, q, k, g, v, gate, y, gain):
                self.st, self.tag, self.nb = st, tag, nb
                self.q, self.k, self.g, self.v, self.gate, self.y, self.gain = q, k, g, v, gate, y, gain
                self.N = nb * T
                self.w = [w[:, 0:self.N] for w in c_w]
                self.kt = c_kt[:, 0:self.N]
                self.padded = nb == 2

        def parity(ap, par):
            return ap.rearrange("p (b r t) -> p b r t", r=2, t=T)[:, :, par, :]

        def scores(pe, x, name, k, q, b0):
            for h in range(H4):
                for t in range(NT):
                    kb = k[:, (h if x.nb == 4 else h // 2) * T + t * P:(h if x.nb == 4 else h // 2) * T + t * P + P]
                    mm = nc.tensor.matmul(inst(bank(b0, 2), h, t), kb, inst(q, h, t), start=True, stop=True)
            mm.then_inc(*E[x.st].step())
            E[x.st].name(x.tag + name)

        def gated_tensor_round(pe, x, n):
            v, tag = V[x.st], x.tag
            b0 = 4 + 2 * (n % 2)
            if n == 0:
                pe.wait_ge(*v.at(tag + "ready"))
                scores(pe, x, "r0", x.k, c_qt if x.padded else x.q, b0)
            else:
                pe.wait_ge(*v.at(f"{tag}q{n}"))
                pe.wait_ge(*G[x.st].at(f"{tag}k{n}"))
                if n >= 2:
                    pe.wait_ge(*v.at(f"{tag}taken{n - 2}"))
                scores(pe, x, f"r{n}", x.kt, c_qt, b0)

        def gated_scalar_round(act, x, n):
            s, v = S[x.st], V[x.st]
            w = x.w[n % 2]
            act.wait_ge(*v.at(f"{x.tag}d{n}"))
            nc.scalar.activation(w, w, ACT.Abs).then_inc(*s.step())
            act.wait_ge(*s.last())
            nc.scalar.activation(w, w, ACT.Exp, scale=-1.0).then_inc(*s.step())
            s.name(f"{x.tag}w{n}")

        def gated_pool_round(pool, x, n):
            pool.wait_ge(*S[x.st].at(f"{x.tag}w{n}"))
            if n >= 2:
                pool.wait_ge(*E[x.st].at(f"{x.tag}r{n - 1}"))
            nc.gpsimd.tensor_tensor(x.kt, x.k, x.w[n % 2], ALU.mult).then_inc(*G[x.st].step())
            G[x.st].name(f"{x.tag}k{n}")

        def gated_difference(dve, x, n):
            v = V[x.st]
            size = LEVELS[n - 1]
            g = x.g.rearrange("p (b i) -> p b i", i=2 * size)
            if n >= 3:
                dve.wait_ge(*G[x.st].at(f"{x.tag}k{n - 2}"))
            nc.vector.tensor_tensor(x.w[n % 2].rearrange("p (b i) -> p b i", i=2 * size), g,
                                    g[:, :, size - 1:size].to_broadcast([P, x.N // (2 * size), 2 * size]),
                                    ALU.subtract).then_inc(*v.step())
            v.name(f"{x.tag}d{n}")

        def scaled_queries(dve, x, w, scale=1.0):
            v = V[x.st]
            if x.padded:
                for par in range(2):
                    ins = nc.vector.scalar_tensor_tensor(
                        parity(c_qt, par), x.q.rearrange("p (b t) -> p b t", t=T),
                        consts[:, C_HALF + par:C_HALF + par + 1], w.rearrange("p (b t) -> p b t", t=T),
                        ALU.mult, ALU.mult).then_inc(*v.step())
            else:
                nc.vector.tensor_tensor(c_qt, x.q, w, ALU.mult).then_inc(*v.step())

        def gated_vector_round(dve, x, n):
            e, s, v = E[x.st], S[x.st], V[x.st]
            tag = x.tag
            if n < NL:
                if n >= 1:
                    dve.wait_ge(*v.last())
                gated_difference(dve, x, n + 1)
            if n >= 1:
                dve.wait_ge(*s.at(f"{tag}w{n}"))
                if n >= 2 or x.padded:
                    dve.wait_ge(*e.at(f"{tag}r{n - 1}"))
                scaled_queries(dve, x, x.w[n % 2])
                v.name(f"{tag}q{n}")
                take_scores(dve, x, n - 1)

        def take_scores(dve, x, n):
            e, v = E[x.st], V[x.st]
            b0 = 4 + 2 * (n % 2)
            dve.wait_ge(*e.at(f"{x.tag}r{n}"))
            if n == 0:
                nc.vector.tensor_tensor(blocks(c_AT), blocks(bank(b0, 2)), spread(eye), ALU.mult).then_inc(*v.step())
            else:
                mask = level_mask(n - 1).bitcast(I32).unsqueeze(1).to_broadcast([P, 8, P])
                nc.vector.copy_predicated(blocks(c_AT), mask, blocks(bank(b0, 2))).then_inc(*v.step())
            v.name(f"{x.tag}taken{n}")
            dve.wait_ge(*v.last())

        def gated_vector_end(dve, x):
            e, s, v = E[x.st], S[x.st], V[x.st]
            tag = x.tag
            take_scores(dve, x, NL)
            dve.wait_ge(*G[x.st].at(f"{tag}k{NL}"))
            chunks = x.g.rearrange("p (b i) -> p b i", i=CH)
            nc.vector.tensor_tensor(x.w[0].rearrange("p (b i) -> p b i", i=CH), chunks,
                                    chunks[:, :, CH - 1:CH].to_broadcast([P, x.N // CH, CH]),
                                    ALU.subtract).then_inc(*v.step())
            v.name(tag + "last")
            dve.wait_ge(*s.at(tag + "eg"))
            scaled_queries(dve, x, x.w[1])
            v.name(tag + "qd")
            nc.vector.tensor_copy(c_decay[:, 0:4 * x.nb], x.w[1][:, CH - 1::CH]).then_inc(*v.step())
            dve.wait_ge(*v.last())

        def gated_scalar_end(act, x):
            s, v = S[x.st], V[x.st]
            tag = x.tag
            act.wait_ge(*v.at(tag + "last"))
            nc.scalar.activation(x.w[1], x.g, ACT.Exp).then_inc(*s.step())
            s.name(tag + "eg")
            nc.scalar.activation(x.w[0], x.w[0], ACT.Abs).then_inc(*s.step())
            act.wait_ge(*s.last())
            nc.scalar.activation(x.w[0], x.w[0], ACT.Exp, scale=-1.0).then_inc(*s.step())
            s.name(tag + "el")
            for b in range(x.N // 512):
                act.wait_ge(*E[x.st].at(f"{tag}kr{b}"))
                for half in range(2):
                    nc.scalar.activation(c_kd[half][:, b * 512:(b + 1) * 512], bank(4 + b), ACT.Copy,
                                         scale=consts[:, C_HALF + half:C_HALF + half + 1]).then_inc(*s.step())
            s.name(tag + "kd")

        def gated_pool_end(pool, x):
            pool.wait_ge(*S[x.st].at(x.tag + "el"))
            nc.gpsimd.tensor_tensor(x.kt, x.k, x.w[0], ALU.mult).then_inc(*G[x.st].step())
            G[x.st].name(x.tag + "kl")

        def gated_tensor_end(pe, x, out=None):
            e, v = E[x.st], V[x.st]
            pe.wait_ge(*G[x.st].at(x.tag + "kl"))
            pe.wait_ge(*v.at(f"{x.tag}taken{NL}"))
            k_rows(pe, x, x.kt)
            attend_tensor(pe, x, out)

        def k_rows(pe, x, k):
            e = E[x.st]
            for b in range(x.N // 512):
                for j in range(4):
                    mm = nc.tensor.transpose(bank(4 + b)[:, j * P:(j + 1) * P],
                                             k[:, b * 512 + j * P:b * 512 + (j + 1) * P], eye)
                mm.then_inc(*e.step())
                e.name(f"{x.tag}kr{b}")

        def attend_tensor(pe, x, out=None):
            e, s, v, tag = E[x.st], S[x.st], V[x.st], x.tag
            pe.wait_ge(*s.at(tag + "kd"))
            pe.wait_ge(*s.at(tag + "v"))
            pe.wait_ge(*v.at(tag + "qd"))

            def value(h, t):
                return x.v[:, t * 512 + h * P:t * 512 + (h + 1) * P]

            def add_to_state(c):
                t = c // 2
                if c >= 2:
                    pe.wait_ge(*v.at(f"{tag}S{c - 2}"))
                for h in range(H4):
                    kd = inst(c_kd[c % 2], h if x.nb == 4 else h // 2, t)
                    mm = nc.tensor.matmul(bank(4 + c % 2)[:, h * P:(h + 1) * P], kd, value(h, t),
                                          start=True, stop=True)
                mm.then_inc(*e.step())
                e.name(f"{tag}Sp{c}")

            add_to_state(0)
            for c in range(NCH):
                t, off = c // 2, (c % 2) * CH
                if c < NCH - 2:
                    add_to_state(c + 1)
                if out:
                    out.fill(1)
                if c:
                    pe.wait_ge(*v.at(f"{tag}S{c - 1}"))
                for h in range(H4):
                    o = bank(6, 2)[:, h * T + c * CH:h * T + (c + 1) * CH]
                    if c:
                        nc.tensor.matmul(o, c_S[(c - 1) % 2][:, h * P:(h + 1) * P],
                                         c_qt[:, h * T + c * CH:h * T + (c + 1) * CH], start=True, stop=False)
                    mm = nc.tensor.matmul(o, value(h, t), inst(c_AT, h, t)[:, off:off + CH],
                                          start=(c == 0), stop=True)
                mm.then_inc(*e.step())
                e.name(f"{tag}o{c}")
            if out:
                out.fill(2)
            pe.wait_ge(*s.at(tag + "osq"))
            for half in range(2):
                mm = nc.tensor.matmul(bank(4 + half), ones[:, :], c_w[0][:, half * 512:(half + 1) * 512],
                                      start=True, stop=True)
            mm.then_inc(*e.step())
            e.name(tag + "osum")

        def attend_vector(dve, x, decay, meanwhile=None):
            e, s, v, tag = E[x.st], S[x.st], V[x.st], x.tag
            for c in range(NCH - 1):
                dve.wait_ge(*e.at(f"{tag}Sp{c}"))
                if c > 1:
                    dve.wait_ge(*e.at(f"{tag}o{c - 1}"))
                for h in range(H4):
                    hs = slice(h * P, (h + 1) * P)
                    if c == 0:
                        nc.vector.tensor_copy(c_S[0][:, hs], bank(4)[:, hs]).then_inc(*v.step())
                    else:
                        nc.vector.scalar_tensor_tensor(c_S[c % 2][:, hs], c_S[(c - 1) % 2][:, hs], decay(h, c),
                                                       bank(4 + c % 2)[:, hs], ALU.mult, ALU.add)\
                            .then_inc(*v.step())
                v.name(f"{tag}S{c}")
                dve.wait_ge(*v.last())
            if meanwhile:
                meanwhile()
            dve.wait_ge(*s.at(tag + "orstd"))
            nc.vector.scalar_tensor_tensor(x.y, bank(6, 2), x.gain, c_w[1], ALU.mult, ALU.mult).then_inc(*v.step())
            dve.wait_ge(*v.last())
            dve.wait_ge(*s.at(tag + "gate"))
            nc.vector.tensor_tensor(x.y, x.y, x.gate, ALU.mult).then_inc(*v.step())
            v.name(tag + "y")
            dve.wait_ge(*v.last())

        def attend_scalar(act, x):
            e, s, tag = E[x.st], S[x.st], x.tag
            act.wait_ge(*e.at(f"{tag}o{NCH - 1}"))
            nc.scalar.activation(c_w[0], bank(6, 2), ACT.Square).then_inc(*s.step())
            s.name(tag + "osq")
            act.wait_ge(*e.at(tag + "osum"))
            nc.scalar.activation(c_w[1], bank(4, 2), ACT.Ln, bias=eps_col, scale=1.0 / P).then_inc(*s.step())
            act.wait_ge(*s.last())
            nc.scalar.activation(c_w[1], c_w[1], ACT.Exp, scale=-0.5).then_inc(*s.step())
            s.name(tag + "orstd")

        def keep_banks(act, st, name, names, base, out, func=ACT.Copy, scale=1.0, parts=range(2)):
            e, s = E[st], S[st]
            b0 = 2 * ((base + names.index(name)) % 2)
            for half in parts:
                round_next(act, st, "two", names, name, half)
                act.wait_ge(*e.at(f"{name}_{half}"))
                nc.scalar.activation(out(half), bank(b0 + half), func, scale=scale).then_inc(*s.step())
                s.name(f"{name}_{half}")

        def halves(ap):
            return lambda half: ap[:, half * 512:(half + 1) * 512]

        B2 = len(PROJ1)
        a_q, a_k, a_v, a_gate, b_v, b_gate = (carve(tail_at + HC * n, HC) for n in range(6))
        b_q, b_k, b_g = (carve(tail_at + HC * 6 + 512 * n, 512) for n in range(3))
        a_cos, a_sin = (carve(tail_at + HC * 6 + 1536 + T * n, T) for n in range(2))
        a_ang, a_turn = (carve(tail_at + HC * 8 + T * n, T) for n in (1, 2))
        b_low = carve(tail_at + HC * 9, T)
        GLA = Gated("mix2", "b", 2, b_q, b_k, b_g, b_v, b_gate, y_cat[:, HC:2 * HC], param("gla_g"))
        RET = Gated("mix2", "a", 4, a_q, a_k, None, a_v, a_gate, y_cat[:, 0:HC], param("ret_g"))

        def mixer2_tensor(pe):
            st = "mix2"
            e, s, v = E[st], S[st], V[st]
            norm_tensor(pe, st, "f")
            norm_tensor(pe, st, "n")
            pe.wait_ge(*v.at("h"))
            tail = param("tail2", 128).rearrange("p (k n) -> p k n", n=16)
            for k in range(KC):
                mm = nc.tensor.matmul(bank(6)[0:16, 0:T], tail[:, k, :], hT[:, k, :], start=(k == 0), stop=(k == KC - 1))
            mm.then_inc(*e.step())
            e.name("low")

            def proj(name, quarters=range(4), rows_=False):
                (project_rows if rows_ else project)(
                    pe, st, "two", name, free_by(st, PROJ2, name, lambda n, half: [s.at(f"{n}_{half}")]), quarters)

            def rotate(x, name):
                for half in range(2):
                    mm = nc.tensor.matmul(bank(6 + half), consts[:, C_ROT:C_ROT + P], x[:, half * 512:(half + 1) * 512],
                                          start=True, stop=True)
                mm.then_inc(*e.step())
                e.name(name)

            proj("bqk")
            pe.wait_ge(*s.at("low"))
            for b in range(2):
                mm = nc.tensor.matmul(bank(7)[:, b * T:(b + 1) * T], param("gla_w", 256)[0:16, b * P:(b + 1) * P],
                                      b_low[0:16, :], start=True, stop=True)
            mm.then_inc(*e.step())
            e.name("z")
            proj("bv", rows_=True)
            gated_tensor_round(pe, GLA, 0)
            n = 1
            for name in ("aq", "ak", "bg"):
                for half in range(2):
                    proj(name, (2 * half, 2 * half + 1))
                    gated_tensor_round(pe, GLA, n)
                    n += 1
            pe.wait_ge(*s.at("aq_1"))
            pe.wait_ge(*v.at(f"btaken{NL - 1}"))
            rotate(a_q, "rotq")
            proj("av", (0, 1), True)
            pe.wait_ge(*s.at("ak_1"))
            pe.wait_ge(*v.at("q_rotated"))
            rotate(a_k, "rotk")
            proj("av", (2, 3), True)
            pe.wait_ge(*v.at("k_rotated"))
            gated_tensor_end(pe, GLA, ProjectionFill(proj, "ag"))
            pe.wait_ge(*v.at("rotated"))
            pe.wait_ge(*v.at("by"))
            scores(pe, RET, "r0", a_k, a_q, 6)
            out = OutProjection(pe, st, "two", "out2", y_cat, range(4, 8), [s.at("ag_0"), s.at("ag_1"), s.at("av_1")])
            out.fill(2)
            pe.wait_ge(*s.at("borstd"))
            k_rows(pe, RET, a_k)
            pe.wait_ge(*v.at("ataken"))
            attend_tensor(pe, RET, out)
            out.finish(v.at("ay"))

        def mixer2_scalar(act, waits):
            st = "mix2"
            e, s, v = E[st], S[st], V[st]
            act.preload_act_table_set(EXP_LN)
            weights_hi_of(act, st, "two", "bqk", range(4))
            norm_scalar(act, st, "f", waits)
            norm_scalar(act, st, "n", [v.at("x_first"), v.at("x")])
            tokens_hi(act, st)
            act.wait_ge(*v.at("angles"))
            nc.scalar.activation(a_sin, a_ang, ACT.Sin).then_inc(*s.step())
            nc.scalar.activation(a_cos, a_turn, ACT.Sin).then_inc(*s.step())
            s.name("sincos")
            act.preload_act_table_set(EXP_LN)
            act.wait_ge(*e.at("low"))
            nc.scalar.activation(b_low[0:16, :], bank(6)[0:16, 0:T], ACT.Copy).then_inc(*s.step())
            s.name("low")

            def keep(name, out, **kw):
                keep_banks(act, st, name, PROJ2, B2, out, **kw)

            for half, (name, out, scale) in enumerate((("bqk_0", b_q, 64 ** -0.5), ("bqk_1", b_k, 1.0))):
                round_next(act, st, "two", PROJ2, "bqk", half)
                act.wait_ge(*e.at(name))
                nc.scalar.activation(out, bank(2 * (B2 % 2) + half), ACT.Copy, scale=scale).then_inc(*s.step())
                s.name(name)
            act.wait_ge(*v.at("z"))
            nc.scalar.activation(c_qt[:, 0:512], c_qt[:, 0:512], ACT.Exp).then_inc(*s.step())
            act.wait_ge(*s.last())
            nc.scalar.activation(c_qt[:, 0:512], c_qt[:, 0:512], ACT.Ln, bias=1.0).then_inc(*s.step())
            s.name("softplus")
            keep("bv", halves(b_v))
            s.name("bv")
            n = 1
            for name, out, kw in (("aq", a_q, {}), ("ak", a_k, {"scale": float(P) ** -0.5}), ("bg", b_gate, {})):
                for part in range(2):
                    gated_scalar_round(act, GLA, n)
                    keep(name, halves(out), parts=(part,), **kw)
                    n += 1
            act.wait_ge(*s.last())
            nc.scalar.activation(b_gate, b_gate, ACT.Silu).then_inc(*s.step())
            s.name("bgate")
            act.preload_act_table_set(EXP_LN)
            gated_scalar_end(act, GLA)
            keep("av", halves(a_v))
            s.name("av")
            keep("ag", halves(a_gate))
            attend_scalar(act, GLA)
            for b in range(2):
                act.wait_ge(*e.at(f"akr{b}"))
                for half in range(2):
                    for h in (2 * b, 2 * b + 1):
                        nc.scalar.activation(c_kd[half][:, h * T:(h + 1) * T],
                                             bank(4 + b)[:, (h % 2) * T:(h % 2 + 1) * T], ACT.Copy,
                                             scale=c_retk[:, half * 4 + h:half * 4 + h + 1]).then_inc(*s.step())
            s.name("akd")
            nc.scalar.activation(a_gate, a_gate, ACT.Silu).then_inc(*s.step())
            s.name("agate")
            act.preload_act_table_set(EXP_LN)
            attend_scalar(act, RET)

        def mixer2_pool(pool):
            def lo(name, quarters=range(4)):
                weights_lo_of(pool, "mix2", "two", name, quarters)

            lo("bqk")
            lo("bv")
            lo("aq", (0, 1))
            n = 1
            for name, after in (("aq", "ak"), ("ak", "bg"), ("bg", "av")):
                gated_pool_round(pool, GLA, n)
                lo(name, (2, 3))
                gated_pool_round(pool, GLA, n + 1)
                lo(after, (0, 1))
                n += 2
            lo("av", (2, 3))
            gated_pool_end(pool, GLA)
            lo("ag")

        def mixer2_vector(dve):
            st = "mix2"
            e, s, v = E[st], S[st], V[st]
            norm_vector(dve, st, "f", param("final_g", 8), xT, "x")

            def do(ins):
                ins.then_inc(*v.step())
                dve.wait_ge(*v.last())

            dve.wait_ge(loaded_positions, 16)
            do(nc.vector.tensor_copy(a_ang, a_pos))
            do(nc.vector.tensor_scalar(a_ang, a_ang, consts[:, C_FREQ:C_FREQ + 1], None, ALU.mult))
            magic = float(3 << 22)
            do(nc.vector.tensor_scalar(a_turn, a_ang, float(1 / (2 * np.pi)), magic, ALU.mult, ALU.add))
            do(nc.vector.tensor_scalar(a_turn, a_turn, -magic, None, ALU.add))
            for part in (6.28125, 0.0019340515136718750, 2 * np.pi - 6.28125 - 0.0019340515136718750):
                do(nc.vector.scalar_tensor_tensor(a_ang, a_turn, -float(part), a_ang, ALU.mult, ALU.add))
            limit = 3.1415925
            do(nc.vector.tensor_scalar(a_ang, a_ang, limit, -limit, ALU.min, ALU.max))
            do(nc.vector.scalar_tensor_tensor(a_turn, a_ang, -1.0, a_ang, ALU.mult, ALU.min))
            nc.vector.tensor_scalar(a_turn, a_turn, float(np.pi / 2), None, ALU.add).then_inc(*v.step())
            v.name("angles")
            norm_vector(dve, st, "n", param("mix2_g", 8), hT, "h")
            tokens_lo(dve, st)
            for half in range(2):
                do(nc.vector.tensor_scalar(c_retk[:, half * 4:half * 4 + 4], consts[:, C_RETK:C_RETK + 4],
                                           consts[:, C_HALF + half:C_HALF + half + 1], None, ALU.mult))
            v.name("retk")
            dve.wait_ge(*e.at("z"))
            for b in range(2):
                do(nc.vector.tensor_scalar(b_g[:, b * T:(b + 1) * T], bank(7)[:, b * T:(b + 1) * T],
                                           param("gla_b", 1, b), None, ALU.add))
            nc.vector.scalar_tensor_tensor(c_qt[:, 0:512], b_g, -1.0, b_g, ALU.mult, ALU.min).then_inc(*v.step())
            v.name("z")
            dve.wait_ge(*s.at("softplus"))
            do(nc.vector.scalar_tensor_tensor(b_g, b_g, 0.0, c_qt[:, 0:512], ALU.min, ALU.subtract))
            do(nc.vector.tensor_scalar(b_g, b_g, 1.0 / 16.0, None, ALU.mult))
            cumulate(dve, GLA)
            dve.wait_ge(*v.last())
            dve.wait_ge(*s.at("bqk_1"))
            for par in range(2):
                nc.vector.tensor_scalar(parity(c_qt, par), b_q.rearrange("p (b t) -> p b t", t=T),
                                        consts[:, C_HALF + par:C_HALF + par + 1], None, ALU.mult)\
                    .then_inc(*v.step())
            v.name("bready")
            for n in range(NL + 1):
                gated_vector_round(dve, GLA, n)
            gated_vector_end(dve, GLA)
            dve.wait_ge(*s.at("sincos"))
            turned = y_cat[:, 0:HC]
            for x, name in ((a_q, "q"), (a_k, "k")):
                dve.wait_ge(*e.at(f"rot{name}"))
                nc.vector.tensor_tensor(per_head(turned), per_head(bank(6, 2)), a_sin.unsqueeze(1).to_broadcast([P, H4, T]),
                                        ALU.mult).then_inc(*v.step())
                v.name(f"{name}_rotated")
                do(nc.vector.tensor_tensor(per_head(x), per_head(x), a_cos.unsqueeze(1).to_broadcast([P, H4, T]),
                                           ALU.mult))
                do(nc.vector.tensor_tensor(x, x, turned, ALU.add))
            v.name("rotated")
            attend_vector(dve, GLA, lambda h, c: c_decay[:, (h // 2) * 4 + c:(h // 2) * 4 + c + 1])
            dve.wait_ge(*e.at("ar0"))
            for h in range(H4):
                at = c_AT[:, h * T:(h + 1) * T].rearrange("p (t i) -> p t i", i=P)
                mask = consts[:, C_RET + h * P:C_RET + (h + 1) * P].unsqueeze(1).to_broadcast([P, NT, P])
                nc.vector.tensor_tensor(at, bank(6, 2)[:, h * T:(h + 1) * T].rearrange("p (t i) -> p t i", i=P),
                                        mask, ALU.mult).then_inc(*v.step())
            v.name("ataken")
            qdec = consts[:, C_RETQ:C_RETQ + H4 * CH].rearrange("p (h i) -> p h i", h=H4)
            for c in range(NCH):
                cs = slice(c * CH, (c + 1) * CH)
                nc.vector.tensor_tensor(per_head(c_qt)[:, :, cs], per_head(a_q)[:, :, cs], qdec, ALU.mult)\
                    .then_inc(*v.step())
            v.name("aqd")
            attend_vector(dve, RET, lambda h, c: CHUNK_DECAY[h])
            for n in range(2):
                ffn_weights_lo(dve, n)
            add_residual(dve, st, "out2")

        def cumulate(dve, x):
            v = V[x.st]
            for c in range(x.N // CH):
                g = x.g[:, c * CH:(c + 1) * CH]
                nc.vector.tensor_tensor_scan(g, ones[:, 0:CH], g, 0.0, ALU.mult, ALU.add).then_inc(*v.step())

        f_silu = [carve(2400 + 512 * n, 512) for n in range(2)]
        f_hid = [carve(3424 + 512 * n, 512) for n in range(2)]
        f_hi_at = ARENA_CUTS[0] + ARENA_CUTS[1]
        f_hid_hi = [carve_r(512 * n, 512) for n in range(2)]
        f_hid_lo = [carve_r(1024 + 512 * n, 512) for n in range(2)]
        F_UNITS = [("g", 0), ("u", 0)]
        for c in range(1, FFC):
            F_UNITS += [("g", c), ("u", c), ("d", c - 1)]
        F_UNITS.append(("d", FFC - 1))
        F_HI = 4

        def ffn_unit(n):
            what, c = F_UNITS[n]
            name = f"ffn_d{c}" if what == "d" else f"ffn_gu{c}"
            slot = slot_of("two", name)
            _, landed_sem, value = piece("two", name)
            hi = carve_r(f_hi_at + (n % F_HI) * HALF, HALF)
            if what == "d":
                views = [x.rearrange("p (f n) -> p f n", n=D)
                         for x in (ring[:, slot, 0:HALF], ring_r[slot][:, 0:HALF], hi)]
            else:
                a = "gu".index(what)
                views = [x.rearrange("p (k a n) -> p k a n", a=2, n=256)[:, :, a, :]
                         for x in (ring[:, slot, :], ring_r[slot][:, :])]
                views.append(hi.rearrange("p (k n) -> p k n", n=256))
            return (*views, (landed_sem, value), f"{name}_{1 if what == 'd' else a}")

        def ffn_tensor(pe):
            st = "ffn"
            e, s, v = E[st], S[st], V[st]
            norm_tensor(pe, st, "n")

            def gate_or_up(n, a, c):
                _, lo, hi, _, name = ffn_unit(n)
                for j in range(2):
                    for k in range(KC):
                        if n == 0 and j == 0 and k % 4 == 0:
                            pe.wait_ge(*v.at(f"tok_lo{k // 4}"))
                        x = slice(j * P, (j + 1) * P)
                        mm = three(bank(2 * (c % 2) + a)[:, j * T:(j + 1) * T], (hi[:, k, x], lo[:, k, x]),
                                   (tok[0][:, k, :], tok[1][:, k, :]), k == 0, k == KC - 1)
                mm.then_inc(*e.step())
                e.name(name)

            def down(n, c):
                _, lo, hi, _, name = ffn_unit(n)
                pe.wait_ge(*v.at(f"hid_lo{c}"))
                for f in range(2):
                    y = slice(f * T, (f + 1) * T)
                    for d in range(KC):
                        x = slice(d * P, (d + 1) * P)
                        mm = three(bank(4 + d // 2)[:, (d % 2) * T:(d % 2 + 1) * T], (hi[:, f, x], lo[:, f, x]),
                                   (f_hid_hi[c % 2][:, y], f_hid_lo[c % 2][:, y]),
                                   c == 0 and f == 0 and d % 2 == 0, c == FFC - 1 and f == 1,
                                   skip_group_check=True)
                mm.then_inc(*e.step())
                e.name(name)

            for n, (what, c) in enumerate(F_UNITS):
                pe.wait_ge(*v.at(f"w_lo{n}"))
                if what == "d":
                    down(n, c)
                else:
                    if what == "g" and c >= 2:
                        pe.wait_ge(*v.at(f"hid{c - 2}"))
                    gate_or_up(n, "gu".index(what), c)

        def ffn_steps(split, after):
            for n in range(2, len(F_UNITS) + 2):
                if n < len(F_UNITS):
                    split(n)
                after(*F_UNITS[n - 2])

        def ffn_scalar(act):
            st = "ffn"
            e, s, v = E[st], S[st], V[st]

            def split(n):
                src, _, hi, landed_at, _ = ffn_unit(n)
                act.wait_ge(*landed_at)
                if n >= F_HI:
                    act.wait_ge(*e.at(ffn_unit(n - F_HI)[4]))
                nc.scalar.activation(hi, src, ACT.Copy).then_inc(*s.step())
                s.name(f"w_hi{n}")

            def hidden_hi(c):
                act.wait_ge(*v.at(f"hid{c}"))
                if c >= 2:
                    act.wait_ge(*e.at(f"ffn_d{c - 2}_1"))
                nc.scalar.activation(f_hid_hi[c % 2], f_hid[c % 2], ACT.Copy).then_inc(*s.step())
                s.name(f"hid_hi{c}")

            def after(what, c):
                if what == "g":
                    act.wait_ge(*e.at(f"ffn_gu{c}_0"))
                    if c >= 2:
                        act.wait_ge(*v.at(f"hid{c - 2}"))
                    nc.scalar.activation(f_silu[c % 2], bank(2 * (c % 2)), ACT.Silu).then_inc(*s.step())
                    s.name(f"silu{c}")
                    if c:
                        hidden_hi(c - 1)
                elif what == "u" and c == FFC - 1:
                    hidden_hi(c)

            act.wait_ge(*V["mix2"].at("ay"))
            for n in range(2):
                split(n)
            norm_scalar(act, st, "n", [V["mix2"].at("x_out2_first"), V["mix2"].at("x_out2")])
            tokens_hi(act, st)
            ffn_steps(split, after)

        def ffn_weights_lo(dve, n):
            src, lo, hi, _, _ = ffn_unit(n)
            dve.wait_ge(*S["ffn"].at(f"w_hi{n}"))
            nc.vector.tensor_tensor(lo, src, hi.bitcast(F32), ALU.subtract).then_inc(*V["ffn"].step())
            V["ffn"].name(f"w_lo{n}")

        def ffn_vector(dve):
            st = "ffn"
            e, s, v = E[st], S[st], V[st]
            norm_vector(dve, st, "n", param("ffn2_g", 8), hT, "h")
            tokens_lo(dve, st)

            def hidden_lo(c):
                dve.wait_ge(*s.at(f"hid_hi{c}"))
                if c >= 2:
                    dve.wait_ge(*e.at(f"ffn_d{c - 2}_1"))
                nc.vector.tensor_tensor(f_hid_lo[c % 2], f_hid[c % 2], f_hid_hi[c % 2].bitcast(F32), ALU.subtract)\
                    .then_inc(*v.step())
                v.name(f"hid_lo{c}")

            def after(what, c):
                if what == "u":
                    dve.wait_ge(*s.at(f"silu{c}"))
                    dve.wait_ge(*e.at(f"ffn_gu{c}_1"))
                    if c >= 2:
                        dve.wait_ge(*v.at(f"hid_lo{c - 2}"))
                    nc.vector.tensor_tensor(f_hid[c % 2], f_silu[c % 2], bank(2 * (c % 2) + 1), ALU.mult)\
                        .then_inc(*v.step())
                    v.name(f"hid{c}")
                if what == "g" and c:
                    hidden_lo(c - 1)
                elif what == "u" and c == FFC - 1:
                    hidden_lo(c)

            ffn_steps(lambda n: ffn_weights_lo(dve, n), after)
            dve.wait_ge(*e.at(f"ffn_d{FFC - 1}_1"))
            for b in range(4):
                x = xT[:, 2 * b:2 * b + 2, :]
                nc.vector.tensor_tensor(x, x, bank(4 + b).rearrange("p (b t) -> p b t", t=T), ALU.add)\
                    .then_inc(*v.step())
                if b == 1:
                    v.name("x_first")
            v.name("x")

        B3 = len(PROJ1) + len(PROJ2)
        HG = []
        for half in range(2):
            g_, k_, q_, v_, gate_ = (carve(tail_at + HC * (5 * half + n), HC) for n in range(5))
            HG.append(Gated("hgrn", f"h{half}", 4, q_, k_, g_, v_, gate_, y_cat[:, half * HC:(half + 1) * HC],
                            param("hgrn_g")))

        def hgrn_tensor(pe):
            st = "hgrn"
            e, s, v = E[st], S[st], V[st]
            norm_tensor(pe, st, "n", [V["ffn"].at("x")])
            pe.wait_ge(*v.at("h"))

            def proj(name, quarters=range(4)):
                (project_rows if name[1] == "i" else project)(
                    pe, st, "two", name, free_by(st, PROJ3, name, lambda n, half: [s.at(f"{n}_{half}")]), quarters)

            for what in "fqi":
                proj(f"h{what}0")
            gated_tensor_round(pe, HG[0], 0)
            n = 1
            for name in ("hg0", "hf1", "hq1"):
                for half in range(2):
                    proj(name, (2 * half, 2 * half + 1))
                    gated_tensor_round(pe, HG[0], n)
                    n += 1
            proj("hi1")
            gated_tensor_end(pe, HG[0], ProjectionFill(proj, "hg1"))
            out = OutProjection(pe, st, "two", "out3", y_cat, range(4), [v.at("h0y"), s.at("hg1_1")])
            pe.wait_ge(*s.at("h0orstd"))
            for n in range(NL + 1):
                gated_tensor_round(pe, HG[1], n)
                if n >= 2:
                    out.fill(1)
            gated_tensor_end(pe, HG[1], out)
            out.finish(v.at("h1y"))

        def hgrn_scalar(act):
            st = "hgrn"
            e, s, v = E[st], S[st], V[st]
            act.preload_act_table_set(EXP_LN)
            weights_hi_of(act, st, "two", "hf0", range(4))
            norm_scalar(act, st, "n", [V["ffn"].at("x_first"), V["ffn"].at("x")])
            tokens_hi(act, st)
            act.wait_ge(*v.at("lbdiff"))
            nc.scalar.activation(c_small[:, 40:56], c_small[:, 40:56], ACT.Exp).then_inc(*s.step())
            s.name("lbexp")

            def keep(half, what, out, **kw):
                keep_banks(act, st, f"h{what}{half}", PROJ3, B3, out, **kw)

            def log_decay(half):
                act.wait_ge(*v.at(f"h{half}f"))
                nc.scalar.activation(HG[half].g, HG[half].g, ACT.Ln).then_inc(*s.step())
                s.name(f"h{half}ln")

            keep(0, "f", halves(HG[0].k), func=ACT.Exp, scale=-1.0)
            keep(0, "q", halves(HG[0].q), func=ACT.Silu)
            act.preload_act_table_set(EXP_LN)
            log_decay(0)
            keep(0, "i", halves(HG[0].v))
            s.name("h0v")
            n = 1
            for half, what, kw in ((0, "g", {}), (1, "f", {"func": ACT.Exp, "scale": -1.0}), (1, "q", {})):
                for part in range(2):
                    gated_scalar_round(act, HG[0], n)
                    keep(half, what, halves({"g": HG[0].gate, "f": HG[1].k, "q": HG[1].q}[what]), parts=(part,), **kw)
                    n += 1
            act.wait_ge(*s.last())
            nc.scalar.activation(HG[1].q, HG[1].q, ACT.Silu).then_inc(*s.step())
            s.name("hq1_silu")
            nc.scalar.activation(HG[0].gate, HG[0].gate, ACT.Silu).then_inc(*s.step())
            s.name("h0gate")
            act.preload_act_table_set(EXP_LN)
            keep(1, "i", halves(HG[1].v))
            s.name("h1v")
            gated_scalar_end(act, HG[0])
            log_decay(1)
            keep(1, "g", halves(HG[1].gate))
            attend_scalar(act, HG[0])
            for n in range(1, NL + 1):
                gated_scalar_round(act, HG[1], n)
                if n == 2:
                    nc.scalar.activation(HG[1].gate, HG[1].gate, ACT.Silu).then_inc(*s.step())
                    s.name("h1gate")
                    act.preload_act_table_set(EXP_LN)
            gated_scalar_end(act, HG[1])
            attend_scalar(act, HG[1])

        def hgrn_pool(pool):
            def lo(name, quarters=range(4)):
                weights_lo_of(pool, "hgrn", "two", name, quarters)

            for name in ("hf0", "hq0", "hi0"):
                lo(name)
            lo("hg0", (0, 1))
            n = 1
            for name, after in (("hg0", "hf1"), ("hf1", "hq1"), ("hq1", "hi1")):
                gated_pool_round(pool, HG[0], n)
                lo(name, (2, 3))
                gated_pool_round(pool, HG[0], n + 1)
                lo(after, (0, 1))
                n += 2
            lo("hi1", (2, 3))
            gated_pool_end(pool, HG[0])
            lo("hg1")
            for n in range(1, NL + 1):
                gated_pool_round(pool, HG[1], n)
            gated_pool_end(pool, HG[1])

        def hgrn_vector(dve):
            st = "hgrn"
            e, s, v = E[st], S[st], V[st]

            def do(ins):
                ins.then_inc(*v.step())
                dve.wait_ge(*v.last())

            lb = param("lb", 16)
            l0, l1 = c_small[:, 40:48], c_small[:, 48:56]
            m = c_small[:, 56:64]
            dve.wait_ge(*V["ffn"].at("x"))
            do(nc.vector.tensor_tensor(m, lb[:, 0:8], lb[:, 8:16], ALU.max))
            do(nc.vector.tensor_tensor(l0, lb[:, 0:8], m, ALU.subtract))
            do(nc.vector.tensor_tensor(l1, lb[:, 8:16], m, ALU.subtract))
            v.name("lbdiff")
            norm_vector(dve, st, "n", param("mix2_g", 8, 8), hT, "h")
            tokens_lo(dve, st)
            dve.wait_ge(*s.at("lbexp"))
            do(nc.vector.tensor_tensor(m, l0, l1, ALU.add))
            do(nc.vector.reciprocal(m, m))
            do(nc.vector.tensor_tensor(l0, l0, m, ALU.mult))
            do(nc.vector.tensor_tensor(l1, l1, m, ALU.mult))
            do(nc.vector.tensor_tensor(l1, l1, l0, ALU.add))
            do(nc.vector.tensor_tensor(c_lb, l1, l0, ALU.subtract))
            do(nc.vector.tensor_scalar(c_omlb, c_lb, -1.0, 1.0, ALU.mult, ALU.add))
            do(nc.vector.tensor_scalar(c_lb, c_lb, 1e-19, None, ALU.max))

            def forget_start(half):
                x = HG[half]
                dve.wait_ge(*s.at(f"hf{half}_1"))
                do(nc.vector.tensor_scalar(x.k, x.k, BIG, None, ALU.min))
                do(nc.vector.tensor_scalar(x.g, x.k, 1.0, None, ALU.add))

            def forget_reciprocal(half, h0, n):
                g = HG[half].g[:, h0 * T:(h0 + n) * T]
                do(nc.vector.reciprocal(g, g))

            def forget_end(half):
                x = HG[half]
                for h in range(H4):
                    hs = slice(h * T, (h + 1) * T)
                    n = half * H4 + h
                    nc.vector.scalar_tensor_tensor(x.k[:, hs], x.k[:, hs], c_omlb[:, n:n + 1], x.g[:, hs],
                                                   ALU.mult, ALU.mult).then_inc(*v.step())
                dve.wait_ge(*v.last())
                for h in range(H4):
                    hs = slice(h * T, (h + 1) * T)
                    n = half * H4 + h
                    nc.vector.tensor_scalar(x.g[:, hs], x.g[:, hs], c_omlb[:, n:n + 1], c_lb[:, n:n + 1],
                                            ALU.mult, ALU.add).then_inc(*v.step())
                v.name(f"h{half}f")

            def second(half):
                x = HG[half]
                dve.wait_ge(*s.at(f"h{half}ln"))
                cumulate(dve, x)
                dve.wait_ge(*v.last())
                dve.wait_ge(*s.at("hq0_1" if half == 0 else "hq1_silu"))
                do(nc.vector.tensor_scalar(x.q, x.q, float(P) ** -0.5, None, ALU.mult))
                v.name(f"h{half}ready")

            forget_start(0)
            forget_reciprocal(0, 0, H4)
            forget_end(0)
            second(0)
            for n in range(NL + 1):
                gated_vector_round(dve, HG[0], n)
                if n == 4:
                    forget_start(1)
                    forget_reciprocal(1, 0, 1)
                elif n == 5:
                    forget_reciprocal(1, 1, 2)
                elif n == 6:
                    forget_reciprocal(1, 3, 1)
            gated_vector_end(dve, HG[0])
            forget_end(1)

            def decay(h, c):
                return c_decay[:, h * 4 + c:h * 4 + c + 1]

            attend_vector(dve, HG[0], decay, lambda: second(1))
            for n in range(NL + 1):
                gated_vector_round(dve, HG[1], n)
            gated_vector_end(dve, HG[1])
            attend_vector(dve, HG[1], decay)
            add_residual(dve, st, "out3")

        def final_tensor(pe):
            norm_tensor(pe, "final", "n")

        def final_scalar(act, waits):
            act.preload_act_table_set(EXP_LN)
            norm_scalar(act, "final", "n", waits)

        def final_vector(dve):
            norm_vector(dve, "final", "n", param("final2_g", 8), hT, "h")

        @block.tensor
        def _(pe):
            mixer1_tensor(pe)
            route_tensor(pe, M1)
            moe_tensor(pe, M1)
            mixer2_tensor(pe)
            ffn_tensor(pe)
            hgrn_tensor(pe)
            route_tensor(pe, M2)
            moe2_tensor(pe)
            final_tensor(pe)

        @block.scalar
        def _(act):
            mixer1_scalar(act)
            route_scalar(act, M1, [V["mix1"].at("x_out1_first"), V["mix1"].at("x_out1")])
            n = moe_scalar(act, M1)
            mixer2_scalar(act, [(moe_sems["moe1"]["spread_added"], n * 4 + x) for x in (3, 5)])
            ffn_scalar(act)
            hgrn_scalar(act)
            route_scalar(act, M2, [V["hgrn"].at("x_out3_first"), V["hgrn"].at("x_out3")])
            n = moe2_scalar(act)
            final_scalar(act, [(moe_sems["moe2"]["spread_added"], n * 4 + x) for x in (3, 5)])

        @block.gpsimd
        def _(pool):
            mixer1_pool(pool)
            mixer2_pool(pool)
            hgrn_pool(pool)

        @block.vector
        def _(dve):
            mixer1_vector(dve)
            route_vector(dve, M1)
            moe_vector(dve, M1)
            mixer2_vector(dve)
            ffn_vector(dve)
            hgrn_vector(dve)
            route_vector(dve, M2)
            moe2_vector(dve)
            final_vector(dve)
    return found


_BIG = ["w_in", "w_out", "w_gate", "w_up", "w_down", "ab_w_in_2", "ab_w_out_2", "ffn_w_gate_2", "ffn_w_up_2",
        "ffn_w_down_2", "c_w_in_2", "c_w_out_2", "moe_w_gate_2", "moe_w_up_2", "moe_w_down_2"]


def laid_out(inputs):
    a = {k: np.asarray(v) for k, v in inputs.items()}

    def columns(v):
        v = v.reshape(-1, v.shape[-1] // P, P)
        return v.transpose(2, 0, 1).reshape(P, -1)

    def matrix(w):
        return w.reshape(KC, P, -1).transpose(1, 0, 2).reshape(P, -1)

    def every(v):
        return np.broadcast_to(v.reshape(1, -1), (P, v.size))

    gla_w = np.zeros((P, 256), np.float32)
    gla_w[:16] = a["gla_w_a2_2"][0]
    parts = {
        "mix_g": columns(a["mix_norm_g"]), "ffn_g": columns(a["ffn_norm_g"]), "final_g": columns(a["final_norm_g"]),
        "mix2_g": columns(a["norm_mix_g_2"]), "ffn2_g": columns(a["norm_ffn_g_2"]),
        "final2_g": columns(a["final_norm_g_2"]), "conv_a": columns(a["conv_a_w"][0]),
        "conv_a_g": columns(a["conv_a_norm_g"]), "dn_conv": columns(a["dn_conv_w"][0]),
        "dn_g": columns(a["dn_norm_g"]), "ret_g": columns(a["ret_norm_g_2"]), "gla_g": columns(a["gla_norm_g_2"]),
        "hgrn_g": columns(a["hgrn_norm_g_2"]), "lb": columns(a["hgrn_lb_logits_2"]),
        "gla_b": columns(a["gla_b_a2_2"]), "a_log": every(a["dn_a_log"]), "dt_bias": every(a["dn_dt_bias"]),
        "router1": matrix(np.concatenate([a["router_group_w"][0], a["router_expert_w"][0]], axis=1)),
        "router2": matrix(a["moe_router_2"][0]), "tail1": matrix(a["w_in"][0][:, 3584:]),
        "tail2": matrix(a["ab_w_in_2"][0][:, 3584:]), "gla_w": gla_w,
    }
    out = {name: np.ascontiguousarray(a[name]) for name in _BIG}
    out["small"] = np.ascontiguousarray(np.concatenate([parts[n] for n, _ in _SMALL], axis=1))
    out["consts"] = constants()
    out["xT"] = np.ascontiguousarray(a["x"][0].reshape(T, KC, P).transpose(2, 1, 0))
    out["positions"] = np.ascontiguousarray(np.broadcast_to(a["positions_2"].reshape(1, T), (P, T)))
    return out


def write_out(nc, known, arrays):
    A = {n: nc.dram_tensor(f"in_{n}", a.shape, mybir.dt.from_np(a.dtype), kind="ExternalInput").ap()
         for n, a in arrays.items()}
    A["out"] = nc.dram_tensor("out_0", (P, KC, T), F32, kind="ExternalOutput").ap()
    return program(nc, known, A)


def kernel(**inputs):
    import concourse.bacc as _bacc
    from concourse.bass_utils import run_bass_kernel_spmd as _run

    arrays = laid_out(inputs)
    core = {"target_bir_lowering": False, "num_devices": 1, "dynamic_dma_scratch_size": 1024}
    known = write_out(_bacc.Bacc("TRN2", **core), {}, arrays)
    nc = _bacc.Bacc("TRN2", **core)
    write_out(nc, known, arrays)
    r = _run(nc, [{f"in_{n}": a for n, a in arrays.items()}], core_ids=[0])
    out = r.results[0]["out_0"]
    return out.transpose(2, 1, 0).reshape(1, T, D)
```
